# Optimizing a Trainium2 kernel written in Bass

```python
import math
import jax, jax.numpy as jnp
from jax import lax
import numpy as np

D_MODEL = 1024
BATCH = 1
SEQ = 1024
DEPTH = 1
DEC_BATCH = 8
DEC_SEQ = 1
PAST_LEN = 1024
PAGE_SIZE = 128

HEAD_DIM = 64
H_FOX = 6
H_SB = 6
FOX_W = H_FOX * HEAD_DIM
SB_W = H_SB * HEAD_DIM
D_LRU = D_MODEL - FOX_W - SB_W
LRU_BLOCKS = 4
LRU_BW = D_LRU // LRU_BLOCKS
LRU_C = 8.0
LRU_CONV = 4
D_FF = 2816
FFN_CONV = 3
Q_BLOCK = 128
DN_ALPHA = (2 * DEPTH) ** 0.25
DN_BETA = (8 * DEPTH) ** -0.25
LN_EPS = 1e-5
FGATE_BIAS = 3.0
IN_SIZES = (FOX_W, FOX_W, FOX_W, H_FOX, SB_W, SB_W, SB_W, D_LRU, D_LRU)
IN_SCALES = (1.0, 1.0, DN_BETA, 1.0, 1.0, 1.0, DN_BETA, 1.0, 1.0)
IN_SPLITS = tuple(int(v) for v in np.cumsum(IN_SIZES)[:-1])

kernel_name = "hybrid_fox_sb_rglru_step"

def layer_norm(x, g, b):
    xf = x.astype(jnp.float32)
    mu = xf.mean(-1, keepdims=True)
    var = jnp.square(xf - mu).mean(-1, keepdims=True)
    return ((xf - mu) * lax.rsqrt(var + LN_EPS) * g + b).astype(x.dtype)

def causal_dwconv(x, prev, w, b):
    width = w.shape[0]
    T = x.shape[1]
    xp = jnp.concatenate([prev.astype(x.dtype), x], axis=1)
    y = b + sum(xp[:, k:k + T] * w[k] for k in range(width))
    return y, xp[:, xp.shape[1] - (width - 1):]

def gather_pages(pool, page_table):
    g = pool[page_table]
    return g.reshape(g.shape[0], g.shape[1] * g.shape[2], *g.shape[3:])

def sweep_query_blocks(fn, qpos, *qs):
    T = qpos.shape[0]
    if T % Q_BLOCK != 0 or T <= Q_BLOCK:
        return fn(qpos, *qs)
    nb = T // Q_BLOCK
    blocks = tuple(jnp.moveaxis(a.reshape(a.shape[0], nb, Q_BLOCK, *a.shape[2:]), 1, 0) for a in qs)
    out = lax.map(lambda args: fn(*args), (qpos.reshape(nb, Q_BLOCK),) + blocks)
    out = jnp.moveaxis(out, 0, 1)
    return out.reshape(out.shape[0], T, *out.shape[3:])

def fox_attention(q, k, v, f_q, f_k, qpos, kpos):
    scale = HEAD_DIM ** -0.5
    fk_t = jnp.swapaxes(f_k, 1, 2)

    def block(qp, qb, fqb):
        s = jnp.einsum('bqhd,bkhd->bhqk', qb, k, preferred_element_type=jnp.float32) * scale
        s = s + (jnp.swapaxes(fqb, 1, 2)[..., :, None] - fk_t[..., None, :])
        mask = kpos[None, :] <= qp[:, None]
        p = jax.nn.softmax(jnp.where(mask, s, -jnp.inf), axis=-1)
        return jnp.einsum('bhqk,bkhd->bqhd', p.astype(v.dtype), v)

    return sweep_query_blocks(block, qpos, q, f_q)

def stick_breaking_attention(q, k, v, qpos, kpos):
    scale = HEAD_DIM ** -0.5

    def block(qp, qb):
        z = jnp.einsum('bqhd,bkhd->bhqk', qb, k, preferred_element_type=jnp.float32) * scale
        mask = kpos[None, :] < qp[:, None]
        log_fail = jnp.where(mask, jax.nn.log_sigmoid(-z), 0.0)
        tail = lax.cumsum(log_fail, axis=3, reverse=True) - log_fail
        w = jnp.where(mask, jnp.exp(jax.nn.log_sigmoid(z) + tail), 0.0)
        return jnp.einsum('bhqk,bkhd->bqhd', w.astype(v.dtype), v)

    return sweep_query_blocks(block, qpos, q)

def recurrent_branch(xr, xg, conv_prev, h0, w_conv, b_conv, w_r, b_r, w_i, b_i, lam):
    xc, conv_new = causal_dwconv(xr, conv_prev, w_conv, b_conv)
    B, T, _ = xc.shape
    xb = xc.reshape(B, T, LRU_BLOCKS, LRU_BW)
    r = jax.nn.sigmoid((jnp.einsum('btni,nij->btnj', xb, w_r).reshape(B, T, D_LRU) + b_r).astype(jnp.float32))
    i = jax.nn.sigmoid((jnp.einsum('btni,nij->btnj', xb, w_i).reshape(B, T, D_LRU) + b_i).astype(jnp.float32))
    log_a = LRU_C * r * jax.nn.log_sigmoid(lam.astype(jnp.float32))
    a = jnp.exp(log_a)
    u = jnp.sqrt(-jnp.expm1(2.0 * log_a)) * i * xc.astype(jnp.float32)

    def step(h, au):
        h = au[0] * h + au[1]
        return h, h

    h_last, hs = lax.scan(step, h0.astype(jnp.float32), (jnp.swapaxes(a, 0, 1), jnp.swapaxes(u, 0, 1)))
    y = jnp.swapaxes(hs, 0, 1).astype(xr.dtype) * jax.nn.gelu(xg)
    return y, h_last.astype(xr.dtype), conv_new

def decoder_layer(x, c, past_fox_k, past_fox_v, past_fox_logf, past_sb_k, past_sb_v, h0, lru_conv_prev, ffn_conv_prev,
                  w_ada, b_ada, w_in, b_fgate, w_lru_conv, b_lru_conv, w_rgate, b_rgate, w_igate, b_igate, lru_lambda,
                  w_out, ln1_g, ln1_b, w_up, w_ffn_conv, b_ffn_conv, w_down, ln2_g, ln2_b):
    B, T, _ = x.shape
    P = past_fox_k.shape[1]
    mod = jax.nn.silu(c) @ w_ada + b_ada
    sh1, sc1, g1, sh2, sc2, g2 = [m[:, None, :] for m in jnp.split(mod, 6, axis=-1)]

    h = x * (1 + sc1) + sh1
    fq, fk, fv, fg, sq, sk, sv, xr, xg = jnp.split(h @ w_in, IN_SPLITS, axis=-1)
    fq = fq.reshape(B, T, H_FOX, HEAD_DIM)
    fk = fk.reshape(B, T, H_FOX, HEAD_DIM)
    fv = fv.reshape(B, T, H_FOX, HEAD_DIM)
    sq = sq.reshape(B, T, H_SB, HEAD_DIM)
    sk = sk.reshape(B, T, H_SB, HEAD_DIM)
    sv = sv.reshape(B, T, H_SB, HEAD_DIM)
    logf = jax.nn.log_sigmoid((fg + b_fgate).astype(jnp.float32))
    f_cum = jnp.cumsum(jnp.concatenate([past_fox_logf.astype(jnp.float32), logf], axis=1), axis=1)
    kpos = jnp.arange(P + T)
    qpos = P + jnp.arange(T)
    fox = fox_attention(fq, jnp.concatenate([past_fox_k.astype(fk.dtype), fk], 1),
                        jnp.concatenate([past_fox_v.astype(fv.dtype), fv], 1), f_cum[:, P:], f_cum, qpos, kpos)
    sb = stick_breaking_attention(sq, jnp.concatenate([past_sb_k.astype(sk.dtype), sk], 1),
                                  jnp.concatenate([past_sb_v.astype(sv.dtype), sv], 1), qpos, kpos)
    lru, h_last, lru_conv_new = recurrent_branch(xr, xg, lru_conv_prev, h0, w_lru_conv, b_lru_conv,
                                                 w_rgate, b_rgate, w_igate, b_igate, lru_lambda)
    mix = jnp.concatenate([fox.reshape(B, T, FOX_W), sb.reshape(B, T, SB_W), lru], axis=-1) @ w_out
    x = layer_norm(DN_ALPHA * x + g1 * mix, ln1_g, ln1_b)

    h2 = x * (1 + sc2) + sh2
    ua, ub = jnp.split(h2 @ w_up, 2, axis=-1)
    uc, ffn_conv_new = causal_dwconv(ua, ffn_conv_prev, w_ffn_conv, b_ffn_conv)
    ffn = (jax.nn.gelu(uc) * ub) @ w_down
    x = layer_norm(DN_ALPHA * x + g2 * ffn, ln2_g, ln2_b)
    return x, (fk, fv, logf, sk, sv, h_last, lru_conv_new, ffn_conv_new)

def setup_inputs(seed: int = 0) -> dict:
    key = jax.random.key(seed)
    ks = iter(jax.random.split(key, 48))

    def nrm(shape, s):
        return s * jax.random.normal(next(ks), shape, jnp.float32)

    n_pages = PAST_LEN // PAGE_SIZE
    n_used = DEC_BATCH * n_pages
    n_pool = n_used + (n_used + 3) // 4
    page_table = jax.random.permutation(next(ks), n_pool)[:n_used].reshape(DEC_BATCH, n_pages).astype(jnp.int32)

    x_prompt = nrm((BATCH, SEQ, D_MODEL), 1.0)
    x_sample = nrm((DEC_BATCH, DEC_SEQ, D_MODEL), 1.0)
    cache_fox_k = nrm((DEPTH, n_pool, PAGE_SIZE, H_FOX, HEAD_DIM), 1.0)
    cache_fox_v = nrm((DEPTH, n_pool, PAGE_SIZE, H_FOX, HEAD_DIM), 1.0)
    cache_fox_logf = jax.nn.log_sigmoid(FGATE_BIAS + nrm((DEPTH, n_pool, PAGE_SIZE, H_FOX), 1.0))
    cache_sb_k = nrm((DEPTH, n_pool, PAGE_SIZE, H_SB, HEAD_DIM), 1.0)
    cache_sb_v = nrm((DEPTH, n_pool, PAGE_SIZE, H_SB, HEAD_DIM), 1.0)
    state_lru_h = nrm((DEPTH, DEC_BATCH, D_LRU), 0.5)
    state_lru_conv = nrm((DEPTH, DEC_BATCH, LRU_CONV - 1, D_LRU), 1.0)
    state_ffn_conv = nrm((DEPTH, DEC_BATCH, FFN_CONV - 1, D_FF), 1.0)
    c_prompt = nrm((BATCH, D_MODEL), 1.0)
    c_sample = nrm((DEC_BATCH, D_MODEL), 1.0)

    w_ada = nrm((DEPTH, D_MODEL, 6 * D_MODEL), 0.5 * D_MODEL ** -0.5)
    b_ada = nrm((DEPTH, 6 * D_MODEL), 0.02)
    w_in = jnp.concatenate([nrm((DEPTH, D_MODEL, n), s * D_MODEL ** -0.5) for n, s in zip(IN_SIZES, IN_SCALES)], axis=-1)
    b_fgate = FGATE_BIAS + nrm((DEPTH, H_FOX), 0.5)
    w_lru_conv = nrm((DEPTH, LRU_CONV, D_LRU), LRU_CONV ** -0.5)
    b_lru_conv = nrm((DEPTH, D_LRU), 0.02)
    w_rgate = nrm((DEPTH, LRU_BLOCKS, LRU_BW, LRU_BW), LRU_BW ** -0.5)
    b_rgate = nrm((DEPTH, D_LRU), 0.1)
    w_igate = nrm((DEPTH, LRU_BLOCKS, LRU_BW, LRU_BW), LRU_BW ** -0.5)
    b_igate = nrm((DEPTH, D_LRU), 0.1)
    a_c = jax.random.uniform(next(ks), (DEPTH, D_LRU), jnp.float32, minval=0.9, maxval=0.999)
    s_lam = a_c ** (1.0 / LRU_C)
    lru_lambda = jnp.log(s_lam) - jnp.log1p(-s_lam)
    w_out = nrm((DEPTH, D_MODEL, D_MODEL), DN_BETA * D_MODEL ** -0.5)
    ln1_g = 1.0 + nrm((DEPTH, D_MODEL), 0.05)
    ln1_b = nrm((DEPTH, D_MODEL), 0.02)
    w_up = nrm((DEPTH, D_MODEL, 2 * D_FF), D_MODEL ** -0.5)
    w_ffn_conv = nrm((DEPTH, FFN_CONV, D_FF), FFN_CONV ** -0.5)
    b_ffn_conv = nrm((DEPTH, D_FF), 0.02)
    w_down = nrm((DEPTH, D_FF, D_MODEL), DN_BETA * D_FF ** -0.5)
    ln2_g = 1.0 + nrm((DEPTH, D_MODEL), 0.05)
    ln2_b = nrm((DEPTH, D_MODEL), 0.02)
    return {"x_prompt": x_prompt, "x_sample": x_sample,
            "cache_fox_k": cache_fox_k, "cache_fox_v": cache_fox_v, "cache_fox_logf": cache_fox_logf,
            "cache_sb_k": cache_sb_k, "cache_sb_v": cache_sb_v,
            "state_lru_h": state_lru_h, "state_lru_conv": state_lru_conv, "state_ffn_conv": state_ffn_conv,
            "page_table": page_table, "c_prompt": c_prompt, "c_sample": c_sample,
            "w_ada": w_ada, "b_ada": b_ada, "w_in": w_in, "b_fgate": b_fgate,
            "w_lru_conv": w_lru_conv, "b_lru_conv": b_lru_conv, "w_rgate": w_rgate, "b_rgate": b_rgate,
            "w_igate": w_igate, "b_igate": b_igate, "lru_lambda": lru_lambda, "w_out": w_out,
            "ln1_g": ln1_g, "ln1_b": ln1_b, "w_up": w_up, "w_ffn_conv": w_ffn_conv, "b_ffn_conv": b_ffn_conv,
            "w_down": w_down, "ln2_g": ln2_g, "ln2_b": ln2_b}

def reference(x_prompt, x_sample, cache_fox_k, cache_fox_v, cache_fox_logf, cache_sb_k, cache_sb_v,
              state_lru_h, state_lru_conv, state_ffn_conv, page_table, c_prompt, c_sample,
              w_ada, b_ada, w_in, b_fgate, w_lru_conv, b_lru_conv, w_rgate, b_rgate, w_igate, b_igate,
              lru_lambda, w_out, ln1_g, ln1_b, w_up, w_ffn_conv, b_ffn_conv, w_down, ln2_g, ln2_b):
    B = x_prompt.shape[0]
    dt = x_prompt.dtype
    empty_fox = jnp.zeros((B, 0, H_FOX, HEAD_DIM), dt)
    empty_logf = jnp.zeros((B, 0, H_FOX), jnp.float32)
    empty_sb = jnp.zeros((B, 0, H_SB, HEAD_DIM), dt)
    h0_p = jnp.zeros((B, D_LRU), dt)
    lru_conv_p = jnp.zeros((B, LRU_CONV - 1, D_LRU), dt)
    ffn_conv_p = jnp.zeros((B, FFN_CONV - 1, D_FF), dt)

    y_p, y_s = x_prompt, x_sample
    st_p, st_s = [], []
    for l in range(DEPTH):
        lw = (w_ada[l], b_ada[l], w_in[l], b_fgate[l], w_lru_conv[l], b_lru_conv[l], w_rgate[l], b_rgate[l],
              w_igate[l], b_igate[l], lru_lambda[l], w_out[l], ln1_g[l], ln1_b[l], w_up[l], w_ffn_conv[l],
              b_ffn_conv[l], w_down[l], ln2_g[l], ln2_b[l])
        y_p, new_p = decoder_layer(y_p, c_prompt, empty_fox, empty_fox, empty_logf, empty_sb, empty_sb,
                                   h0_p, lru_conv_p, ffn_conv_p, *lw)
        y_s, new_s = decoder_layer(y_s, c_sample,
                                   gather_pages(cache_fox_k[l], page_table), gather_pages(cache_fox_v[l], page_table),
                                   gather_pages(cache_fox_logf[l], page_table),
                                   gather_pages(cache_sb_k[l], page_table), gather_pages(cache_sb_v[l], page_table),
                                   state_lru_h[l], state_lru_conv[l], state_ffn_conv[l], *lw)
        st_p.append(new_p)
        st_s.append(new_s)

    p_fox_k, p_fox_v, p_fox_logf, p_sb_k, p_sb_v, p_lru_h, p_lru_conv, p_ffn_conv = [
        jnp.stack([st[i] for st in st_p], axis=0) for i in range(8)]
    s_fox_k, s_fox_v, s_fox_logf, s_sb_k, s_sb_v, s_lru_h, s_lru_conv, s_ffn_conv = [
        jnp.stack([st[i] for st in st_s], axis=0) for i in range(8)]
    return (y_p, y_s,
            p_fox_k, p_fox_v, p_fox_logf, p_sb_k, p_sb_v, p_lru_h, p_lru_conv, p_ffn_conv,
            s_fox_k, s_fox_v, s_fox_logf, s_sb_k, s_sb_v, s_lru_h, s_lru_conv, s_ffn_conv)


_drawn_inputs = setup_inputs


def setup_inputs(seed=0):
    import zlib

    import numpy as np

    out = dict(_drawn_inputs(seed))
    spreads = {}
    factors = {'cache_fox_k': 2.886, 'cache_fox_logf': 24.595, 'ln1_b': 2.839, 'b_ffn_conv': 26.228}
    for name, (base, spread) in spreads.items():
        noise = np.random.default_rng([zlib.crc32(name.encode()), seed]).standard_normal(out[name].shape)
        drawn = base * np.exp(spread * noise) if base else spread * noise
        out[name] = __import__('jax').numpy.asarray(drawn.astype(out[name].dtype))
    for name, factor in factors.items():
        out[name] = (out[name] * factor).astype(out[name].dtype)
    return out
```

```python
import concourse.bass as bass
from concourse import mybir
from concourse.alu_op_type import AluOpType as ALU
from contextlib import ExitStack

F32 = mybir.dt.float32
F32R = mybir.dt.float32r
I32 = mybir.dt.int32
ACT = mybir.ActivationFunctionType
AX = mybir.AxisListType
ds = bass.ds
P = 128


def hybrid_step(nc, i, o):
    SEQ, D = i["x_prompt"].shape[1:]
    NB = i["x_sample"].shape[0]
    TOK = SEQ + NB
    NCH = 3
    CH = TOK // NCH
    KT = D // P
    TT = SEQ // P
    HD = i["cache_fox_k"].shape[4]
    H = i["cache_fox_k"].shape[3]
    W = H * HD
    WT = W // P
    DL = i["state_lru_h"].shape[2]
    LT = DL // P
    DFF = i["w_down"].shape[1]
    FT = DFF // P
    NPG = i["page_table"].shape[1]
    NPOOL = i["cache_fox_k"].shape[1]
    NC = NB + 1
    FQ, FK, FV, FG = 0, W, 2 * W, 3 * W
    SQ = FG + H
    SK, SV, XR = SQ + W, SQ + 2 * W, SQ + 3 * W
    XG = XR + DL
    assert CH * NCH == TOK and CH % 2 == 0

    w_in = i["w_in"][0].rearrange("(k p) n -> p k n", p=P)
    w_ada = i["w_ada"][0].rearrange("(k p) n -> p k n", p=P)

    with ExitStack() as ctx:
        def sb(name, shape, dt=F32):
            return ctx.enter_context(nc.sbuf_tensor(name, shape, dt))

        def sem(name):
            return ctx.enter_context(nc.semaphore(name))

        def sems(name, n):
            return [sem(f"{name}{k}") for k in range(n)]

        qk_scr = nc.dram_tensor("qk_scr", [2, 2 * W, SEQ], F32).ap()
        f_scr = nc.dram_tensor("f_scr", [4, H, SEQ], F32).ap()
        sq_scr = nc.dram_tensor("sq_scr", [NB, 2 * W], F32).ap()

        psA = ctx.enter_context(nc.psum_tensor("psA", [P, 3, 512], F32))
        psB = ctx.enter_context(nc.psum_tensor("psB", [P, 3, 512], F32))
        psT = ctx.enter_context(nc.psum_tensor("psT", [P, 2, 512], F32))
        proj_ps = (psA, psB)

        ident = sb("ident", [P, P])
        acts_hi = sb("acts_hi", [P, KT, TOK], F32R)
        acts_lo = sb("acts_lo", [P, KT, TOK], F32R)
        modT = sb("modT", [P, 6 * KT, NC])
        NVA = 6 * KT + 4 * LT + 4 * LT + 2 * KT
        NVB = 4 * FT
        NVC = NB * 3 * LT + NB * LT
        NVD = NB * 2 * FT
        vecT = sb("vecT", [P, NVA + NVB + NVC + NVD])
        cT = sb("cT", [P, KT, NC])
        w_raw = sb("w_raw", [P, 4, KT, P])
        w_hi = sb("w_hi", [P, 2, KT, P], F32R)
        w_lo = sb("w_lo", [P, 2, KT, P], F32R)
        misc = sb("misc", [P, TOK])
        fgT = misc[0:H]
        ones = sb("ones", [P, 1])
        ln_st = sb("ln_st", [P, 2, 16])
        stA = ExitStack()

        def sbA(name, shape, dt=F32):
            return stA.enter_context(nc.sbuf_tensor(name, shape, dt))

        xrT = sbA("xrT", [P, LT, TOK])
        xgT = sbA("xgT", [P, LT, TOK])
        table = sbA("table", [1, NB * NPG], I32)
        scores = sbA("scores", [P, 2, NPG, NB, H])
        lf_pages = sbA("lf_pages", [P, NPG, NB, H])
        smpT = sbA("smpT", [P, 6 * WT, NB])
        smp_out = sbA("smp_out", [NB, 4 * WT, P])
        ident_r = sbA("ident_r", [P, P], F32R)
        mask_f = sbA("mask_f", [P, 2, P])
        mask_r = sbA("mask_r", [P, 2, P], F32R)
        tri = sbA("tri", [P, 2, P])
        bfg = sbA("bfg", [H, 1])
        lgT = sbA("lgT", [H, TOK])

        A_ADA = 0
        A_WLC = 6 * KT
        A_BLC = A_WLC + 4 * LT
        A_BR = A_BLC + LT
        A_BI = A_BR + LT
        A_LAM = A_BI + LT
        A_L1G = A_LAM + LT
        A_L1B = A_L1G + KT
        A_WFC = NVA
        A_BFC = NVA + 3 * FT
        A_SLC = NVA + NVB
        A_SLH = A_SLC + NB * 3 * LT
        A_SFC = NVA + NVB + NVC

        st = ExitStack()

        def sb1(name, shape, dt=F32):
            return st.enter_context(nc.sbuf_tensor(name, shape, dt))

        x_rows = sb1("x_rows", [P, TT, D])
        vec_rows = sb1("vec_rows", [P, 6, P])
        c_rows = xrT[0:NC, 0, 0:D]
        xs_rows = xrT[0:NB, 1, 0:D]
        h_full = xgT[:, :, 0:512]
        c_half = xgT[0:NC, 0, 0:D]
        hs_full = sb1("hs_full", [P, KT, NB])
        w_ada1 = sb1("w_ada1", [P, 2, KT, 512])
        st.close()
        st2 = ExitStack()

        def sb2(name, shape, dt=F32):
            return st2.enter_context(nc.sbuf_tensor(name, shape, dt))

        tile_out = sb2("tile_out", [P, 2, TOK])
        tok_out = sb2("tok_out", [P, 2, TT, P])
        k_page = sb2("k_page", [P, NPG, W])
        q_row = sb2("q_row", [P, 2, W])
        st2.close()
        st3 = ExitStack()

        def sb3(name, shape, dt=F32):
            return st3.enter_context(nc.sbuf_tensor(name, shape, dt))

        fg_y = sb3("fg_y", [H, TOK])
        fg_e = sb3("fg_e", [H, TOK])
        fcum = sb3("fcum", [H, SEQ])
        fparts = sb3("fparts", [H, 4, SEQ], F32R)
        lg_out = sb3("lg_out", [P, TT + 1, H])
        st3.close()
        st4 = ExitStack()

        def sb4(name, shape, dt=F32):
            return st4.enter_context(nc.sbuf_tensor(name, shape, dt))

        k_st = sb4("k_st", [P, 2, SEQ], F32R)
        v_raw = sb4("v_raw", [P, 2, TT, HD])
        v_st = sb4("v_st", [P, 2, TT, 2 * HD], F32R)
        o_low = misc[:, 0:512]
        o_sum = misc[:, 512:1024]
        st5 = ExitStack()

        def sb5(name, shape, dt=F32):
            return st5.enter_context(nc.sbuf_tensor(name, shape, dt))

        fq_rows = sb5("fq_rows", [P, 2, SEQ], F32R)
        fk_rows = sb5("fk_rows", [P, 2, SEQ], F32R)
        probs = sb5("probs", [P, 3, SEQ])
        pt_hi = sb5("pt_hi", [P, 2, TT, P], F32R)
        pt_lo = sb5("pt_lo", [P, 2, TT, P], F32R)
        row_max = sb5("row_max", [P, 16])
        row_sum = sb5("row_sum", [P, 16])
        row_inv = sb5("row_inv", [P, 16])
        st5.close()
        st6 = ExitStack()

        def sb6(name, shape, dt=F32):
            return st6.enter_context(nc.sbuf_tensor(name, shape, dt))

        z_s = sb6("z_s", [P, 4, 512])
        z_e = sb6("z_e", [P, 3, 512])
        z_sp = sb6("z_sp", [P, 4, 512])
        z_w = sb6("z_w", [P, 4, 512])
        w_hi2 = sb6("w_hi2", [P, 2, 512], F32R)
        w_lo2 = sb6("w_lo2", [P, 2, 512], F32R)
        st6.close()
        st4.close()
        st7 = ExitStack()

        def sb7(name, shape, dt=F32):
            return st7.enter_context(nc.sbuf_tensor(name, shape, dt))

        v_page = sb7("v_page", [P, 2, NPG, W])
        r_xc = sb7("r_xc", [P, LT, TOK])
        r_a = sb7("r_a", [P, LT, TOK])
        r_t = sb7("r_t", [P, LT, TOK])
        r_i = sb7("r_i", [P, LT, TOK])
        r_h = sb7("r_h", [P, LT, TOK])
        gate_w = sb7("gate_w", [P, 2, LT, P])
        r_c = sb7("r_c", [P, 6, LT])
        lru_cols = sb7("lru_cols", [P, LT, 4 + 2 * NB])
        lru_rows = misc[0:4 + 2 * NB, 0:DL]
        R48 = NB * H
        d_f, d_g, d_z, d_e = [x[0:R48].rearrange("p a n -> p (a n)")[:, 0:n]
                              for x, n in ((r_a, SEQ + 1), (r_t, SEQ + 1), (r_i, SEQ), (r_h, SEQ))]
        xc_flat = r_xc[:].rearrange("p a n -> p (a n)")
        NP2 = 2 * NPG * R48
        d_p = xc_flat[:, 0:NP2].rearrange("p (e k n) -> p e k n", e=2, k=NPG)
        d_zq = xc_flat[:, NP2:NP2 + WT * R48].rearrange("p (w b h) -> p w b h", w=WT, b=NB)
        d_small = sb7("d_small", [R48, 8])
        d_diag = sb7("d_diag", [R48, R48])
        d_grp = sb7("d_grp", [R48, NB])
        d_self = xc_flat[0:NB, NP2 + WT * R48:NP2 + WT * R48 + R48]
        d_qk = sb7("d_qk", [P, WT, NB])
        d_hm = sb7("d_hm", [P, WT, H])
        d_spread = sb7("d_spread", [H, NB, H])
        d_out = sb7("d_out", [P, 2 * WT, NB])
        st7.close()
        stA.close()
        resT = sb("resT", [P, KT, TOK])
        st8 = ExitStack()

        def sb8(name, shape, dt=F32):
            return st8.enter_context(nc.sbuf_tensor(name, shape, dt))

        x_tile = sb8("x_tile", [P, 2, D])
        x_hat = sb8("x_hat", [P, 4, D])
        xs_hat = sb8("xs_hat", [NB, 2, D])
        h2_full = sb8("h2_full", [P, 2, 512])
        hs2 = sb8("hs2", [P, 2, KT, NB])
        ln_f = sb8("ln_f", [P, 4, KT])
        st8.close()
        GMAX = 6
        GROUPS = []
        while sum(GROUPS) < FT:
            left = -(-(FT - sum(GROUPS)) // GMAX)
            GROUPS.append(-(-(FT - sum(GROUPS)) // left))
        st9 = ExitStack()

        def sb9(name, shape, dt=F32):
            return st9.enter_context(nc.sbuf_tensor(name, shape, dt))

        g_hi = sb9("g_hi", [P, GMAX, TOK], F32R)
        g_lo = sb9("g_lo", [P, GMAX, TOK], F32R)
        u_a = sb9("u_a", [P, TOK])
        u_c = sb9("u_c", [P, TOK])
        u_g = sb9("u_g", [P, TOK])
        ffn_cols = sb9("ffn_cols", [P, FT, 2 + NB])
        g_tmp = sb9("g_tmp", [P, NB])
        st9.close()
        stB = ExitStack()

        def sbB(name, shape, dt=F32):
            return stB.enter_context(nc.sbuf_tensor(name, shape, dt))

        y_pad = sbB("y_pad", [P, 2 * TOK])
        ln2g = sbB("ln2g", [P, D])
        ln2b = sbB("ln2b", [P, D])
        y_tile = sbB("y_tile", [P, 3, D])
        ffn_rows = sbB("ffn_rows", [2 + NB, FT, P])
        stB.close()

        s_c = sem("s_c")
        s_small = sem("s_small")
        s_x = sems("s_x", 2)
        s_idz = sem("s_idz")
        s_ident = sem("s_ident")
        s_csil = sem("s_csil")
        s_ctanh = sem("s_ctanh")
        s_vt = sem("s_vt")
        s_vte = sem("s_vte")
        s_al = sems("s_al", 2)
        s_amm = sem("s_amm")
        s_aev = sem("s_aev")
        s_one = sem("s_one")
        s_xt = sem("s_xt")
        s_hf = sem("s_hf")
        s_hhi = sem("s_hhi")
        s_hlo = sem("s_hlo")
        s_hs = sem("s_hs")
        s_wl = sems("s_wl", 2)
        s_whi = sem("s_whi")
        s_wlo = sem("s_wlo")
        s_pm = sem("s_pm")
        s_pe = sem("s_pe")
        s_tt = sem("s_tt")
        s_te = sem("s_te")
        s_st = sems("s_st", 2)
        s_so = sems("s_so", 2)
        s_sq = sem("s_sq")
        s_kfree = sem("s_kfree")
        s_kl = sems("s_kl", NPG)
        s_ql = sems("s_ql", 2)
        s_km = sem("s_km")
        s_tab = sem("s_tab")
        s_gw0 = sem("s_gw0")
        s_gw = sem("s_gw")
        r_d = sem("r_d")
        r_s = sem("r_s")
        r_p = sem("r_p")
        s_lr = sem("s_lr")
        s_cc = sem("s_cc")
        d_d = sem("d_d")
        d_a = sem("d_a")
        d_t = sem("d_t")
        s_vl = sems("s_vl", 2)
        d_v = sem("d_v")
        g_wl = sems("g_wl", 2)
        g_wh = sem("g_wh")
        g_ws = sem("g_ws")
        g_pm = sem("g_pm")
        g_ev = sems("g_ev", 2)
        m_ev = sem("m_ev")
        n_x = sems("n_x", 2)
        n_t = sem("n_t")
        n_r = sem("n_r")
        n_q = sem("n_q")
        n_b = sem("n_b")
        n_e = sem("n_e")
        n_h = sem("n_h")
        n_hi = sem("n_hi")
        n_lo = sem("n_lo")
        n_s = sem("n_s")
        n_k = sem("n_k")
        u_d = sem("u_d")
        u_g_ = sem("u_g_")
        u_m = sem("u_m")
        u_h = sem("u_h")
        u_l = sem("u_l")
        u_s = sem("u_s")
        y_b = sem("y_b")
        y_t = sem("y_t")
        y_d = sem("y_d")
        y_q = sem("y_q")
        y_n = sem("y_n")
        y_g = sem("y_g")
        y_o = sem("y_o")
        y_s = sems("y_s", 3)
        y_f = sem("y_f")
        y_fs = sem("y_fs")
        s_lf = sem("s_lf")
        s_const = sem("s_const")
        s_cr = sem("s_cr")
        s_fc = sem("s_fc")
        s_fa = sem("s_fa")
        s_fp = sem("s_fp")
        s_fs = sem("s_fs")
        s_lo_ = sem("s_lo_")
        s_fz = sem("s_fz")
        s_hl = sems("s_hl", 2)
        s_bh = sem("s_bh")
        s_b = sem("s_b")
        f_s = sem("f_s")
        f_m = sem("f_m")
        f_e = sem("f_e")
        f_r = sem("f_r")
        f_n = sem("f_n")
        f_t = sem("f_t")
        f_h = sem("f_h")
        f_l = sem("f_l")
        f_o = sem("f_o")
        o_c = sem("o_c")
        o_x = sem("o_x")
        o_h = sem("o_h")
        o_l = sem("o_l")
        b_z = sem("b_z")
        b_c = sem("b_c")
        b_m = sem("b_m")
        b_e = sem("b_e")
        b_l = sem("b_l")
        b_s = sem("b_s")
        b_k = sem("b_k")
        b_t = sem("b_t")
        b_w = sem("b_w")
        b_h = sem("b_h")
        b_lo = sem("b_lo")
        b_o = sem("b_o")

        q_raw = w_raw[:, 0:2].rearrange("p a k n -> p a (k n)")
        k_raw = w_raw[:, 2:4].rearrange("p a k n -> p a (k n)")
        q_hi = w_hi[:].rearrange("p a k n -> p a (k n)")
        q_lo = w_lo[:].rearrange("p a k n -> p a (k n)")
        F_STEPS = 2 * TT
        F_USES = [(s, b) for s in range(F_STEPS) for b in range(1 if s % TT < 4 else 2)]
        F_N = len(F_USES)

        def f_cum(s):
            return sum(1 for x, _ in F_USES if x <= s)

        B_ONE = [(c, kb, max(0, kb * P - 512 * c)) for c in range(2) for kb in range(4 * c + 3, -1, -1)]
        B_STEPS = [(par,) + x for x in B_ONE for par in range(2)]
        B_N = len(B_STEPS)
        B_LAST = [max(k for k, x in enumerate(B_STEPS) if x[0] == g % 2 and x[1] == g // 2) for g in range(4)]
        assert B_N % 4 == 0 and TT == 8
        SCALE = HD ** -0.5
        BIG = 40.0
        LN_EXP = "natural_log_exp_and_others"

        R_CONV = 7 * LT + 1
        R_LOGA = R_CONV + 4 + LT
        R_ONE = R_LOGA + 3
        R_COLS = R_ONE + 2 + LT + 2 + 1
        R_ROWS = R_COLS + 4
        D_SELF, D_MAX, D_MIN = 4, 8, 10
        D_FOX, D_SB, D_P = D_MIN + 3, D_MIN + 6, D_MIN + 7
        D_LAST = D_P + 3

        def y_bank(tt):
            return (psT[:, 0:2], psB[:, 1:3])[tt % 2]

        def z_bank(k):
            return (psA[:, 0], psB[:, 0], psT[:, 0])[k % 3]


        block = ctx.enter_context(nc.Block())

        ADA1 = 2 * KT * P // 512
        ADA2 = 4 * KT * P // 512
        ADA_IN = ADA2 - 2 * WT
        NSMALL = 16
        pools = (i["cache_fox_k"][0].rearrange("n t h d -> n t (h d)"),
                 i["cache_sb_k"][0].rearrange("n t h d -> n t (h d)"))
        ALPHA = 2.0 ** 0.25
        EPS = 1e-5
        NF = [sum(GROUPS[:k]) for k in range(len(GROUPS) + 1)]
        G_UP0 = [KT + 2 * NF[k] + KT * k for k in range(len(GROUPS))]
        G_DN0 = [KT + 2 * NF[k + 1] + KT * k for k in range(len(GROUPS))]
        w_out = i["w_out"][0].rearrange("(k p) n -> p k n", p=P)
        w_up = i["w_up"][0].rearrange("(k p) n -> p k n", p=P)
        w_down = i["w_down"][0].rearrange("(k p) n -> p k n", p=P)
        x_rows_d = i["x_prompt"][0].rearrange("(t p) d -> p t d", p=P)
        xs_rows_d = i["x_sample"].rearrange("b t d -> (b t) d")
        vpools = (i["cache_fox_v"][0].rearrange("n t h d -> n t (h d)"),
                  i["cache_sb_v"][0].rearrange("n t h d -> n t (h d)"))
        y_rows_d = o["y_prompt"][0].rearrange("(t p) d -> p t d", p=P)

        @block.sync
        def _(sp):
            small = 0

            def load(dst, src):
                nonlocal small
                small += 16
                sp.dma_start(dst, src).then_inc(s_small, 16)

            sp.dma_start(c_rows[0:1], i["c_prompt"]).then_inc(s_c, 16)
            sp.dma_start(c_rows[1:NC], i["c_sample"]).then_inc(s_c, 16)
            for n in range(2):
                sp.dma_start(w_ada1[:, n], w_ada[:, :, n * 512:n * 512 + 512]).then_inc(s_al[n], 16)
            at = 0
            for name in ("b_ada", "w_lru_conv", "b_lru_conv", "b_rgate", "b_igate", "lru_lambda", "ln1_g", "ln1_b"):
                src = i[name]
                if len(src.shape) == 3:
                    src = src.rearrange("a b c -> a (b c)")
                src = src.rearrange("a (r p) -> (a r) p", p=P)
                load(vec_rows[at:at + src.shape[0], 0], src)
                at += src.shape[0]
            load(vec_rows[0:3 * FT, 1], i["w_ffn_conv"].rearrange("a k (f p) -> (a k f) p", p=P))
            load(vec_rows[3 * FT:4 * FT, 1], i["b_ffn_conv"].rearrange("a (f p) -> (a f) p", p=P))
            load(vec_rows[0:NB * 3 * LT, 2], i["state_lru_conv"].rearrange("a b k (f p) -> (a b k f) p", p=P))
            load(vec_rows[NB * 3 * LT:NVC, 2], i["state_lru_h"].rearrange("a b (f p) -> (a b f) p", p=P))
            sfc = i["state_ffn_conv"].rearrange("a b k (f p) -> (a b k f) p", p=P)
            for n in range(3):
                r = min(P, NVD - n * P)
                load(vec_rows[0:r, 3 + n], sfc[n * P:n * P + r])
            load(xs_rows, i["x_sample"].rearrange("b t d -> (b t) d"))
            sp.dma_start(table[:], i["page_table"].rearrange("b n -> (b n)").rearrange("(a n) -> a n", a=1)).then_inc(s_tab, 16)
            assert small == 16 * NSMALL
            xv = i["x_prompt"][0].rearrange("(t p) d -> p t d", p=P)
            for h in range(2):
                sp.dma_start(x_rows[:, h * TT // 2:(h + 1) * TT // 2], xv[:, h * TT // 2:(h + 1) * TT // 2]).then_inc(s_x[h], 16)

            def ada_load(n, slot):
                sp.wait_ge(s_amm, n - 1)
                sp.dma_start(w_ada1[:, slot], w_ada[:, :, ds(n * 512, 512)]).then_inc(s_al[slot], 16)

            def w_load(n, slot, col):
                sp.wait_ge(s_wlo, n + 1)
                sp.dma_start(w_raw[:, slot], w_in[:, :, ds(col, P)]).then_inc(s_wl[slot], 16)

            for n in range(2, ADA1):
                ada_load(n, n % 2)
            for j, base in enumerate((FQ, SQ)):
                w_load(j, j, base)
            for n in range(ADA1, ADA1 + ADA_IN):
                ada_load(n, n % 2)

            def pages(u, b, kind):
                sp.wait_ge(s_km, 8 * u + 8)
                sp.dma_start(q_row[:, kind], sq_scr[ds(b, 1), kind * W:kind * W + W].to_broadcast([P, W])).then_inc(s_ql[kind], 16)
                for p in range(NPG):
                    page = sp.value_load(table[0:1, ds(b * NPG + p, 1)], min_val=0, max_val=NPOOL - 1)
                    sp.wait_ge(s_kfree, 8 * u + p + 1)
                    if kind == 0:
                        sp.dma_start(lf_pages[:, p, ds(b, 1), :].rearrange("p a h -> p (a h)"),
                                     i["cache_fox_logf"][0][ds(page, 1)].rearrange("a t h -> (a t) h")).then_inc(s_lf, 16)
                    sp.dma_start(k_page[:, p], pools[kind][ds(page, 1)].rearrange("a t w -> (a t) w")).then_inc(s_kl[p], 16)

            def q_tile(t, columns):
                for j in range(2):
                    w_load(2 * t + j + 2, j, columns[j])
                    ada_load(ADA1 + ADA_IN + 2 * t + j, j)

            with sp.Fori(0, WT - 1) as t:
                q_tile(t, (FQ + P * t + P, SQ + P * t + P))
            q_tile(WT - 1, (FK, SK))
            sp.wait_ge(s_tab, 16)

            def kv_tile(t, columns):
                for j in range(4):
                    w_load(2 * WT + 4 * t + j + 2, j % 2, columns[j])
                    if j == 0:
                        sp.wait_ge(s_sq, 16)
                    pages(4 * t + j, 2 * t + j // 2, j % 2)

            with sp.Fori(0, WT - 1) as t:
                kv_tile(t, (FV + P * t, SV + P * t, FK + P * t + P, SK + P * t + P))
            kv_tile(WT - 1, (FV + P * WT - P, SV + P * WT - P, XR, XG))
            for t in range(LT):
                for j, base in enumerate((XR, XG)):
                    if t < LT - 1:
                        w_load(6 * WT + 2 * t + j + 2, j, base + P * t + P)
                    elif j == 0:
                        sp.wait_ge(s_wlo, 6 * WT + 2 * LT + 1)
                        sp.dma_start(w_raw[:, 0, :, 0:H], w_in[:, :, FG:FG + H]).then_inc(s_wl[0], 16)
                    pages(4 * WT + 2 * t + j, 2 * WT + t, j)

            sp.dma_start(bfg[:], i["b_fgate"].rearrange("a h -> h a")).then_inc(s_c, 16)
            sp.wait_ge(s_fc, 10)
            for n in range(4):
                sp.dma_start(f_scr[n], fparts[:, n].bitcast(F32)).then_inc(s_fs, 16)
            sp.wait_ge(s_fp, 2)
            sp.dma_start(o["p_fox_logf"][0, 0].rearrange("(t p) h -> p t h", p=P), lg_out[:, 0:TT]).then_inc(s_lo_, 16)
            sp.dma_start(o["s_fox_logf"][0, :, 0], lg_out[0:NB, TT]).then_inc(s_lo_, 16)
            sp.wait_ge(s_fs, 64)
            sp.wait_ge(s_lo_, 32)
            sp.wait_ge(s_fz, 2)
            for h in range(2):
                sp.wait_ge(s_st[h], 16 * 2 * WT)
                sp.wait_ge(s_so[h], 16 * 2 * WT)

            def head_loads(fox, t, par):
                hd = 2 * t + par
                row = hd * HD + (0 if fox else W)
                sp.wait_ge(s_b, hd + 1 + (0 if fox else H))
                for half in range(2):
                    sp.dma_start(q_raw[half * HD:half * HD + HD, par], qk_scr[0, ds(row, HD)]).then_inc(s_hl[par], 16)
                    sp.dma_start(k_raw[half * HD:half * HD + HD, par], qk_scr[1, ds(row, HD)]).then_inc(s_hl[par], 16)
                v = o["p_fox_v" if fox else "p_sb_v"][0, 0].rearrange("(t p) h d -> p t h d", p=P)
                sp.dma_start(v_raw[:, par], v[:, :, ds(hd, 1)].rearrange("p t a d -> p t (a d)")).then_inc(s_hl[par], 16)
                if fox:
                    sp.wait_ge(f_s, F_STEPS * t)
                    sp.dma_start(fq_rows[0:2, par].bitcast(F32), f_scr[0:2, ds(hd, 1)].rearrange("n a s -> n (a s)")).then_inc(s_hl[par], 16)
                    sp.dma_start(fk_rows[2:4, par].bitcast(F32), f_scr[2:4, ds(hd, 1)].rearrange("n a s -> n (a s)")).then_inc(s_hl[par], 16)

            with sp.Fori(0, WT) as t:
                for par in range(2):
                    head_loads(True, t, par)
            with sp.Fori(0, WT) as t:
                for par in range(2):
                    head_loads(False, t, par)
            sp.wait_ge(s_gw0, 1)
            for g, name in enumerate(("w_rgate", "w_igate")):
                bw = i[name].shape[2]
                for n in range(i[name].shape[1]):
                    r = n * bw % P
                    sp.dma_start(gate_w[r:r + bw, g, n * bw // P, r:r + bw], i[name][0, n]).then_inc(s_gw, 16)
            sp.dma_start(o["s_lru_conv"][0, :, 0:2], i["state_lru_conv"][0, :, 1:3]).then_inc(s_cc, 16)
            sp.dma_start(o["s_ffn_conv"][0, :, 0:1], i["state_ffn_conv"][0, :, 1:2]).then_inc(s_cc, 16)
            with sp.Fori(0, NB) as b:
                for kind in range(2):
                    for p in range(NPG):
                        page = sp.value_load(table[0:1, ds(b * NPG + p, 1)], min_val=0, max_val=NPOOL - 1)
                        if p == 0:
                            sp.wait_ge(d_v, 2 * b + kind + 1)
                        sp.dma_start(v_page[:, kind, p], vpools[kind][ds(page, 1)].rearrange("a t w -> (a t) w")).then_inc(s_vl[kind], 16)
            sp.wait_ge(r_p, 5)
            sp.wait_ge(r_d, R_ROWS)
            sp.dma_start(o["p_lru_conv"][0, 0], lru_rows[0:3]).then_inc(s_lr, 16)
            sp.dma_start(o["p_lru_h"][0], lru_rows[3:4]).then_inc(s_lr, 16)
            sp.dma_start(o["s_lru_h"][0], lru_rows[4:4 + NB]).then_inc(s_lr, 16)
            sp.dma_start(o["s_lru_conv"][0, :, 2], lru_rows[4 + NB:4 + 2 * NB]).then_inc(s_lr, 16)

            def g_load(m, slot, src, nk=KT):
                sp.wait_ge(g_ws, m + 1)
                sp.dma_start(w_raw[:, slot, 0:nk], src).then_inc(g_wl[slot], 16)

            sp.wait_ge(s_b, 2 * H + 2)
            with sp.Fori(0, KT // 2) as t:
                for j in range(2):
                    g_load(2 * t + j, j, w_out[:, :, ds((2 * t + j) * P, P)])
            for j in range(2):
                g_load(KT + j, j, w_up[:, :, j * DFF:j * DFF + P])
            for tt in range(TT):
                if tt == 0:
                    sp.wait_ge(d_v, 2 * NB + 2)
                    sp.wait_ge(s_lr, 64)
                    sp.wait_ge(d_d, D_LAST)
                    sp.wait_ge(d_t, 4)
                    sp.wait_ge(r_p, 5)
                if tt >= 2:
                    sp.wait_ge(n_r, 6 * (tt - 2) + 6)
                sp.dma_start(x_tile[:, tt % 2], x_rows_d[:, tt]).then_inc(n_x[tt % 2], 16)
            sp.dma_start(xs_hat[:, 0], xs_rows_d).then_inc(y_b, 16)
            for k, gs in enumerate(GROUPS):
                with sp.Fori(1 if k == 0 else 0, gs) as f:
                    for j in range(2):
                        g_load(G_UP0[k] + 2 * f + j, j, w_up[:, :, ds((NF[k] + f) * P + j * DFF, P)])
                with sp.Fori(0, KT // 2) as t:
                    for j in range(2):
                        g_load(G_DN0[k] + 2 * t + j, j, w_down[:, NF[k]:NF[k] + gs, ds((2 * t + j) * P, P)], gs)
            sp.wait_ge(g_pm, G_DN0[-1] + KT + 2)
            sp.dma_start(ln2g[:], i["ln2_g"].to_broadcast([P, D])).then_inc(y_b, 16)
            sp.dma_start(ln2b[:], i["ln2_b"].to_broadcast([P, D])).then_inc(y_b, 16)
            for tt in range(TT + 1):
                sp.wait_ge(y_o, tt + 1)
                if tt < TT:
                    sp.dma_start(y_rows_d[:, tt], y_tile[:, tt % 3]).then_inc(y_s[tt % 3], 16)
                else:
                    sp.dma_start(o["y_sample"][:, 0], y_tile[0:NB, tt % 3]).then_inc(y_s[tt % 3], 16)
            sp.wait_ge(y_f, 4)
            sp.dma_start(o["p_ffn_conv"][0, 0].rearrange("r (f p) -> r f p", p=P), ffn_rows[0:2]).then_inc(y_fs, 16)
            sp.dma_start(o["s_ffn_conv"][0, :, 1].rearrange("r (f p) -> r f p", p=P), ffn_rows[2:2 + NB]).then_inc(y_fs, 16)
            for n in range(3):
                sp.wait_ge(y_s[n], 16 * 3)
            sp.wait_ge(y_fs, 32)
            sp.wait_ge(s_lr, 64)
            sp.wait_ge(s_cc, 32)
            sp.wait_ge(s_sq, 16 * 5)

        @block.gpsimd
        def _(pool):
            nc.gpsimd.memset(ident[:], 0.0).then_inc(s_idz, 1)
            pool.wait_ge(s_idz, 1)
            nc.gpsimd.affine_select(out=ident[:], in_=ident[:], compare_op=ALU.not_equal, fill=1.0, base=0,
                                    pattern=[[-1, P]], channel_multiplier=1).then_inc(s_ident, 1)

            nc.gpsimd.memset(mask_f[:], 0.0)
            nc.gpsimd.memset(tri[:], 1.0)
            nc.gpsimd.memset(ones[:], 1.0).then_inc(s_const, 1)
            pool.wait_ge(s_const, 1)
            nc.gpsimd.affine_select(out=mask_f[:, 0], in_=mask_f[:, 0], compare_op=ALU.is_ge, fill=-1e30, base=0,
                                    pattern=[[-1, P]], channel_multiplier=1)
            nc.gpsimd.affine_select(out=mask_f[:, 1], in_=mask_f[:, 1], compare_op=ALU.is_ge, fill=-1e30, base=-1,
                                    pattern=[[1, P]], channel_multiplier=-1)
            nc.gpsimd.affine_select(out=tri[:, 0], in_=tri[:, 0], compare_op=ALU.is_ge, fill=0.0, base=0,
                                    pattern=[[-1, P]], channel_multiplier=1)
            nc.gpsimd.affine_select(out=tri[:, 1], in_=tri[:, 1], compare_op=ALU.is_ge, fill=0.0, base=-1,
                                    pattern=[[1, P]], channel_multiplier=-1).then_inc(s_const, 1)

            def unit(u, kind, round_):
                for p in range(NPG):
                    if p == 0:
                        pool.wait_ge(s_ql[kind], 16 * round_)
                    pool.wait_ge(s_kl[p], 16 * (u + 1))
                    last = nc.gpsimd.tensor_tensor(k_page[:, p], k_page[:, p], q_row[:, kind], ALU.mult)
                    last.then_inc(s_km, 1)

            pool.sem_inc(s_km, 2 * NPG)
            with pool.Fori(0, WT) as t:
                for j in range(4):
                    unit(4 * t + j, j % 2, 2 * t + j // 2 + 1)
            with pool.Fori(0, LT) as t:
                for j in range(2):
                    unit(4 * WT + 2 * t + j, j, 2 * WT + t + 1)

        @block.vector
        def _(dve):
            dve.sem_inc(s_wlo, 2)
            dve.sem_inc(s_kfree, NPG)
            dve.wait_ge(s_c, 32)
            nc.vector.tensor_scalar(c_half, c_rows, 0.5, None, ALU.mult).then_inc(s_csil, 1)
            dve.wait_ge(s_ctanh, 1)
            nc.vector.scalar_tensor_tensor(out=c_rows, in0=c_rows, scalar=1.0, in1=c_half,
                                           op0=ALU.add, op1=ALU.mult).then_inc(s_csil, 1)
            dve.wait_ge(s_vt, 1)
            nc.vector.tensor_copy(cT[:], psT[:, 0, 0:KT * NC].rearrange("p (k c) -> p k c", c=NC)).then_inc(s_vte, 1)
            dve.wait_ge(s_vt, 2)
            nc.vector.tensor_copy(vecT[:, 0:NVA + NVB + NVC], psT[:, 1, 0:NVA + NVB + NVC]).then_inc(s_vte, 1)
            nc.vector.tensor_copy(vecT[:, A_SFC:A_SFC + NVD], psT[:, 0, 0:NVD]).then_inc(s_vte, 1)
            dve.wait_ge(s_vte, 3)

            def mod_evict(n, chunk, bank):
                dve.wait_ge(s_amm, n + 1)
                nc.vector.tensor_tensor(modT[:, ds(4 * chunk, 4)], bank.rearrange("p (k c) -> p k c", c=NC),
                                        vecT[:, ds(4 * chunk, 4)].rearrange("p (k c) -> p k c", c=1).to_broadcast([P, 4, NC]),
                                        ALU.add).then_inc(s_aev, 1)

            for n in range(ADA1):
                mod_evict(n, n, psA[:, n % 2, 0:4 * NC])
            dve.wait_ge(s_aev, ADA1)
            nc.vector.tensor_scalar(modT[:, KT:2 * KT], modT[:, KT:2 * KT], 1.0, None, ALU.add).then_inc(s_one, 1)

            def split(n, half, round_, cols=P):
                dve.wait_ge(s_wl[half], 16 * round_)
                dve.wait_ge(s_pm, n + 1)
                nc.vector.tensor_copy(w_hi[:, half, :, 0:cols], w_raw[:, half, :, 0:cols]).then_inc(s_whi, 1)
                dve.wait_ge(s_whi, n + 1)
                nc.vector.tensor_tensor(w_lo[:, half, :, 0:cols], w_raw[:, half, :, 0:cols], w_hi[:, half, :, 0:cols].bitcast(F32),
                                        ALU.subtract).then_inc(s_wlo, 1)

            split(0, 0, 1)
            for h in range(2):
                for f in range(KT):
                    n = h * KT + f
                    dve.wait_ge(s_hf, n + 1)
                    nc.vector.tensor_copy(acts_hi[:, f, h * 512:h * 512 + 512], h_full[:, n % 2]).then_inc(s_hhi, 1)
                    dve.wait_ge(s_hhi, n + 1)
                    nc.vector.tensor_tensor(acts_lo[:, f, h * 512:h * 512 + 512], h_full[:, n % 2],
                                            acts_hi[:, f, h * 512:h * 512 + 512].bitcast(F32), ALU.subtract).then_inc(s_hlo, 1)
            dve.wait_ge(s_vt, 3)
            dve.wait_ge(s_one, 1)
            nc.vector.tensor_tensor(hs_full[:], psB[:, 2, 0:KT * NB].rearrange("p (k b) -> p k b", b=NB), modT[:, KT:2 * KT, 1:NC], ALU.mult).then_inc(s_hs, 1)
            dve.wait_ge(s_hs, 1)
            nc.vector.tensor_tensor(hs_full[:], hs_full[:], modT[:, 0:KT, 1:NC], ALU.add).then_inc(s_hs, 1)
            dve.wait_ge(s_hs, 2)
            nc.vector.tensor_copy(acts_hi[:, :, SEQ:TOK], hs_full[:]).then_inc(s_hs, 1)
            dve.wait_ge(s_hs, 3)
            nc.vector.tensor_tensor(acts_lo[:, :, SEQ:TOK], hs_full[:], acts_hi[:, :, SEQ:TOK].bitcast(F32), ALU.subtract).then_inc(s_hs, 1)

            for n in range(ADA1, ADA1 + ADA_IN):
                mod_evict(n, n, psT[:, n % 2, 0:4 * NC])

            def reduce(u, kind, b):
                for p in range(NPG):
                    dve.wait_ge(s_km, 8 * u + p + 1 + 2 * NPG)
                    nc.vector.tensor_reduce(scores[:, kind, p, ds(b, 1), :].rearrange("p a h -> p (a h)"),
                                            k_page[:, p].rearrange("p (h d) -> p h d", d=HD),
                                            AX.X, ALU.add).then_inc(s_kfree, 1)

            with dve.Fori(0, WT) as t:
                for j in range(2):
                    split(2 * t + j + 1, 1 - j, t + j + 1)
                    c = ADA1 + ADA_IN + 2 * t + j
                    mod_evict(c, c, psT[:, j, 0:4 * NC])
            with dve.Fori(0, WT) as t:
                for j in range(4):
                    split(2 * WT + 4 * t + j + 1, (j + 1) % 2, WT + 2 * t + (j + 1) // 2 + 1)
                    reduce(4 * t + j, j % 2, 2 * t + j // 2)
            for t in range(LT):
                for j in range(2):
                    n = 6 * WT + 2 * t + j + 1
                    split(n, n % 2, n // 2 + 1, H if n == 6 * WT + 2 * LT else P)
                    reduce(4 * WT + 2 * t + j, j, 2 * WT + t)
            dve.wait_ge(s_aev, ADA1 + ADA2)
            nc.vector.tensor_scalar(modT[:, 4 * KT:5 * KT], modT[:, 4 * KT:5 * KT], 1.0, None, ALU.add).then_inc(s_one, 1)

            V = nc.vector
            fc = 0

            def step(ins):
                nonlocal fc
                fc += 1
                ins.then_inc(s_fc, 1)

            dve.wait_ge(s_const, 2)
            V.tensor_copy(ident_r[:], ident[:])
            V.tensor_copy(mask_r[:], mask_f[:]).then_inc(s_cr, 1)
            dve.wait_ge(s_c, 48)
            dve.wait_ge(s_pe, 6 * WT + 2 * LT + 3)
            for h in range(2):
                dve.wait_ge(s_st[h], 16 * 2 * WT)
                dve.wait_ge(s_so[h], 16 * 2 * WT)
            step(V.tensor_scalar(fg_y[:], fgT, bfg[:, 0:1], -1.0, ALU.add, ALU.mult))
            dve.wait_ge(s_fc, 1)
            step(V.tensor_scalar(fg_e[:], fg_y[:], BIG, None, ALU.min))
            dve.wait_ge(s_fa, 2)
            step(V.tensor_tensor(fg_e[:], fg_e[:], fg_y[:], ALU.max))
            dve.wait_ge(s_fc, 3)
            step(V.tensor_scalar(lgT[:], fg_e[:], -1.0, None, ALU.mult))
            dve.wait_ge(s_fc, 4)
            step(V.tensor_tensor_scan(fcum[:], ones[0:H].to_broadcast([H, SEQ]), lgT[:, 0:SEQ], 0.0, ALU.mult, ALU.add))
            dve.wait_ge(s_fc, 5)
            step(V.tensor_copy(fparts[:, 0], fcum[:]))
            dve.wait_ge(s_fc, 6)
            step(V.tensor_tensor(fparts[:, 1], fcum[:], fparts[:, 0].bitcast(F32), ALU.subtract))
            step(V.tensor_scalar(fparts[:, 2], fparts[:, 0].bitcast(F32), -1.0, None, ALU.mult))
            dve.wait_ge(s_fc, 7)
            step(V.tensor_scalar(fparts[:, 3], fparts[:, 1].bitcast(F32), -1.0, None, ALU.mult))
            dve.wait_ge(s_fp, 1)
            step(V.tensor_copy(lg_out[:, 0:TT], psT[:, 0, 0:TT * H].rearrange("p (t h) -> p t h", h=H)))
            V.tensor_copy(lg_out[0:NB, TT], psT[0:NB, 0, TT * H:TT * H + H]).then_inc(s_fp, 1)

            dve.sem_inc(s_b, 2)

            def build(fox, t, par):
                n = 2 * t + par + (0 if fox else H)
                dve.wait_ge(s_hl[par], (16 * 7 * (t + 1)) if fox else (16 * 7 * WT + 16 * 5 * (t + 1)))
                V.tensor_scalar(q_hi[:, par], q_raw[:, par], SCALE, None, ALU.mult)
                V.tensor_copy(k_st[:, par], k_raw[:, par])
                V.tensor_copy(v_st[:, par, :, 0:HD], v_raw[:, par]).then_inc(s_bh, 1)
                dve.wait_ge(s_bh, n + 1)
                V.scalar_tensor_tensor(out=q_lo[:, par], in0=q_raw[:, par], scalar=SCALE, in1=q_hi[:, par].bitcast(F32),
                                       op0=ALU.mult, op1=ALU.subtract)
                V.tensor_tensor(k_st[HD:P, par], k_raw[HD:P, par], k_st[HD:P, par].bitcast(F32), ALU.subtract)
                V.tensor_tensor(v_st[:, par, :, HD:2 * HD], v_raw[:, par], v_st[:, par, :, 0:HD].bitcast(F32), ALU.subtract).then_inc(s_b, 1)

            def out_bank(g, n, par, tile, q0, bank):
                r = slice(par * HD, par * HD + HD)
                dve.wait_ge(o_c, n + 1)
                V.tensor_tensor(o_sum[r], bank[0:HD], o_low[r], ALU.add).then_inc(o_x, 1)
                dve.wait_ge(o_x, n + 1)
                V.tensor_copy(acts_hi[r, ds(tile, 1), q0:q0 + 512].rearrange("p a n -> p (a n)"), o_sum[r]).then_inc(o_h, 1)
                dve.wait_ge(o_h, n + 1)
                V.tensor_tensor(acts_lo[r, ds(tile, 1), q0:q0 + 512].rearrange("p a n -> p (a n)"), o_sum[r],
                                acts_hi[r, ds(tile, 1), q0:q0 + 512].rearrange("p a n -> p (a n)").bitcast(F32), ALU.subtract).then_inc(o_l, 1)

            dve.wait_ge(s_fs, 64)
            dve.wait_ge(s_lo_, 32)
            V.memset(fq_rows[:].bitcast(F32), 0.0)
            V.memset(fk_rows[:].bitcast(F32), 0.0).then_inc(s_fz, 1)
            dve.wait_ge(s_fz, 1)
            V.memset(fq_rows[0:4].bitcast(F32), 1.0)
            V.memset(fk_rows[0:4].bitcast(F32), 1.0).then_inc(s_fz, 1)
            with dve.Fori(0, WT) as t:
                build(True, t, 0)
                for s in range(F_STEPS + 5):
                    if s < F_STEPS:
                        dve.wait_ge(f_s, F_STEPS * t + s + 1)
                        nk = (s % TT + 1) * P
                        ps = proj_ps[s % 2][:, 0:2].rearrange("p a n -> p (a n)")[:, 0:nk]
                        V.tensor_reduce(row_max[:, s:s + 1], ps, AX.X, ALU.max, negate=True).then_inc(f_m, 1)
                    if 1 <= s < F_STEPS + 1:
                        x = s - 1
                        dve.wait_ge(f_e, F_STEPS * t + x + 1)
                        V.reciprocal(row_inv[:, x:x + 1], row_sum[:, x:x + 1]).then_inc(f_r, 1)
                        dve.wait_ge(f_r, F_STEPS * t + x + 1)
                        nk = (x % TT + 1) * P
                        V.tensor_scalar(probs[:, x % 3, 0:nk], probs[:, x % 3, 0:nk], row_inv[:, x:x + 1], None, ALU.mult).then_inc(f_n, 1)
                    if 2 <= s < F_STEPS + 2:
                        x = s - 2
                        for u, (y, b) in enumerate(F_USES):
                            if y == x:
                                nb = min(4, x % TT + 1 - 4 * b)
                                dve.wait_ge(f_h, F_N * t + u + 1)
                                V.tensor_tensor(pt_lo[:, x % 2, 4 * b:4 * b + nb], psT[:, b, 0:nb * P].rearrange("p (k n) -> p k n", n=P),
                                                pt_hi[:, x % 2, 4 * b:4 * b + nb].bitcast(F32), ALU.subtract).then_inc(f_l, 1)
                    if s >= 7 and (s - 4) % 4 == 3:
                        g = (s - 4) // 4
                        out_bank(g, 4 * t + g, g // 2, t, g % 2 * 512, proj_ps[g % 2][:, 2])
                    if s == 4:
                        build(True, t, 1)

            with dve.Fori(0, WT) as t:
                build(False, t, 0)
                build(False, t, 1)
                for k in range(B_N + 5):
                    if k < B_N:
                        par, c, kb, q0 = B_STEPS[k]
                        dve.wait_ge(b_c, B_N * t + k + 1)
                        V.tensor_scalar(z_e[:, k % 3, q0:512], z_s[:, k % 4, q0:512], BIG, None, ALU.min).then_inc(b_m, 1)
                    if 2 <= k < B_N + 2:
                        x = k - 2
                        par, c, kb, q0 = B_STEPS[x]
                        dve.wait_ge(b_k, B_N * t + x + 1)
                        V.tensor_tensor(z_w[:, x % 4, q0:512], z_s[:, x % 4, q0:512], proj_ps[par][:, 2, q0:512], ALU.subtract).then_inc(b_t, 1)
                    if 4 <= k < B_N + 4:
                        x = k - 4
                        par, c, kb, q0 = B_STEPS[x]
                        dve.wait_ge(b_w, B_N * t + x + 1)
                        dve.wait_ge(b_o, B_N * t + max(0, x - 1))
                        V.tensor_copy(w_hi2[:, x % 2, q0:512], z_w[:, x % 4, q0:512]).then_inc(b_h, 1)
                    if 1 <= k < B_N + 1:
                        x = k - 1
                        par, c, kb, q0 = B_STEPS[x]
                        dve.wait_ge(b_l, B_N * t + x + 1)
                        V.tensor_tensor(z_sp[:, x % 4, q0:512], z_e[:, x % 3, q0:512], z_s[:, x % 4, q0:512], ALU.max).then_inc(b_s, 1)
                    if 4 <= k < B_N + 4:
                        x = k - 4
                        par, c, kb, q0 = B_STEPS[x]
                        dve.wait_ge(b_h, B_N * t + x + 1)
                        V.tensor_tensor(w_lo2[:, x % 2, q0:512], z_w[:, x % 4, q0:512], w_hi2[:, x % 2, q0:512].bitcast(F32), ALU.subtract).then_inc(b_lo, 1)
                    for g in range(4):
                        if k == min(B_LAST[g] + 5, B_N + 4):
                            out_bank(g, 4 * WT + 4 * t + g, g % 2, WT + t, g // 2 * 512, proj_ps[g % 2][:, 1])

            rd = 0

            def rstep(ins):
                nonlocal rd
                rd += 1
                ins.then_inc(r_d, 1)
                dve.wait_ge(r_d, rd)

            V.memset(gate_w[:], 0.0).then_inc(s_gw0, 1)
            for t in range(LT):
                rstep(V.tensor_scalar(r_xc[:, t], xrT[:, t], vecT[:, A_WLC + 3 * LT + t:A_WLC + 3 * LT + t + 1],
                                      vecT[:, A_BLC + t:A_BLC + t + 1], ALU.mult, ALU.add))
                for k in range(3):
                    w = vecT[:, A_WLC + k * LT + t:A_WLC + k * LT + t + 1]
                    rstep(V.scalar_tensor_tensor(out=r_xc[:, t, 3 - k:SEQ], in0=xrT[:, t, 0:SEQ - 3 + k], scalar=w,
                                                 in1=r_xc[:, t, 3 - k:SEQ], op0=ALU.mult, op1=ALU.add))
                    past = vecT[:, A_SLC:A_SLH].rearrange("p (b k f) -> p b k f", k=3, f=LT)[:, :, k, t]
                    now = r_xc[:, t, SEQ:TOK]
                    rstep(V.scalar_tensor_tensor(out=now, in0=past, scalar=w, in1=now, op0=ALU.mult, op1=ALU.add))
            rstep(V.tensor_scalar(r_c[:, 0:2], vecT[:, A_BR:A_BR + 2 * LT].rearrange("p (g t) -> p g t", t=LT), 0.5, None, ALU.mult))
            assert rd == R_CONV
            rstep(V.tensor_scalar(r_c[:, 2], vecT[:, A_LAM:A_LAM + LT], -1.0, None, ALU.mult))
            rstep(V.tensor_scalar(r_c[:, 3], r_c[:, 2], BIG, None, ALU.min))
            dve.wait_ge(r_s, 2)
            rstep(V.tensor_tensor(r_c[:, 3], r_c[:, 3], r_c[:, 2], ALU.max))
            rstep(V.tensor_scalar(r_c[:, 4], r_c[:, 3], -4.0, None, ALU.mult))
            dve.wait_ge(r_s, 6)
            for t in range(LT):
                rstep(V.tensor_scalar(r_t[:, t], r_t[:, t], r_c[:, 4, t:t + 1], r_c[:, 4, t:t + 1], ALU.mult, ALU.add))
            assert rd == R_LOGA
            dve.wait_ge(r_s, 8)
            rstep(V.tensor_tensor(r_t[:], r_a[:], r_a[:], ALU.mult))
            rstep(V.tensor_scalar(r_t[:], r_t[:], 1.0, None, ALU.add))
            rstep(V.scalar_tensor_tensor(out=r_h[:], in0=r_h[:], scalar=-1.0, in1=r_t[:], op0=ALU.mult, op1=ALU.mult))
            assert rd == R_ONE
            rstep(V.scalar_tensor_tensor(out=r_i[:], in0=r_i[:], scalar=1.0, in1=r_xc[:], op0=ALU.add, op1=ALU.mult))
            dve.wait_ge(r_s, 9)
            rstep(V.scalar_tensor_tensor(out=r_i[:], in0=r_i[:], scalar=0.5, in1=r_h[:], op0=ALU.mult, op1=ALU.mult))
            for t in range(LT):
                rstep(V.tensor_tensor_scan(r_t[:, t, 0:SEQ], r_a[:, t, 0:SEQ], r_i[:, t, 0:SEQ], 0.0, ALU.mult, ALU.add))
            h0 = vecT[:, A_SLH:A_SLH + NB * LT].rearrange("p (b f) -> p f b", f=LT)
            rstep(V.tensor_tensor(r_t[:, :, SEQ:TOK], r_a[:, :, SEQ:TOK], h0, ALU.mult))
            rstep(V.tensor_tensor(r_t[:, :, SEQ:TOK], r_t[:, :, SEQ:TOK], r_i[:, :, SEQ:TOK], ALU.add))
            V.tensor_copy(lru_cols[:, :, 0:3], xrT[:, :, SEQ - 3:SEQ])
            V.tensor_copy(lru_cols[:, :, 3:4 + NB], r_t[:, :, SEQ - 1:TOK])
            rstep(V.tensor_copy(lru_cols[:, :, 4 + NB:4 + 2 * NB], xrT[:, :, SEQ:TOK]))
            assert rd == R_COLS
            dve.wait_ge(r_s, 10)
            rstep(V.tensor_tensor(r_xc[:], r_t[:], xgT[:], ALU.mult))
            rstep(V.tensor_copy(acts_hi[:, 2 * WT:KT], r_xc[:]))
            rstep(V.tensor_tensor(acts_lo[:, 2 * WT:KT], r_xc[:], acts_hi[:, 2 * WT:KT].bitcast(F32), ALU.subtract))
            dve.wait_ge(r_p, 5)
            rstep(V.tensor_copy(lru_rows[:], psA[0:4 + 2 * NB, 0, 0:DL]))
            assert rd == R_ROWS

            dd = 0

            def dstep(ins):
                nonlocal dd
                dd += 1
                ins.then_inc(d_d, 1)
                dve.wait_ge(d_d, dd)

            dstep(V.tensor_tensor(d_qk[:], smpT[:, 0:2 * WT:2], smpT[:, 2 * WT:6 * WT:4], ALU.mult))
            V.memset(d_hm[:], 0.0).then_inc(d_d, 1)
            dd += 1
            dve.wait_ge(d_d, dd)
            for t in range(WT):
                V.memset(d_hm[0:HD, t, 2 * t:2 * t + 1], 1.0)
                last = V.memset(d_hm[HD:P, t, 2 * t + 1:2 * t + 2], 1.0)
            dstep(last)
            for t in range(WT):
                V.tensor_tensor(d_zq[:, t], d_qk[:, t].rearrange("p (b a) -> p b a", a=1).to_broadcast([P, NB, H]),
                                d_hm[:, t].rearrange("p (a h) -> p a h", a=1).to_broadcast([P, NB, H]), ALU.mult)
            V.tensor_reduce(d_grp[:], ident[0:R48, 0:R48].rearrange("p (b h) -> p b h", h=H), AX.X, ALU.add)
            dstep(V.tensor_tensor(d_spread[:], lgT[:, SEQ:TOK].rearrange("p (b a) -> p b a", a=1).to_broadcast([H, NB, H]),
                                  ident[0:H, 0:H].rearrange("p (a h) -> p a h", a=1).to_broadcast([H, NB, H]), ALU.mult))
            assert dd == D_SELF
            dve.wait_ge(d_t, 2)
            dstep(V.tensor_copy(d_g[:, SEQ:SEQ + 1], psA[0:R48, 2, 1:2]))
            dstep(V.tensor_tensor_scan(d_g[:, 0:SEQ][:, ::-1], ones[0:R48].to_broadcast([R48, SEQ]),
                                       psT[0:R48].rearrange("p a n -> p (a n)")[:, ::-1], d_g[:, SEQ:SEQ + 1], ALU.mult, ALU.add))
            V.tensor_scalar(d_f[:, SEQ:SEQ + 1], psA[0:R48, 2, 0:1], SCALE, None, ALU.mult)
            dstep(V.scalar_tensor_tensor(out=d_f[:, 0:SEQ], in0=psA[0:R48, 0:2].rearrange("p a n -> p (a n)"), scalar=SCALE,
                                         in1=d_g[:, 1:SEQ + 1], op0=ALU.mult, op1=ALU.add))
            dstep(V.tensor_reduce(d_small[:, 0:1], d_f[:], AX.X, ALU.max, negate=True))
            assert dd == D_MAX
            dstep(V.tensor_scalar(d_z[:], psB[0:R48, 0:2].rearrange("p a n -> p (a n)"), SCALE, None, ALU.mult))
            dstep(V.tensor_scalar(d_e[:], d_z[:], BIG, None, ALU.min))
            assert dd == D_MIN
            dve.wait_ge(d_a, 1)
            dstep(V.reciprocal(d_small[:, 2:3], d_small[:, 1:2]))
            dstep(V.tensor_scalar(d_f[:], d_f[:], d_small[:, 2:3], None, ALU.mult))
            dstep(V.tensor_scalar(d_diag[:], ident[0:R48, 0:R48], d_f[:, SEQ:SEQ + 1], None, ALU.mult))
            assert dd == D_FOX
            dve.wait_ge(d_a, 3)
            dstep(V.tensor_tensor(d_e[:], d_e[:], d_z[:], ALU.max))
            dstep(V.tensor_tensor_scan(d_g[:, 0:SEQ][:, ::-1], ones[0:R48].to_broadcast([R48, SEQ]), d_e[:, ::-1], 0.0, ALU.mult, ALU.add))
            dstep(V.tensor_tensor(d_z[:], d_z[:], d_g[:, 0:SEQ], ALU.subtract))
            assert dd == D_SB
            dve.wait_ge(d_t, 4)
            V.tensor_copy(d_self[:], psA[0:NB, 2, 0:R48])
            V.tensor_copy(d_p[:, 0], psT[:, 0, 0:NPG * R48].rearrange("p (k n) -> p k n", n=R48))
            dstep(V.tensor_copy(d_p[:, 1], psT[:, 1, 0:NPG * R48].rearrange("p (k n) -> p k n", n=R48)))
            assert dd == D_P
            dve.wait_ge(d_v, 2 * NB + 2)
            ov = psA[:, 0, 0:4 * WT * NB].rearrange("p (k b e) -> p k b e", b=NB, e=2)
            V.tensor_copy(d_out[0:HD], ov[0:HD, :, :, 0])
            dstep(V.tensor_copy(d_out[HD:P], ov[HD:P, :, :, 1]))
            dstep(V.tensor_copy(acts_hi[:, 0:2 * WT, SEQ:TOK], d_out[:]))
            dstep(V.tensor_tensor(acts_lo[:, 0:2 * WT, SEQ:TOK], d_out[:], acts_hi[:, 0:2 * WT, SEQ:TOK].bitcast(F32), ALU.subtract))
            assert dd == D_LAST

            dve.sem_inc(g_ws, 2)

            def g_split(m, slot, round_, nk=KT):
                dve.wait_ge(g_wl[slot], 16 * round_)
                dve.wait_ge(g_pm, m + 1)
                V.tensor_copy(w_hi[:, slot, 0:nk], w_raw[:, slot, 0:nk]).then_inc(g_wh, 1)
                dve.wait_ge(g_wh, m + 1)
                V.tensor_tensor(w_lo[:, slot, 0:nk], w_raw[:, slot, 0:nk], w_hi[:, slot, 0:nk].bitcast(F32), ALU.subtract).then_inc(g_ws, 1)

            def col(ap):
                return ap.rearrange("p a n -> p (a n)")

            dve.wait_ge(s_lr, 64)
            g_split(0, 0, 1)
            with dve.Fori(0, KT // 2) as t:
                for j in range(2):
                    m = 2 * t + j
                    g_split(m + 1, 1 - j, t + 1 + j)
                    dve.wait_ge(m_ev, m + 1)
                    V.tensor_tensor(resT[:, ds(m, 1), SEQ:TOK], proj_ps[j][:, 2:3, CH - NB:CH], modT[:, ds(2 * KT + m, 1), 1:NC], ALU.mult).then_inc(g_ev[j], 1)
            k1 = slice(4 * KT, 5 * KT)
            V.tensor_tensor(ln_f[:, 0], vecT[:, A_L1G:A_L1G + KT], modT[:, k1, 0], ALU.mult)
            V.tensor_tensor(ln_f[:, 1], vecT[:, A_L1B:A_L1B + KT], modT[:, k1, 0], ALU.mult)
            V.tensor_scalar(ln_f[:, 2], vecT[:, A_L1G:A_L1G + KT], ALPHA, None, ALU.mult)
            V.tensor_scalar(ln_f[:, 3], vecT[:, A_L1B:A_L1B + KT], ALPHA, None, ALU.mult).then_inc(n_k, 1)
            dve.wait_ge(n_k, 1)
            V.tensor_tensor(ln_f[:, 1], ln_f[:, 1], modT[:, 3 * KT:4 * KT, 0], ALU.add).then_inc(n_k, 1)

            def norm_rows(n, rows, src, sem_, sq, inc0):
                st = ln_st[0:rows, n % 2]
                for c in range(2):
                    last = V.bn_stats(st[:, 6 * c:6 * c + 6], src[:, 512 * c:512 * c + 512])
                last.then_inc(sem_, 1)
                dve.wait_ge(sem_, inc0 + 1)
                V.bn_aggr(st[:, 12:14], st[:, 0:12]).then_inc(sem_, 1)
                dve.wait_ge(sem_, inc0 + 2)
                V.tensor_scalar(st[:, 14:15], st[:, 13:14], EPS, None, ALU.add).then_inc(sem_, 1)
                dve.wait_ge(sq, n + 1)
                V.reciprocal(st[:, 15:16], st[:, 14:15]).then_inc(sem_, 1)
                dve.wait_ge(sem_, inc0 + 4)

            def halves(h):
                for f in range(KT):
                    n = h * KT + f
                    dve.wait_ge(n_h, n + 1)
                    V.tensor_copy(acts_hi[:, f, h * 512:h * 512 + 512], h2_full[:, n % 2]).then_inc(n_hi, 1)
                    dve.wait_ge(n_hi, n + 1)
                    V.tensor_tensor(acts_lo[:, f, h * 512:h * 512 + 512], h2_full[:, n % 2],
                                    acts_hi[:, f, h * 512:h * 512 + 512].bitcast(F32), ALU.subtract).then_inc(n_lo, 1)

            for tt in range(TT + 1):
                if tt < TT:
                    dve.wait_ge(n_x[tt % 2], 16 * (tt // 2 + 1))
                    x, rows = x_tile[:, tt % 2], P
                else:
                    dve.wait_ge(y_b, 16)
                    x, rows = xs_hat[:, 0], NB
                dve.wait_ge(n_t, tt + 1)
                src = psT[0:rows].rearrange("p a n -> p (a n)")
                V.scalar_tensor_tensor(out=x, in0=x, scalar=ALPHA, in1=src, op0=ALU.mult, op1=ALU.add).then_inc(n_r, 1)
                dve.wait_ge(n_r, 6 * tt + 1)
                norm_rows(tt, rows, x, n_r, n_q, 6 * tt + 1)
                if tt == 4:
                    dve.wait_ge(n_b, KT)
                dst = x_hat[:, tt % 4] if tt < TT else xs_hat[:, 1]
                st = ln_st[0:rows, tt % 2]
                V.tensor_scalar(dst, x, st[:, 12:13], st[:, 15:16], ALU.subtract, ALU.mult).then_inc(n_r, 1)
                if tt == 3:
                    halves(0)
            halves(1)
            dve.wait_ge(n_b, 2 * KT + 1)

            def over_b(ap):
                return ap.rearrange("p (k a) -> p k a", a=1).to_broadcast([P, KT, NB])

            xs = psA[:, 2, 0:KT * NB].rearrange("p (k b) -> p k b", b=NB)
            V.tensor_tensor(hs2[:, 0], xs, over_b(vecT[:, A_L1G:A_L1G + KT]), ALU.mult).then_inc(n_s, 1)
            dve.wait_ge(n_s, 1)
            V.tensor_tensor(hs2[:, 0], hs2[:, 0], over_b(vecT[:, A_L1B:A_L1B + KT]), ALU.add).then_inc(n_s, 1)
            dve.wait_ge(n_s, 2)
            V.tensor_scalar(resT[:, :, SEQ:TOK], hs2[:, 0], ALPHA, None, ALU.mult)
            V.tensor_tensor(hs2[:, 1], hs2[:, 0], modT[:, k1, 1:NC], ALU.mult).then_inc(n_s, 1)
            dve.wait_ge(n_s, 3)
            V.tensor_tensor(hs2[:, 1], hs2[:, 1], modT[:, 3 * KT:4 * KT, 1:NC], ALU.add).then_inc(n_s, 1)
            dve.wait_ge(n_s, 4)
            V.tensor_copy(acts_hi[:, :, SEQ:TOK], hs2[:, 1]).then_inc(n_s, 1)
            dve.wait_ge(n_s, 5)
            V.tensor_tensor(acts_lo[:, :, SEQ:TOK], hs2[:, 1], acts_hi[:, :, SEQ:TOK].bitcast(F32), ALU.subtract).then_inc(n_s, 1)
            dve.wait_ge(n_s, 6)

            sfc = vecT[:, A_SFC:A_SFC + NVD].rearrange("p (b k f) -> p b k f", k=2, f=FT)
            def wc(n, F):
                return vecT[:, ds(A_WFC + n * FT + F, 1)]

            def conv(k, F):
                dve.wait_ge(g_ev[0], KT // 2 * (k + 1) + F + 2)
                V.tensor_scalar(u_c[:], u_a[:], wc(2, F), vecT[:, ds(A_BFC + F, 1)], ALU.mult, ALU.add).then_inc(u_d, 1)
                dve.wait_ge(u_d, 3 * F + 1)
                for n in (1, 0):
                    d = 2 - n
                    V.scalar_tensor_tensor(out=u_c[:, d:SEQ], in0=u_a[:, 0:SEQ - d], scalar=wc(n, F), in1=u_c[:, d:SEQ], op0=ALU.mult, op1=ALU.add)
                    V.scalar_tensor_tensor(out=u_c[:, SEQ:TOK], in0=sfc[:, :, n, ds(F, 1)].rearrange("p b a -> p (b a)"), scalar=wc(n, F),
                                           in1=u_c[:, SEQ:TOK], op0=ALU.mult, op1=ALU.add).then_inc(u_d, 1)
                    if n == 1:
                        dve.wait_ge(u_d, 3 * F + 2)

            def gated(k, f, F):
                dve.wait_ge(u_g_, F + 1)
                dve.wait_ge(g_pm, G_UP0[k] + 2 * f + 4)
                V.tensor_tensor(u_g[:].rearrange("p (c n) -> p c n", c=NCH), u_g[:].rearrange("p (c n) -> p c n", c=NCH),
                                psB[:, :, 0:CH], ALU.mult).then_inc(g_ev[1], 1)
                dve.wait_ge(g_ev[1], KT // 2 * (k + 1) + F + 2)
                V.tensor_copy(g_hi[:, ds(f, 1)], u_g[:].rearrange("p (a n) -> p a n", a=1)).then_inc(u_h, 1)
                dve.wait_ge(u_h, F + 1)
                V.tensor_tensor(g_lo[:, ds(f, 1)], u_g[:].rearrange("p (a n) -> p a n", a=1), g_hi[:, ds(f, 1)].bitcast(F32), ALU.subtract).then_inc(u_l, 1)

            def up(k, f):
                F = NF[k] + f
                round_ = KT // 2 * (k + 1) + F + 1
                g_split(G_UP0[k] + 2 * f + 1, 1, round_)
                if not (isinstance(f, int) and f == 0):
                    gated(k, f - 1, F - 1)
                g_split(G_UP0[k] + 2 * f + 2, 0, round_ + 1)
                conv(k, F)

            def down(k, t, last):
                for j in range(2):
                    m = 2 * t + j
                    M = G_DN0[k] + m
                    round_ = KT // 2 * (k + 1) + NF[k + 1] + t + 1
                    if not (last and j == 1 and k == len(GROUPS) - 1):
                        g_split(M + 1, 1 - j, round_ + j)
                    gate = modT[:, ds(5 * KT + m, 1), 0:1].rearrange("p a n -> p (a n)")
                    dve.wait_ge(g_pm, M + 3)
                    acc = resT[:, ds(m, 1)].rearrange("p a n -> p (a n)")
                    V.scalar_tensor_tensor(out=acc[:, 0:2 * CH].rearrange("p (c n) -> p c n", c=2), in0=proj_ps[j][:, 0:2, 0:CH], scalar=gate,
                                           in1=acc[:, 0:2 * CH].rearrange("p (c n) -> p c n", c=2), op0=ALU.mult, op1=ALU.add)
                    V.scalar_tensor_tensor(out=acc[:, 2 * CH:SEQ], in0=proj_ps[j][:, 2, 0:SEQ - 2 * CH], scalar=gate,
                                           in1=acc[:, 2 * CH:SEQ], op0=ALU.mult, op1=ALU.add)
                    V.tensor_tensor(g_tmp[:], proj_ps[j][:, 2, CH - NB:CH], modT[:, ds(5 * KT + m, 1), 1:NC].rearrange("p a n -> p (a n)"),
                                    ALU.mult).then_inc(g_ev[j], 1)
                    dve.wait_ge(g_ev[j], round_ + 1)
                    V.tensor_tensor(acc[:, SEQ:TOK], acc[:, SEQ:TOK], g_tmp[:], ALU.add).then_inc(u_s, 1)
                    dve.wait_ge(u_s, KT * k + m + 1)

            for k, gs in enumerate(GROUPS):
                up(k, 0)
                with dve.Fori(1, gs) as f:
                    up(k, f)
                gated(k, gs - 1, NF[k + 1] - 1)
                with dve.Fori(0, KT // 2 - 1) as t:
                    down(k, t, False)
                down(k, KT // 2 - 1, True)

            for tt in range(TT + 1):
                rows = P if tt < TT else NB
                dve.wait_ge(y_t, tt + 1)
                norm_rows(tt, rows, y_bank(tt)[0:rows].rearrange("p a n -> p (a n)"), y_d, y_q, 4 * tt)
                if tt >= 3:
                    dve.wait_ge(y_s[tt % 3], 16 * (tt // 3))
                st = ln_st[0:rows, tt % 2]
                V.tensor_scalar(y_tile[0:rows, tt % 3], y_bank(tt)[0:rows].rearrange("p a n -> p (a n)"), st[:, 12:13], st[:, 15:16],
                                ALU.subtract, ALU.mult).then_inc(y_n, 1)
                dve.wait_ge(y_n, tt + 1)
                if tt == 0:
                    dve.wait_ge(y_b, 48)
                V.tensor_tensor(y_tile[0:rows, tt % 3], y_tile[0:rows, tt % 3], ln2g[0:rows], ALU.mult).then_inc(y_g, 1)
                dve.wait_ge(y_g, tt + 1)
                V.tensor_tensor(y_tile[0:rows, tt % 3], y_tile[0:rows, tt % 3], ln2b[0:rows], ALU.add).then_inc(y_o, 1)
            for c in range(2):
                dve.wait_ge(y_f, c + c + 1)
                nf = FT // 2
                bank = (psA, psB)[c]
                V.tensor_copy(ffn_rows[:, c * nf:(c + 1) * nf], bank[0:2 + NB].rearrange("p a n -> p (a n)")[:, 0:nf * P].rearrange("p (f n) -> p f n", n=P)).then_inc(y_f, 1)

        @block.scalar
        def _(act):
            act.wait_ge(s_csil, 1)
            nc.scalar.activation(c_rows, c_half, ACT.Tanh).then_inc(s_ctanh, 1)
            act.wait_ge(s_one, 1)
            for h in range(2):
                for f in range(KT):
                    n = h * KT + f
                    act.wait_ge(s_xt, n + 1)
                    if n >= 2:
                        act.wait_ge(s_hlo, n - 1)
                    nc.scalar.activation(h_full[:, n % 2], proj_ps[n % 2][:, n // 2 % 2], ACT.Identity,
                                         bias=modT[:, f, 0:1], scale=modT[:, KT + f, 0:1]).then_inc(s_hf, 1)

            def evict(n, half, dst, rows=P, samples=False):
                act.wait_ge(s_pm, n + 3)
                if samples:
                    nc.scalar.activation(smpT[:, ds(n, 1), :].rearrange("p a b -> p (a b)"), proj_ps[half][:, NCH - 1, CH - NB:CH], ACT.Copy)
                nc.scalar.activation(dst.rearrange("p (c n) -> p c n", c=NCH), proj_ps[half][0:rows, :, 0:CH], ACT.Copy).then_inc(s_pe, 1)

            with act.Fori(0, WT) as t:
                for j in range(2):
                    n = 2 * t + j
                    act.wait_ge(s_st[j], 16 * t)
                    evict(n, j, tile_out[:, j], samples=True)
                    act.wait_ge(s_pe, n + 3)
                    act.dma_start(qk_scr[0, ds(j * W + P * t, P)], tile_out[:, j, 0:SEQ]).then_inc(s_st[j], 16)
            act.wait_ge(s_tt, 1)
            nc.scalar.activation(smp_out[:, 0:2 * WT].rearrange("p (a j) n -> p a (j n)", a=2), psT[0:NB, :, 0:W], ACT.Copy).then_inc(s_te, 1)
            act.wait_ge(s_te, 1)
            act.dma_start(sq_scr.rearrange("b (k w) -> b k w", k=2), smp_out[:, 0:2 * WT].rearrange("p (k j) n -> p k (j n)", k=2)).then_inc(s_sq, 16)
            act.wait_ge(s_sq, 16)
            toks = [o[k][0].rearrange("a (t p) h d -> p (a t) (h d)", p=P) for k in ("p_fox_k", "p_sb_k", "p_fox_v", "p_sb_v")]
            smps = [o[k][0].rearrange("b t h d -> (b t) (h d)") for k in ("s_fox_k", "s_sb_k", "s_fox_v", "s_sb_v")]

            def tok_evict(t, j):
                m = 4 * t + j
                act.wait_ge(s_tt, m + 2)
                act.wait_ge(s_so[j % 2], 16 * (2 * t + j // 2))
                nc.scalar.activation(tok_out[:, j % 2].rearrange("p (a t) n -> p a (t n)", a=2), psT[:], ACT.Copy).then_inc(s_te, 1)
                act.wait_ge(s_te, m + 2)
                act.dma_start(toks[j][:, :, ds(P * t, P)], tok_out[:, j % 2]).then_inc(s_so[j % 2], 16)

            with act.Fori(0, WT) as t:
                for j in range(4):
                    n = 2 * WT + 4 * t + j
                    act.wait_ge(s_st[j % 2], 16 * (WT + t + (1 if j >= 2 else 0)))
                    evict(n, j % 2, tile_out[:, j % 2], samples=True)
                    if j < 2:
                        act.wait_ge(s_pe, n + 3)
                        act.dma_start(qk_scr[1, ds(j * W + P * t, P)], tile_out[:, j % 2, 0:SEQ]).then_inc(s_st[j % 2], 16)
                    if j >= 1:
                        tok_evict(t, j - 1)
                tok_evict(t, 3)
            act.wait_ge(s_tt, 4 * WT + 2)
            nc.scalar.activation(smp_out[:].rearrange("p (t j) n -> p t (j n)", j=4), psB[0:NB], ACT.Copy).then_inc(s_te, 1)
            act.wait_ge(s_te, 4 * WT + 2)
            for j in range(4):
                act.dma_start(smps[j].rearrange("b (t n) -> b t n", n=P), smp_out[:].rearrange("p (t j) n -> p j t n", j=4)[:, j]).then_inc(s_sq, 16)
            with act.Fori(0, LT) as t:
                for j, dst in enumerate((xrT, xgT)):
                    evict(6 * WT + 2 * t + j, j, dst[:, ds(t, 1), :].rearrange("p a n -> p (a n)"))
            evict(6 * WT + 2 * LT, 0, fgT, H)
            act.wait_ge(s_sq, 16 * 5)
            act.preload_act_table_set(LN_EXP)
            act.wait_ge(s_fc, 2)
            nc.scalar.activation(fg_e[:], fg_e[:], ACT.Exp).then_inc(s_fa, 1)
            act.wait_ge(s_fa, 1)
            nc.scalar.activation(fg_e[:], fg_e[:], ACT.Ln, bias=1.0).then_inc(s_fa, 1)

            def low_half(n, par, bank):
                act.wait_ge(o_x, n)
                nc.scalar.activation(o_low[par * HD:par * HD + HD], bank[HD:P], ACT.Copy).then_inc(o_c, 1)

            with act.Fori(0, WT) as t:
                for s in range(F_STEPS + 5):
                    if s < F_STEPS:
                        act.wait_ge(f_m, F_STEPS * t + s + 1)
                        act.wait_ge(f_t, F_N * t + (f_cum(s - 3) if s >= 3 else 0))
                        nk = (s % TT + 1) * P
                        ps = proj_ps[s % 2][:, 0:2].rearrange("p a n -> p (a n)")[:, 0:nk]
                        nc.scalar.activation(probs[:, s % 3, 0:nk], ps, ACT.Exp, bias=row_max[:, s:s + 1],
                                             accum_out=row_sum[:, s:s + 1]).then_inc(f_e, 1)
                    if 2 <= s < F_STEPS + 2:
                        x = s - 2
                        act.wait_ge(f_o, F_STEPS * t + max(0, x - 1))
                        for u, (y, b) in enumerate(F_USES):
                            if y == x:
                                nb = min(4, x % TT + 1 - 4 * b)
                                act.wait_ge(f_t, F_N * t + u + 1)
                                nc.scalar.activation(pt_hi[:, x % 2, 4 * b:4 * b + nb], psT[:, b, 0:nb * P].rearrange("p (k n) -> p k n", n=P),
                                                     ACT.Copy).then_inc(f_h, 1)
                    if s >= 7 and (s - 4) % 4 == 3:
                        g = (s - 4) // 4
                        act.wait_ge(f_o, F_STEPS * t + 4 * g + 4)
                        low_half(4 * t + g, g // 2, proj_ps[g % 2][:, 2])
            with act.Fori(0, WT) as t:
                for k in range(B_N + 5):
                    if k < B_N:
                        par, c, kb, q0 = B_STEPS[k]
                        act.wait_ge(b_z, B_N * t + k + 1)
                        act.wait_ge(b_t, B_N * t + max(0, k - 3))
                        nc.scalar.activation(z_s[:, k % 4, q0:512], z_bank(k)[:, q0:512], ACT.Copy).then_inc(b_c, 1)
                    if 1 <= k < B_N + 1:
                        x = k - 1
                        par, c, kb, q0 = B_STEPS[x]
                        act.wait_ge(b_m, B_N * t + x + 1)
                        nc.scalar.activation(z_e[:, x % 3, q0:512], z_e[:, x % 3, q0:512], ACT.Exp).then_inc(b_e, 1)
                        act.wait_ge(b_e, B_N * t + x + 1)
                        nc.scalar.activation(z_e[:, x % 3, q0:512], z_e[:, x % 3, q0:512], ACT.Ln, bias=1.0).then_inc(b_l, 1)
                    if 3 <= k < B_N + 3:
                        x = k - 3
                        par, c, kb, q0 = B_STEPS[x]
                        act.wait_ge(b_t, B_N * t + x + 1)
                        nc.scalar.activation(z_w[:, x % 4, q0:512], z_w[:, x % 4, q0:512], ACT.Exp).then_inc(b_w, 1)
                    for g in range(4):
                        if k == min(B_LAST[g] + 5, B_N + 4):
                            act.wait_ge(b_o, B_N * t + B_LAST[g] + 1)
                            low_half(4 * WT + 4 * t + g, g % 2, proj_ps[g % 2][:, 1])

            A = nc.scalar
            act.wait_ge(r_d, R_CONV + 2)
            A.activation(r_c[:, 3], r_c[:, 3], ACT.Exp).then_inc(r_s, 1)
            act.wait_ge(r_s, 1)
            A.activation(r_c[:, 3], r_c[:, 3], ACT.Ln, bias=1.0).then_inc(r_s, 1)
            act.wait_ge(r_d, R_CONV)
            for g in range(2):
                for t in range(LT):
                    act.wait_ge(r_p, 2 * g + t + 1)
                    A.activation((r_t, r_i)[g][:, t].rearrange("p (c n) -> p c n", c=NCH), proj_ps[t][:, :, 0:CH], ACT.Tanh,
                                 bias=r_c[:, g, t:t + 1], scale=0.5).then_inc(r_s, 1)
            act.wait_ge(r_d, R_LOGA)
            A.activation(r_a[:], r_t[:], ACT.Exp).then_inc(r_s, 1)
            A.activation(r_h[:], r_t[:], ACT.Tanh).then_inc(r_s, 1)
            act.wait_ge(r_d, R_ONE)
            A.activation(r_h[:], r_h[:], ACT.Sqrt).then_inc(r_s, 1)
            A.activation(xgT[:], xgT[:], ACT.Gelu_apprx_tanh).then_inc(r_s, 1)
            act.wait_ge(d_d, D_MAX)
            act.preload_act_table_set(LN_EXP)
            A.activation(d_f[:], d_f[:], ACT.Exp, bias=d_small[:, 0:1], accum_out=d_small[:, 1:2]).then_inc(d_a, 1)
            act.wait_ge(d_d, D_MIN)
            A.activation(d_e[:], d_e[:], ACT.Exp).then_inc(d_a, 1)
            act.wait_ge(d_a, 2)
            A.activation(d_e[:], d_e[:], ACT.Ln, bias=1.0).then_inc(d_a, 1)
            act.wait_ge(d_d, D_SB)
            A.activation(d_z[:], d_z[:], ACT.Exp).then_inc(d_a, 1)
            act.wait_ge(s_lr, 64)
            act.wait_ge(d_d, D_LAST)
            act.wait_ge(d_v, 2 * NB + 2)
            with act.Fori(0, KT // 2) as t:
                for j in range(2):
                    m = 2 * t + j
                    act.wait_ge(g_pm, m + 3)
                    A.activation(resT[:, ds(m, 1)].rearrange("p a (c n) -> p (a c) n", c=NCH), proj_ps[j][:, :, 0:CH], ACT.Identity,
                                 scale=modT[:, ds(2 * KT + m, 1), 0:1].rearrange("p a n -> p (a n)")).then_inc(m_ev, 1)

            def roots(n, rows, d, q, count):
                act.wait_ge(d, count)
                A.activation(ln_st[0:rows, n % 2, 14:15], ln_st[0:rows, n % 2, 14:15], ACT.Sqrt).then_inc(q, 1)

            act.wait_ge(n_k, 2)
            for tt in range(TT + 1):
                roots(tt, P if tt < TT else NB, n_r, n_q, 6 * tt + 4)
                if tt in (3, TT):
                    h = 0 if tt == 3 else 1
                    for f in range(KT):
                        n = h * KT + f
                        act.wait_ge(n_b, n + 1)
                        bank = proj_ps[n % 2][:, n // 2 % 2]
                        A.activation(resT[:, f, h * 512:h * 512 + 512], bank, ACT.Identity, bias=ln_f[:, 3, f:f + 1], scale=ln_f[:, 2, f:f + 1])
                        if n >= 2:
                            act.wait_ge(n_lo, n - 1)
                        A.activation(h2_full[:, n % 2], bank, ACT.Identity, bias=ln_f[:, 1, f:f + 1], scale=ln_f[:, 0, f:f + 1]).then_inc(n_h, 1)
            act.wait_ge(n_s, 6)
            for k, gs in enumerate(GROUPS):
                with act.Fori(0, gs) as f:
                    F = NF[k] + f
                    act.wait_ge(g_pm, G_UP0[k] + 2 * f + 3)
                    act.wait_ge(u_d, 3 * F)
                    A.activation(ffn_cols[:, ds(F, 1)].rearrange("p a n -> p (a n)"), psA[:, 2, CH - NB - 2:CH], ACT.Copy)
                    A.activation(u_a[:].rearrange("p (c n) -> p c n", c=NCH), psA[:, :, 0:CH], ACT.Copy).then_inc(g_ev[0], 1)
                    act.wait_ge(u_d, 3 * F + 3)
                    act.wait_ge(u_l, F)
                    A.activation(u_g[:], u_c[:], ACT.Gelu_apprx_tanh).then_inc(u_g_, 1)
            for tt in range(TT + 1):
                roots(tt, P if tt < TT else NB, y_d, y_q, 4 * tt + 3)

        @block.tensor
        def _(pe):
            pe.sem_inc(s_pm, 2)
            pe.wait_ge(s_ident, 1)
            pe.wait_ge(s_csil, 2)
            for k in range(KT):
                last = nc.tensor.transpose(psT[:, 0, k * NC:(k + 1) * NC], c_rows[:, k * P:(k + 1) * P], ident[0:NC, 0:NC])
            last.then_inc(s_vt, 1)
            pe.wait_ge(s_small, 16 * NSMALL)
            pe.wait_ge(s_vte, 1)
            at = 0
            for n, r in enumerate((NVA, NVB, NVC)):
                nc.tensor.transpose(psT[:, 1, at:at + r], vec_rows[0:r, n], ident[0:r, 0:r])
                at += r
            for n in range(3):
                r = min(P, NVD - n * P)
                last = nc.tensor.transpose(psT[:, 0, n * P:n * P + r], vec_rows[0:r, 3 + n], ident[0:r, 0:r])
            last.then_inc(s_vt, 1)

            def ada(w, dst):
                for m in range(4):
                    for k in range(KT):
                        last = nc.tensor.matmul(dst[:, m * NC:(m + 1) * NC], w[:, k, m * P:(m + 1) * P], cT[:, k],
                                                start=k == 0, stop=k == KT - 1)
                last.then_inc(s_amm, 1)

            for n in range(ADA1):
                pe.wait_ge(s_al[n % 2], 16 * (n // 2 + 1))
                if n >= 2:
                    pe.wait_ge(s_aev, n - 1)
                ada(w_ada1[:, n % 2], psA[:, n % 2, 0:4 * NC])
            for k in range(KT):
                last = nc.tensor.transpose(psB[:, 2, k * NB:(k + 1) * NB], xs_rows[:, k * P:(k + 1) * P], ident[0:NB, 0:NB])
            last.then_inc(s_vt, 1)
            pe.wait_ge(s_aev, ADA1)
            for h in range(2):
                pe.wait_ge(s_x[h], 16)
                for f in range(KT):
                    n = h * KT + f
                    if n >= 4:
                        pe.wait_ge(s_hf, n - 3)
                    for q in range(TT // 2):
                        last = nc.tensor.transpose(proj_ps[n % 2][:, n // 2 % 2, q * P:(q + 1) * P],
                                                   x_rows[:, h * TT // 2 + q, f * P:(f + 1) * P], ident[:])
                    last.then_inc(s_xt, 1)
            for n in range(ADA1, ADA1 + ADA_IN):
                pe.wait_ge(s_al[n % 2], 16 * (n // 2 + 1))
                ada(w_ada1[:, n % 2], psT[:, n % 2, 0:4 * NC])
            pe.wait_ge(s_hf, 2 * KT)
            pe.wait_ge(s_hlo, 2 * KT)
            pe.wait_ge(s_hs, 4)

            def project(n, half, cols=P):
                pe.wait_ge(s_wlo, n + 3)
                pe.wait_ge(s_pe, n + 1)
                for k in range(KT):
                    for w, a in ((w_hi, acts_hi), (w_hi, acts_lo), (w_lo, acts_hi)):
                        for c in range(NCH):
                            last = nc.tensor.matmul(proj_ps[half][0:cols, c, 0:CH], w[:, half, k, 0:cols], a[:, k, c * CH:(c + 1) * CH],
                                                    start=k == 0 and w is w_hi and a is acts_hi, stop=k == KT - 1 and w is w_lo)
                last.then_inc(s_pm, 1)

            pe.sem_inc(s_pe, 2)
            with pe.Fori(0, WT) as t:
                for j in range(2):
                    project(2 * t + j, j)
                    c = ADA1 + ADA_IN + 2 * t + j
                    pe.wait_ge(s_al[j], 16 * ((ADA1 + ADA_IN) // 2 + t + 1))
                    pe.wait_ge(s_aev, c - 1)
                    ada(w_ada1[:, j], psT[:, j, 0:4 * NC])
            pe.wait_ge(s_aev, ADA1 + ADA2)
            pe.wait_ge(s_pe, 2 * WT + 2)
            for j in range(2):
                for t in range(WT):
                    last = nc.tensor.transpose(psT[0:NB, j, t * P:(t + 1) * P], smpT[:, 2 * t + j], ident[:])
            last.then_inc(s_tt, 1)

            def to_tokens(t, j):
                pe.wait_ge(s_pe, 2 * WT + 4 * t + j + 3)
                pe.wait_ge(s_te, 4 * t + j + 1)
                for q in range(TT):
                    last = nc.tensor.transpose(psT[:, q // 4, q % 4 * P:q % 4 * P + P], tile_out[:, j % 2, q * P:(q + 1) * P], ident[:])
                last.then_inc(s_tt, 1)

            with pe.Fori(0, WT) as t:
                for j in range(4):
                    project(2 * WT + 4 * t + j, j % 2)
                    if j >= 1:
                        to_tokens(t, j - 1)
                to_tokens(t, 3)
            pe.wait_ge(s_pe, 6 * WT + 2)
            for t in range(WT):
                for j in range(4):
                    last = nc.tensor.transpose(psB[0:NB, t, j * P:(j + 1) * P], smpT[:, 2 * WT + 4 * t + j], ident[:])
            last.then_inc(s_tt, 1)
            pe.wait_ge(s_te, 4 * WT + 2)
            with pe.Fori(0, LT) as t:
                for j in range(2):
                    project(6 * WT + 2 * t + j, j)
            project(6 * WT + 2 * LT, 0, H)
            pe.wait_ge(s_fc, 4)
            for q in range(TT):
                nc.tensor.transpose(psT[:, 0, q * H:(q + 1) * H], lgT[:, q * P:(q + 1) * P], ident[0:H, 0:H])
            nc.tensor.transpose(psT[0:NB, 0, TT * H:TT * H + H], lgT[:, SEQ:TOK], ident[0:H, 0:H]).then_inc(s_fp, 1)
            pe.wait_ge(s_cr, 1)
            pe.wait_ge(s_fp, 2)

            with pe.Fori(0, WT) as t:
                for s in range(F_STEPS + 3):
                    if s < F_STEPS:
                        par, qb = s // TT, s % TT
                        if qb == 0:
                            pe.wait_ge(s_b, 2 * t + par + 3)
                        pe.wait_ge(f_e, F_STEPS * t + max(0, s - 1))
                        rows = slice(qb * P, qb * P + P)
                        for c in range(qb // 4 + 1):
                            ks = slice(c * 512, min(c * 512 + 512, qb * P + P))
                            bank = proj_ps[s % 2][:, c, 0:ks.stop - ks.start]
                            diag = c == qb // 4
                            nc.tensor.matmul(bank, q_hi[:, par, rows], k_st[:, par, ks], start=True, stop=False)
                            nc.tensor.matmul(bank, q_lo[:, par, rows], k_st[:, par, ks], start=False, stop=False)
                            last = nc.tensor.matmul(bank, fq_rows[:, par, rows], fk_rows[:, par, ks], start=False, stop=not diag)
                            if diag:
                                last = nc.tensor.matmul(bank[:, qb % 4 * P:qb % 4 * P + P], ident_r[:], mask_r[:, 0], start=False, stop=True)
                        last.then_inc(f_s, 1)
                    if 2 <= s < F_STEPS + 2:
                        x = s - 2
                        pe.wait_ge(f_n, F_STEPS * t + x + 1)
                        for u, (y, b) in enumerate(F_USES):
                            if y == x:
                                before = [v for v in range(u) if F_USES[v][1] == b]
                                pe.wait_ge(f_l, F_N * t + (before[-1] + 1 if before else 0))
                                for kb in range(4 * b, min(4 * b + 4, x % TT + 1)):
                                    last = nc.tensor.transpose(psT[:, b, kb % 4 * P:kb % 4 * P + P], probs[:, x % 3, kb * P:kb * P + P], ident[:])
                                last.then_inc(f_t, 1)
                    if s >= 3:
                        x = s - 3
                        par, qb = x // TT, x % TT
                        pe.wait_ge(f_l, F_N * t + f_cum(x))
                        if qb % 4 == 0:
                            pe.wait_ge(o_x, 4 * t + max(0, x // 4 - 1))
                        for kb in range(qb + 1):
                            for part in (pt_hi, pt_lo):
                                last = nc.tensor.matmul(proj_ps[x // 4 % 2][:, 2, qb % 4 * P:qb % 4 * P + P], v_st[:, par, kb], part[:, x % 2, kb],
                                                        start=kb == 0 and part is pt_hi, stop=kb == qb and part is pt_lo)
                        last.then_inc(f_o, 1)

            with pe.Fori(0, WT) as t:
                pe.wait_ge(s_b, H + 2 * t + 4)
                for k in range(-1, B_N + 5):
                    if k + 1 < B_N:
                        x = k + 1
                        par, c, kb, q0 = B_STEPS[x]
                        pe.wait_ge(b_c, B_N * t + max(0, x - 2))
                        qs = slice(512 * c + q0, 512 * c + 512)
                        bank = z_bank(x)[:, q0:512]
                        diag = kb >= 4 * c
                        nc.tensor.matmul(bank, k_st[:, par, kb * P:kb * P + P], q_hi[:, par, qs], start=True, stop=False)
                        last = nc.tensor.matmul(bank, k_st[:, par, kb * P:kb * P + P], q_lo[:, par, qs], start=False, stop=not diag)
                        if diag:
                            last = nc.tensor.matmul(bank[:, 0:P], ident_r[:], mask_r[:, 1], start=False, stop=True)
                        last.then_inc(b_z, 1)
                    if 3 <= k < B_N + 3:
                        x = k - 3
                        par, c, kb, q0 = B_STEPS[x]
                        pe.wait_ge(b_t, B_N * t + x + 1)
                        if kb > 0:
                            nc.tensor.matmul(proj_ps[par][:, 2, q0:512], tri[:, 1], z_sp[:, x % 4, q0:512], start=False, stop=True,
                                             skip_group_check=True)
                    if 1 <= k < B_N + 1:
                        x = k - 1
                        par, c, kb, q0 = B_STEPS[x]
                        pe.wait_ge(b_s, B_N * t + x + 1)
                        nc.tensor.matmul(proj_ps[par][:, 2, q0:512], tri[:, 0], z_sp[:, x % 4, q0:512], start=kb == 4 * c + 3, stop=True,
                                         skip_group_check=True).then_inc(b_k, 1)
                    if k >= 5:
                        x = k - 5
                        par, c, kb, q0 = B_STEPS[x]
                        pe.wait_ge(b_lo, B_N * t + x + 1)
                        if kb == 4 * c + 3:
                            pe.wait_ge(o_x, 4 * WT + 4 * t + (0 if c == 0 else par + 1))
                        nc.tensor.matmul(proj_ps[par][:, 1, q0:512], v_st[:, par, kb], w_hi2[:, x % 2, q0:512], start=kb == 4 * c + 3, stop=False,
                                         skip_group_check=True)
                        nc.tensor.matmul(proj_ps[par][:, 1, q0:512], v_st[:, par, kb], w_lo2[:, x % 2, q0:512], start=False, stop=kb == 0,
                                         skip_group_check=True).then_inc(b_o, 1)

            pe.wait_ge(r_d, R_CONV)
            pe.wait_ge(s_gw, 16 * 8)
            pe.wait_ge(o_x, 4 * 2 * WT)
            for g in range(2):
                for t in range(LT):
                    if g == 1:
                        pe.wait_ge(r_s, 3 + t)
                    for c in range(NCH):
                        last = nc.tensor.matmul(proj_ps[t][:, c, 0:CH], gate_w[:, g, t], r_xc[:, t, c * CH:(c + 1) * CH], start=True, stop=True)
                    last.then_inc(r_p, 1)
            pe.wait_ge(r_d, R_COLS)
            for t in range(LT):
                last = nc.tensor.transpose(psA[0:4 + 2 * NB, 0, t * P:(t + 1) * P], lru_cols[:, t], ident[:])
            last.then_inc(r_p, 1)
            pe.wait_ge(r_d, R_ROWS)
            pe.wait_ge(r_s, 6)
            pe.wait_ge(s_kfree, NPG + 2 * NB * NPG)
            pe.wait_ge(s_lf, 16 * NB * NPG)
            for p in range(NPG):
                dst = slice(p % 4 * P, p % 4 * P + P)
                nc.tensor.transpose(psA[0:R48, p // 4, dst], scores[:, 0, p].rearrange("p b h -> p (b h)"), ident[:])
                nc.tensor.transpose(psB[0:R48, p // 4, dst], scores[:, 1, p].rearrange("p b h -> p (b h)"), ident[:])
                last = nc.tensor.transpose(psT[0:R48, p // 4, dst], lf_pages[:, p].rearrange("p b h -> p (b h)"), ident[:])
            last.then_inc(d_t, 1)
            pe.wait_ge(d_d, D_SELF)
            for t in range(WT):
                nc.tensor.matmul(psA[0:R48, 2, 0:1], d_zq[:, t].rearrange("p b h -> p (b h)"), ones[:], start=t == 0, stop=t == WT - 1)
            nc.tensor.matmul(psA[0:R48, 2, 1:2], d_spread[:].rearrange("p b h -> p (b h)"), ones[0:H], start=True, stop=True).then_inc(d_t, 1)
            pe.wait_ge(d_d, D_FOX)
            for p in range(NPG):
                nc.tensor.transpose(psT[:, 0, p * R48:(p + 1) * R48], d_f[:, p * P:(p + 1) * P], ident[0:R48, 0:R48])
            nc.tensor.matmul(psA[0:NB, 2, 0:R48], d_grp[:], d_diag[:], start=True, stop=True).then_inc(d_t, 1)
            pe.wait_ge(d_a, 4)
            for p in range(NPG):
                last = nc.tensor.transpose(psT[:, 1, p * R48:(p + 1) * R48], d_z[:, p * P:(p + 1) * P], ident[0:R48, 0:R48])
            last.then_inc(d_t, 1)
            pe.wait_ge(d_d, D_P)
            pe.sem_inc(d_v, 2)
            with pe.Fori(0, NB) as b:
                for kind in range(2):
                    pe.wait_ge(s_vl[kind], 16 * NPG * (b + 1))
                    for v in range(WT):
                        dst = psA[:, 0, ds(((kind * WT + v) * NB + b) * 2, 2)]
                        for p in range(NPG):
                            last = nc.tensor.matmul(dst, v_page[:, kind, p, v * P:(v + 1) * P], d_p[:, kind, p, ds(b * H + 2 * v, 2)],
                                                    start=p == 0, stop=kind == 1 and p == NPG - 1)
                        if kind == 0:
                            last = nc.tensor.matmul(dst, smp_out[:, 4 * v + 2], d_self[:, ds(b * H + 2 * v, 2)], start=False, stop=True)
                    last.then_inc(d_v, 1)
            pe.wait_ge(d_d, D_LAST)
            pe.wait_ge(o_l, 4 * 2 * WT)

            def g_project(m, half, round_, hi, lo, nk=KT, gated_=None):
                pe.wait_ge(g_ws, m + 3)
                pe.wait_ge(g_ev[half], round_)
                for k in range(nk):
                    if k == nk - 1 and gated_ is not None:
                        pe.wait_ge(u_l, gated_)
                    for w, a in ((w_hi, hi), (w_hi, lo), (w_lo, hi)):
                        for c in range(NCH):
                            last = nc.tensor.matmul(proj_ps[half][:, c, 0:CH], w[:, half, k], a[:, k, c * CH:(c + 1) * CH],
                                                    start=k == 0 and w is w_hi and a is hi, stop=k == nk - 1 and w is w_lo)
                last.then_inc(g_pm, 1)

            pe.sem_inc(g_pm, 2)
            pe.sem_inc(g_ev[0], 1)
            pe.sem_inc(g_ev[1], 1)
            with pe.Fori(0, KT // 2) as t:
                for j in range(2):
                    g_project(2 * t + j, j, t + 1, acts_hi, acts_lo)
            for j in range(2):
                pe.wait_ge(g_ev[j], KT // 2 + 1)

            def to_rows(tt, dst, src):
                cols = slice(tt * P, tt * P + P) if tt < TT else slice(SEQ, TOK)
                for f in range(KT):
                    last = nc.tensor.transpose(dst[0:cols.stop - cols.start, f // 4, f % 4 * P:f % 4 * P + P], src[:, f, cols], ident[:])
                return last

            for tt in range(TT + 1):
                if tt >= 1:
                    pe.wait_ge(n_r, 6 * (tt - 1) + 1)
                to_rows(tt, psT, resT).then_inc(n_t, 1)
                if tt in (3, TT):
                    h = 0 if tt == 3 else 1
                    pe.wait_ge(n_r, 6 * (4 * h + 4))
                    for f in range(KT):
                        n = h * KT + f
                        if n >= 4:
                            pe.wait_ge(n_h, n - 3)
                        for q in range(4):
                            last = nc.tensor.transpose(proj_ps[n % 2][:, n // 2 % 2, q * P:(q + 1) * P], x_hat[:, q, f * P:(f + 1) * P], ident[:])
                        last.then_inc(n_b, 1)
            pe.wait_ge(n_r, 6 * (TT + 1))
            for f in range(KT):
                last = nc.tensor.transpose(psA[:, 2, f * NB:(f + 1) * NB], xs_hat[:, 1, f * P:(f + 1) * P], ident[0:NB, 0:NB])
            last.then_inc(n_b, 1)
            pe.wait_ge(n_h, 2 * KT)
            pe.wait_ge(n_lo, 2 * KT)
            pe.wait_ge(n_s, 6)
            for k, gs in enumerate(GROUPS):
                with pe.Fori(0, gs) as f:
                    for j in range(2):
                        g_project(G_UP0[k] + 2 * f + j, j, KT // 2 * (k + 1) + NF[k] + f + 1, acts_hi, acts_lo)
                pe.wait_ge(u_l, NF[k + 1] - 1)
                for j in range(2):
                    g_project(G_DN0[k] + j, j, KT // 2 * (k + 1) + NF[k + 1] + 1, g_hi, g_lo, gs, NF[k + 1] if j == 0 else None)
                with pe.Fori(1, KT // 2) as t:
                    for j in range(2):
                        g_project(G_DN0[k] + 2 * t + j, j, KT // 2 * (k + 1) + NF[k + 1] + t + 1, g_hi, g_lo, gs)
            pe.wait_ge(u_s, KT * len(GROUPS))
            for tt in range(TT + 1):
                if tt >= 2:
                    pe.wait_ge(y_n, tt - 1)
                to_rows(tt, y_bank(tt), resT).then_inc(y_t, 1)
            for c in range(2):
                nf = FT // 2
                bank = (psA, psB)[c]
                if c == 1:
                    pe.wait_ge(y_n, TT + 1)
                    pe.wait_ge(y_f, 2)
                for f in range(nf):
                    last = nc.tensor.transpose(bank[0:2 + NB, f // 4, f % 4 * P:f % 4 * P + P], ffn_cols[:, c * nf + f], ident[:])
                last.then_inc(y_f, 1)


_INS = ["x_prompt", "x_sample", "cache_fox_k", "cache_fox_v", "cache_fox_logf", "cache_sb_k", "cache_sb_v",
        "state_lru_h", "state_lru_conv", "state_ffn_conv", "page_table", "c_prompt", "c_sample",
        "w_ada", "b_ada", "w_in", "b_fgate", "w_lru_conv", "b_lru_conv", "w_rgate", "b_rgate", "w_igate", "b_igate",
        "lru_lambda", "w_out", "ln1_g", "ln1_b", "w_up", "w_ffn_conv", "b_ffn_conv", "w_down", "ln2_g", "ln2_b"]


def _out_shapes(a):
    d, b, s = a["w_in"].shape[0], a["x_prompt"].shape[0], a["x_prompt"].shape[1]
    nb = a["x_sample"].shape[0]
    h, hd = a["cache_fox_k"].shape[3:]
    dl, ff = a["state_lru_h"].shape[2], a["w_down"].shape[1]
    out = [("y_prompt", a["x_prompt"].shape), ("y_sample", a["x_sample"].shape)]
    for pre, n, t in (("p", b, s), ("s", nb, 1)):
        out += [(pre + "_fox_k", (d, n, t, h, hd)), (pre + "_fox_v", (d, n, t, h, hd)), (pre + "_fox_logf", (d, n, t, h)),
                (pre + "_sb_k", (d, n, t, h, hd)), (pre + "_sb_v", (d, n, t, h, hd)), (pre + "_lru_h", (d, n, dl)),
                (pre + "_lru_conv", (d, n, a["state_lru_conv"].shape[2], dl)), (pre + "_ffn_conv", (d, n, a["state_ffn_conv"].shape[2], ff))]
    return out


def kernel(**inputs):
    import numpy as np
    import concourse.bacc as bacc
    from concourse.bass_utils import run_bass_kernel_spmd

    nc = bacc.Bacc("TRN2", target_bir_lowering=False, num_devices=1)
    arrays = {f"in_{n}": np.ascontiguousarray(inputs[n]) for n in _INS}
    ins = {n: nc.dram_tensor(f"in_{n}", arrays[f"in_{n}"].shape, mybir.dt.from_np(arrays[f"in_{n}"].dtype), kind="ExternalInput").ap()
           for n in _INS}
    shapes = _out_shapes({n: arrays[f"in_{n}"] for n in _INS})
    outs = {n: nc.dram_tensor(f"out_{n}", list(s), F32, kind="ExternalOutput").ap() for n, s in shapes}
    hybrid_step(nc, ins, outs)
    r = run_bass_kernel_spmd(nc, [arrays], core_ids=[0])
    return tuple(r.results[0][f"out_{n}"] for n, _ in shapes)
```

```python
import concourse.bass as bass
from concourse import mybir
from concourse.alu_op_type import AluOpType as ALU
from contextlib import ExitStack

F32 = mybir.dt.float32
F32R = mybir.dt.float32r
I32 = mybir.dt.int32
ACT = mybir.ActivationFunctionType
AX = mybir.AxisListType
ds = bass.ds
P = 128


def hybrid_step(nc, i, o):
    SEQ, D = i["x_prompt"].shape[1:]
    NB = i["x_sample"].shape[0]
    TOK = SEQ + NB
    NCH = 3
    CH = TOK // NCH
    KT = D // P
    TT = SEQ // P
    HD = i["cache_fox_k"].shape[4]
    H = i["cache_fox_k"].shape[3]
    W = H * HD
    WT = W // P
    DL = i["state_lru_h"].shape[2]
    LT = DL // P
    DFF = i["w_down"].shape[1]
    FT = DFF // P
    NPG = i["page_table"].shape[1]
    NPOOL = i["cache_fox_k"].shape[1]
    NC = NB + 1
    FQ, FK, FV, FG = 0, W, 2 * W, 3 * W
    SQ = FG + H
    SK, SV, XR = SQ + W, SQ + 2 * W, SQ + 3 * W
    XG = XR + DL
    assert CH * NCH == TOK and CH % 2 == 0

    w_in = i["w_in"][0].rearrange("(k p) n -> p k n", p=P)
    w_ada = i["w_ada"][0].rearrange("(k p) n -> p k n", p=P)

    with ExitStack() as ctx:
        def sb(name, shape, dt=F32):
            return ctx.enter_context(nc.sbuf_tensor(name, shape, dt))

        def sem(name):
            return ctx.enter_context(nc.semaphore(name))

        def sems(name, n):
            return [sem(f"{name}{k}") for k in range(n)]

        qk_scr = nc.dram_tensor("qk_scr", [2, 2 * W, SEQ], F32).ap()
        f_scr = nc.dram_tensor("f_scr", [4, H, SEQ], F32).ap()
        sq_scr = nc.dram_tensor("sq_scr", [NB, 2 * W], F32).ap()

        psA = ctx.enter_context(nc.psum_tensor("psA", [P, 3, 512], F32))
        psB = ctx.enter_context(nc.psum_tensor("psB", [P, 3, 512], F32))
        psT = ctx.enter_context(nc.psum_tensor("psT", [P, 2, 512], F32))
        proj_ps = (psA, psB)

        ident = sb("ident", [P, P])
        acts_hi = sb("acts_hi", [P, KT, TOK], F32R)
        acts_lo = sb("acts_lo", [P, KT, TOK], F32R)
        modT = sb("modT", [P, 6 * KT, NC])
        NVA = 6 * KT + 4 * LT + 4 * LT + 2 * KT
        NVB = 4 * FT
        NVC = NB * 3 * LT + NB * LT
        NVD = NB * 2 * FT
        vecT = sb("vecT", [P, NVA + NVB + NVC + NVD])
        w_raw = sb("w_raw", [P, 4, KT, P])
        w_hi = sb("w_hi", [P, 2, KT, P], F32R)
        w_lo = sb("w_lo", [P, 2, KT, P], F32R)
        misc = sb("misc", [P, TOK])
        ada_rows = misc[0:2 * NC, 0:1024].rearrange("c (a n) -> c a n", a=2)
        fgT = misc[0:H]
        ones = sb("ones", [P, 1])
        ln_st = sb("ln_st", [P, 2, 16])
        stA = ExitStack()

        def sbA(name, shape, dt=F32):
            return stA.enter_context(nc.sbuf_tensor(name, shape, dt))

        xrT = sbA("xrT", [P, LT, TOK])
        xgT = sbA("xgT", [P, LT, TOK])
        table = sbA("table", [1, NB * NPG], I32)
        scores = sbA("scores", [P, 2, NPG, NB, H])
        lf_pages = sbA("lf_pages", [P, NPG, NB, H])
        smpT = sbA("smpT", [P, 6 * WT, NB])
        smp_out = sbA("smp_out", [NB, 4 * WT, P])
        ident_r = sbA("ident_r", [P, P], F32R)
        mask_f = sbA("mask_f", [P, 2, P])
        mask_r = sbA("mask_r", [P, 2, P], F32R)
        tri = sbA("tri", [P, 2, P])
        bfg = sbA("bfg", [H, 1])
        lgT = sbA("lgT", [H, TOK])

        A_ADA = 0
        A_WLC = 6 * KT
        A_BLC = A_WLC + 4 * LT
        A_BR = A_BLC + LT
        A_BI = A_BR + LT
        A_LAM = A_BI + LT
        A_L1G = A_LAM + LT
        A_L1B = A_L1G + KT
        A_WFC = NVA
        A_BFC = NVA + 3 * FT
        A_SLC = NVA + NVB
        A_SLH = A_SLC + NB * 3 * LT
        A_SFC = NVA + NVB + NVC

        st = ExitStack()

        def sb1(name, shape, dt=F32):
            return st.enter_context(nc.sbuf_tensor(name, shape, dt))

        x_rows = sb1("x_rows", [P, TT, D])
        vec_rows = sb1("vec_rows", [P, 6, P])
        c_rows = xrT[0:NC, 0, 0:D]
        xs_rows = xrT[0:NB, 1, 0:D]
        h_full = xgT[:, :, 0:512]
        c_half = xgT[0:NC, 0, 0:D]
        hs_full = scores[:, 0].rearrange("p k b h -> p (k b h)")[:, 0:KT * NB].rearrange("p (k b) -> p k b", b=NB)
        w_ada1 = sb1("w_ada1", [P, 2, KT, 512])
        cT = sb1("cT", [P, KT, 2 * NC])
        st.close()
        st2 = ExitStack()

        def sb2(name, shape, dt=F32):
            return st2.enter_context(nc.sbuf_tensor(name, shape, dt))

        tile_out = sb2("tile_out", [P, 2, TOK])
        st2b = ExitStack()
        a_hi = st2b.enter_context(nc.sbuf_tensor("a_hi", [P, 3, 2, 512], F32R))
        a_lo = st2b.enter_context(nc.sbuf_tensor("a_lo", [P, 3, 2, 512], F32R))
        c_parts = st2b.enter_context(nc.sbuf_tensor("c_parts", [P, KT, 2 * NC], F32R))
        st2b.close()
        tok_out = sb2("tok_out", [P, 2, TT, P])
        k_page = sb2("k_page", [P, NPG, W])
        q_row = sb2("q_row", [P, 2, W])
        st3 = ExitStack()

        def sb3(name, shape, dt=F32):
            return st3.enter_context(nc.sbuf_tensor(name, shape, dt))

        fg_y = sb3("fg_y", [H, TOK])
        fg_e = sb3("fg_e", [H, TOK])
        fcum = sb3("fcum", [H, SEQ])
        fparts = sb3("fparts", [H, 4, SEQ], F32R)
        lg_out = sb3("lg_out", [P, TT + 1, H])
        st3.close()
        st2.close()
        st4 = ExitStack()

        def sb4(name, shape, dt=F32):
            return st4.enter_context(nc.sbuf_tensor(name, shape, dt))

        k_st = sb4("k_st", [P, 2, SEQ], F32R)
        v_raw = sb4("v_raw", [P, 2, TT, HD])
        v_st = sb4("v_st", [P, 2, TT, 2 * HD], F32R)
        o_low = misc[:, 0:512]
        o_sum = misc[:, 512:1024]
        st5 = ExitStack()

        def sb5(name, shape, dt=F32):
            return st5.enter_context(nc.sbuf_tensor(name, shape, dt))

        fq_rows = sb5("fq_rows", [P, 2, SEQ], F32R)
        fk_rows = sb5("fk_rows", [P, 2, SEQ], F32R)
        probs = sb5("probs", [P, 3, SEQ])
        pt = sb5("pt", [P, 2, TT, 2, P], F32R)
        row_max = sb5("row_max", [P, 16])
        row_sum = sb5("row_sum", [P, 16])
        row_inv = sb5("row_inv", [P, 16])
        st5.close()
        st6 = ExitStack()

        def sb6(name, shape, dt=F32):
            return st6.enter_context(nc.sbuf_tensor(name, shape, dt))

        z_s = sb6("z_s", [P, 4, 512])
        z_e = sb6("z_e", [P, 3, 512])
        z_sp = sb6("z_sp", [P, 4, 512])
        z_w = sb6("z_w", [P, 4, 512])
        w_hi2 = sb6("w_hi2", [P, 2, 512], F32R)
        w_lo2 = sb6("w_lo2", [P, 2, 512], F32R)
        st6.close()
        st4.close()
        st7 = ExitStack()

        def sb7(name, shape, dt=F32):
            return st7.enter_context(nc.sbuf_tensor(name, shape, dt))

        v_page = sb7("v_page", [P, 2, NPG, W])
        r_xc = sb7("r_xc", [P, LT, TOK])
        r_a = sb7("r_a", [P, LT, TOK])
        r_t = sb7("r_t", [P, LT, TOK])
        r_i = sb7("r_i", [P, LT, TOK])
        r_h = sb7("r_h", [P, LT, TOK])
        gate_w = sb7("gate_w", [P, 2, LT, P])
        r_c = sb7("r_c", [P, 6, LT])
        lru_cols = sb7("lru_cols", [P, LT, 4 + 2 * NB])
        lru_rows = misc[0:4 + 2 * NB, 0:DL]
        R48 = NB * H
        flat_a = r_a[0:R48].rearrange("p a n -> p (a n)")
        flat_h = r_h[0:R48].rearrange("p a n -> p (a n)")
        d_f, d_z = flat_a[:, 0:SEQ + 1], flat_a[:, SEQ + 1:2 * SEQ + 1]
        d_g, d_e = flat_h[:, 0:SEQ + 1], flat_h[:, SEQ + 1:2 * SEQ + 1]
        flat_raw = w_raw[:, 2:4].rearrange("p a k n -> p (a k n)")
        d_zq = flat_raw[:, 0:WT * R48].rearrange("p (w b h) -> p w b h", w=WT, b=NB)
        d_self = flat_raw[0:NB, WT * R48:(WT + 1) * R48]
        at = (WT + 1) * R48
        d_heads = flat_raw[:, at:at + 2 * WT * R48].rearrange("p (e w b h) -> p e w b h", e=2, w=WT, b=NB)
        d_p = scores[:].rearrange("p e k b h -> p e k (b h)")
        d_acc = misc[0:R48, DL:DL + 2 * W].rearrange("p (e n) -> p e n", e=2)
        d_small = sb7("d_small", [R48, 8])
        d_diag = sb7("d_diag", [R48, R48])
        d_grp = sb7("d_grp", [R48, NB])
        d_qk = sb7("d_qk", [P, WT, NB])
        d_hm = sb7("d_hm", [P, WT, H])
        d_spread = sb7("d_spread", [H, NB, H])
        d_out = sb7("d_out", [P, 2 * WT, NB])
        st7.close()
        stA.close()
        resT = sb("resT", [P, KT, TOK])
        st8 = ExitStack()

        def sb8(name, shape, dt=F32):
            return st8.enter_context(nc.sbuf_tensor(name, shape, dt))

        x_tile = sb8("x_tile", [P, 2, D])
        x_hat = sb8("x_hat", [P, TT, D])
        xs_hat = sb8("xs_hat", [NB, 2, D])
        h2_full = sb8("h2_full", [P, 2, 512])
        hs2 = sb8("hs2", [P, 2, KT, NB])
        ln_f = sb8("ln_f", [P, 4, KT])
        st8.close()
        GMAX = 6
        GROUPS = []
        while sum(GROUPS) < FT:
            left = -(-(FT - sum(GROUPS)) // GMAX)
            GROUPS.append(-(-(FT - sum(GROUPS)) // left))
        st9 = ExitStack()

        def sb9(name, shape, dt=F32):
            return st9.enter_context(nc.sbuf_tensor(name, shape, dt))

        g_hi = sb9("g_hi", [P, GMAX, TOK], F32R)
        g_lo = sb9("g_lo", [P, GMAX, TOK], F32R)
        u_a = sb9("u_a", [P, TOK])
        u_c = sb9("u_c", [P, TOK])
        u_g = sb9("u_g", [P, TOK])
        ffn_cols = sb9("ffn_cols", [P, FT, 2 + NB])
        g_tmp = sb9("g_tmp", [P, NB])
        st9.close()
        stB = ExitStack()

        def sbB(name, shape, dt=F32):
            return stB.enter_context(nc.sbuf_tensor(name, shape, dt))

        ln2g = sbB("ln2g", [P, D])
        ln2b = sbB("ln2b", [P, D])
        y_tile = sbB("y_tile", [P, 3, D])
        ffn_rows = sbB("ffn_rows", [2 + NB, FT, P])
        stB.close()

        s_c = sem("s_c")
        s_small = sem("s_small")
        s_x = sems("s_x", 2)
        s_idz = sem("s_idz")
        s_ident = sem("s_ident")
        s_csil = sem("s_csil")
        s_ctanh = sem("s_ctanh")
        s_vt = sem("s_vt")
        s_vte = sem("s_vte")
        s_al = sems("s_al", 2)
        s_amm = sem("s_amm")
        s_arow = sem("s_arow")
        s_atr = sem("s_atr")
        s_av = sem("s_av")
        s_ap = sem("s_ap")
        s_aev = sem("s_aev")
        s_one = sem("s_one")
        s_xt = sem("s_xt")
        s_hf = sem("s_hf")
        s_hhi = sem("s_hhi")
        s_hlo = sem("s_hlo")
        s_hs = sem("s_hs")
        s_wl = sems("s_wl", 2)
        s_whi = sem("s_whi")
        s_wlo = sem("s_wlo")
        s_pm = sem("s_pm")
        s_pe = sem("s_pe")
        s_tt = sem("s_tt")
        s_te = sem("s_te")
        s_st = sems("s_st", 2)
        s_so = sems("s_so", 2)
        s_sq = sem("s_sq")
        s_kfree = sem("s_kfree")
        s_kl = sems("s_kl", NPG)
        s_ql = sems("s_ql", 2)
        s_km = sem("s_km")
        s_tab = sem("s_tab")
        s_gw0 = sem("s_gw0")
        s_gw = sem("s_gw")
        r_d = sem("r_d")
        r_s = sem("r_s")
        r_p = sem("r_p")
        s_lr = sem("s_lr")
        s_cc = sem("s_cc")
        d_d = sem("d_d")
        d_a = sem("d_a")
        d_t = sem("d_t")
        s_vl = sems("s_vl", 2 * NPG)
        d_v = sem("d_v")
        d_ac = sem("d_ac")
        g_wl = sems("g_wl", 2)
        g_wh = sem("g_wh")
        g_ws = sem("g_ws")
        g_pm = sem("g_pm")
        g_ev = sems("g_ev", 2)
        m_ev = sem("m_ev")
        n_x = sems("n_x", 2)
        n_t = sem("n_t")
        n_r = sem("n_r")
        n_q = sem("n_q")
        n_b = sem("n_b")
        n_h = sem("n_h")
        n_hi = sem("n_hi")
        n_lo = sem("n_lo")
        n_s = sem("n_s")
        n_k = sem("n_k")
        u_d = sem("u_d")
        u_g_ = sem("u_g_")
        u_h = sem("u_h")
        u_l = sem("u_l")
        u_s = sem("u_s")
        y_b = sem("y_b")
        y_t = sem("y_t")
        y_d = sem("y_d")
        y_q = sem("y_q")
        y_n = sem("y_n")
        y_g = sem("y_g")
        y_o = sem("y_o")
        y_s = sems("y_s", 3)
        y_f = sem("y_f")
        y_fs = sem("y_fs")
        s_lf = sem("s_lf")
        s_const = sem("s_const")
        s_cr = sem("s_cr")
        s_fc = sem("s_fc")
        s_fa = sem("s_fa")
        s_fp = sem("s_fp")
        s_fs = sem("s_fs")
        s_lo_ = sem("s_lo_")
        s_fz = sem("s_fz")
        s_hl = sems("s_hl", 2)
        s_fl = sems("s_fl", 2)
        s_bh = sems("s_bh", 2)
        s_b = sem("s_b")
        f_s = sem("f_s")
        f_m = sem("f_m")
        f_e = sem("f_e")
        f_r = sem("f_r")
        f_n = sem("f_n")
        f_t = sem("f_t")
        f_h = sem("f_h")
        f_l = sem("f_l")
        f_o = sem("f_o")
        o_c = sem("o_c")
        o_x = sem("o_x")
        o_y = sem("o_y")
        o_h = sem("o_h")
        o_l = sem("o_l")
        b_z = sem("b_z")
        b_c = sem("b_c")
        b_m = sem("b_m")
        b_e = sem("b_e")
        b_l = sem("b_l")
        b_s = sem("b_s")
        b_k = sem("b_k")
        b_t = sem("b_t")
        b_w = sem("b_w")
        b_h = sem("b_h")
        b_lo = sem("b_lo")
        b_o = sem("b_o")

        q_raw = w_raw[:, 0:2].rearrange("p a k n -> p a (k n)")
        k_raw = w_raw[:, 2:4].rearrange("p a k n -> p a (k n)")
        q_hi = w_hi[:].rearrange("p a k n -> p a (k n)")
        q_lo = w_lo[:].rearrange("p a k n -> p a (k n)")
        F_STEPS = 2 * TT
        F_USES = [(s, b) for s in range(F_STEPS) for b in range(1 if s % TT < 4 else 2)]
        F_N = len(F_USES)
        F_BANKS = F_STEPS // 2

        def f_cum(s):
            return sum(1 for x, _ in F_USES if x <= s)

        B_ONE = [(c, kb, max(0, kb * P - 512 * c)) for c in range(2) for kb in range(4 * c + 3, -1, -1)]
        B_STEPS = [(par,) + x for x in B_ONE for par in range(2)]
        B_N = len(B_STEPS)
        B_LAST = [max(k for k, x in enumerate(B_STEPS) if x[0] == g % 2 and x[1] == g // 2) for g in range(4)]
        assert B_N % 4 == 0 and TT == 8
        SCALE = HD ** -0.5
        BIG = 40.0
        LN_EXP = "natural_log_exp_and_others"

        R_CONV = 7 * LT + 1
        R_LOGA = R_CONV + 4 + LT
        R_ONE = R_LOGA + 3
        R_COLS = R_ONE + 2 + LT + 2 + 1
        R_ROWS = R_COLS + 4
        D_SELF, D_MAX, D_MIN = 4, 8, 10
        D_FOX, D_SB, D_P = D_MIN + 3, D_MIN + 6, D_MIN + 7
        D_ACC = D_P + 1
        D_LAST = D_ACC + 4

        def y_bank(tt):
            return (psT[:, 0:2], psB[:, 1:3])[tt % 2]

        H2_AT = [range(2 * (tt - TT // 2), 2 * (tt - TT // 2) + 2) if TT // 2 <= tt < TT else range(KT, 2 * KT) if tt == TT else ()
                 for tt in range(TT + 1)]

        V_BANKS = [psA[:, 0], psA[:, 1], psA[:, 2], psB[:, 0], psB[:, 1], psB[:, 2], psT[:, 0], psT[:, 1]]

        def z_bank(k):
            return (psA[:, 0], psB[:, 0], psT[:, 0])[k % 3]


        block = ctx.enter_context(nc.Block())

        FG_N = 6 * WT
        ADA1 = 2 * KT * P // 512
        ADA2 = 4 * KT * P // 512
        ADA_IN = ADA2 - 2 * WT
        NSMALL = 16
        pools = (i["cache_fox_k"][0].rearrange("n t h d -> n t (h d)"),
                 i["cache_sb_k"][0].rearrange("n t h d -> n t (h d)"))
        ALPHA = 2.0 ** 0.25
        EPS = 1e-5
        NF = [sum(GROUPS[:k]) for k in range(len(GROUPS) + 1)]
        G_UP0 = [KT + 2 * NF[k] + KT * k for k in range(len(GROUPS))]
        G_DN0 = [KT + 2 * NF[k + 1] + KT * k for k in range(len(GROUPS))]
        w_out = i["w_out"][0].rearrange("(k p) n -> p k n", p=P)
        w_up = i["w_up"][0].rearrange("(k p) n -> p k n", p=P)
        w_down = i["w_down"][0].rearrange("(k p) n -> p k n", p=P)
        x_rows_d = i["x_prompt"][0].rearrange("(t p) d -> p t d", p=P)
        xs_rows_d = i["x_sample"].rearrange("b t d -> (b t) d")
        vpools = (i["cache_fox_v"][0].rearrange("n t h d -> n t (h d)"),
                  i["cache_sb_v"][0].rearrange("n t h d -> n t (h d)"))
        y_rows_d = o["y_prompt"][0].rearrange("(t p) d -> p t d", p=P)

        def v_pages(engine, b, kind):
            for p in range(NPG):
                page = engine.value_load(table[0:1, ds(b * NPG + p, 1)], min_val=0, max_val=NPOOL - 1)
                engine.wait_ge(d_v, 2 * NPG * b + NPG * kind + p + 1)
                engine.dma_start(v_page[:, kind, p], vpools[kind][ds(page, 1)].rearrange("a t w -> (a t) w")).then_inc(s_vl[NPG * kind + p], 16)

        @block.sync
        def _(sp):
            small = 0

            def load(dst, src):
                nonlocal small
                small += 16
                sp.dma_start(dst, src).then_inc(s_small, 16)

            sp.dma_start(c_rows[0:1], i["c_prompt"]).then_inc(s_c, 16)
            sp.dma_start(c_rows[1:NC], i["c_sample"]).then_inc(s_c, 16)
            for n in range(2):
                sp.dma_start(w_ada1[:, n], w_ada[:, :, n * 512:n * 512 + 512]).then_inc(s_al[n], 16)
            at = 0
            for name in ("b_ada", "w_lru_conv", "b_lru_conv", "b_rgate", "b_igate", "lru_lambda", "ln1_g", "ln1_b"):
                src = i[name]
                if len(src.shape) == 3:
                    src = src.rearrange("a b c -> a (b c)")
                src = src.rearrange("a (r p) -> (a r) p", p=P)
                load(vec_rows[at:at + src.shape[0], 0], src)
                at += src.shape[0]
            load(vec_rows[0:3 * FT, 1], i["w_ffn_conv"].rearrange("a k (f p) -> (a k f) p", p=P))
            load(vec_rows[3 * FT:4 * FT, 1], i["b_ffn_conv"].rearrange("a (f p) -> (a f) p", p=P))
            load(vec_rows[0:NB * 3 * LT, 2], i["state_lru_conv"].rearrange("a b k (f p) -> (a b k f) p", p=P))
            load(vec_rows[NB * 3 * LT:NVC, 2], i["state_lru_h"].rearrange("a b (f p) -> (a b f) p", p=P))
            sfc = i["state_ffn_conv"].rearrange("a b k (f p) -> (a b k f) p", p=P)
            for n in range(3):
                r = min(P, NVD - n * P)
                load(vec_rows[0:r, 3 + n], sfc[n * P:n * P + r])
            load(xs_rows, i["x_sample"].rearrange("b t d -> (b t) d"))
            sp.dma_start(table[:], i["page_table"].rearrange("b n -> (b n)").rearrange("(a n) -> a n", a=1)).then_inc(s_tab, 16)
            assert small == 16 * NSMALL
            xv = i["x_prompt"][0].rearrange("(t p) d -> p t d", p=P)
            for h in range(2):
                sp.dma_start(x_rows[:, h * TT // 2:(h + 1) * TT // 2], xv[:, h * TT // 2:(h + 1) * TT // 2]).then_inc(s_x[h], 16)

            def ada_load(n, slot):
                sp.wait_ge(s_amm, n - 1)
                sp.dma_start(w_ada1[:, slot], w_ada[:, :, ds(n * 512, 512)]).then_inc(s_al[slot], 16)

            def w_load(n, slot, col):
                sp.wait_ge(s_wlo, n + 1)
                sp.dma_start(w_raw[:, slot], w_in[:, :, ds(col, P)]).then_inc(s_wl[slot], 16)

            for n in range(2, ADA1):
                ada_load(n, n % 2)
            for j, base in enumerate((FQ, SQ)):
                w_load(j, j, base)
            for n in range(ADA1, ADA1 + ADA_IN):
                ada_load(n, n % 2)

            def pages(u, b, kind):
                sp.wait_ge(s_km, 8 * u + 8)
                sp.dma_start(q_row[:, kind], sq_scr[ds(b, 1), kind * W:kind * W + W].to_broadcast([P, W])).then_inc(s_ql[kind], 16)
                for p in range(NPG):
                    page = sp.value_load(table[0:1, ds(b * NPG + p, 1)], min_val=0, max_val=NPOOL - 1)
                    sp.wait_ge(s_kfree, 8 * u + p + 1)
                    if kind == 0:
                        sp.dma_start(lf_pages[:, p, ds(b, 1), :].rearrange("p a h -> p (a h)"),
                                     i["cache_fox_logf"][0][ds(page, 1)].rearrange("a t h -> (a t) h")).then_inc(s_lf, 16)
                    sp.dma_start(k_page[:, p], pools[kind][ds(page, 1)].rearrange("a t w -> (a t) w")).then_inc(s_kl[p], 16)

            def q_tile(t, columns):
                for j in range(2):
                    w_load(2 * t + j + 2, j, columns[j])
                    ada_load(ADA1 + ADA_IN + 2 * t + j, j)

            with sp.Fori(0, WT - 1) as t:
                q_tile(t, (FQ + P * t + P, SQ + P * t + P))
            q_tile(WT - 1, (FK, SK))
            sp.wait_ge(s_tab, 16)
            sp.dma_start(bfg[:], i["b_fgate"].rearrange("a h -> h a")).then_inc(s_c, 16)

            def kv_tile(t, columns):
                for j in range(4):
                    if columns[j] is None:
                        sp.wait_ge(s_wlo, FG_N + 1)
                        sp.dma_start(w_raw[:, 0, :, 0:H], w_in[:, :, FG:FG + H]).then_inc(s_wl[0], 16)
                    else:
                        w_load(2 * WT + 4 * t + j + 2, j % 2, columns[j])
                    if j == 0:
                        sp.wait_ge(s_sq, 16)
                    pages(4 * t + j, 2 * t + j // 2, j % 2)

            with sp.Fori(0, WT - 1) as t:
                kv_tile(t, (FV + P * t, SV + P * t, FK + P * t + P, SK + P * t + P))
            kv_tile(WT - 1, (FV + P * WT - P, SV + P * WT - P, None, XR))
            w_load(FG_N + 2, 0, XG)
            for t in range(LT):
                for j, base in enumerate((XR, XG)):
                    if t < LT - 1:
                        w_load(FG_N + 3 + 2 * t + j, 1 - j, base + P * t + P)
                    pages(4 * WT + 2 * t + j, 2 * WT + t, j)

            sp.wait_ge(s_fc, 9)
            for n in range(4):
                sp.dma_start(f_scr[n], fparts[:, n].bitcast(F32)).then_inc(s_fs, 16)
            for h in range(2):
                sp.wait_ge(s_st[h], 16 * 2 * WT)
                sp.wait_ge(s_so[h], 16 * 2 * WT)

            sp.wait_ge(s_wlo, FG_N + 2 * LT + 3)
            def qkv_load(fox, t, par):
                hd = 2 * t + par
                row = hd * HD + (0 if fox else W)
                for half in range(2):
                    sp.dma_start(q_raw[half * HD:half * HD + HD, par], qk_scr[0, ds(row, HD)]).then_inc(s_hl[par], 16)
                    sp.dma_start(k_raw[half * HD:half * HD + HD, par], qk_scr[1, ds(row, HD)]).then_inc(s_hl[par], 16)
                v = o["p_fox_v" if fox else "p_sb_v"][0, 0].rearrange("(t p) h d -> p t h d", p=P)
                sp.dma_start(v_raw[:, par], v[:, :, ds(hd, 1)].rearrange("p t a d -> p t (a d)")).then_inc(s_hl[par], 16)

            def f_load(t, par):
                hd = 2 * t + par
                sp.dma_start(fq_rows[0:2, par].bitcast(F32), f_scr[0:2, ds(hd, 1)].rearrange("n a s -> n (a s)")).then_inc(s_fl[par], 16)
                sp.dma_start(fk_rows[2:4, par].bitcast(F32), f_scr[2:4, ds(hd, 1)].rearrange("n a s -> n (a s)")).then_inc(s_fl[par], 16)

            for par in range(2):
                qkv_load(True, 0, par)
            sp.wait_ge(s_fs, 64)
            sp.wait_ge(s_fz, 2)
            for par in range(2):
                f_load(0, par)
            sp.wait_ge(s_fp, 2)
            sp.dma_start(o["p_fox_logf"][0, 0].rearrange("(t p) h -> p t h", p=P), lg_out[:, 0:TT]).then_inc(s_lo_, 16)
            sp.dma_start(o["s_fox_logf"][0, :, 0], lg_out[0:NB, TT]).then_inc(s_lo_, 16)
            for par in range(2):
                sp.wait_ge(s_b, par + 3)
                qkv_load(True, 1, par)
            with sp.Fori(1, WT - 1) as t:
                for par in range(2):
                    sp.wait_ge(s_b, 2 * t + par + 3)
                    f_load(t, par)
                    qkv_load(True, t + 1, par)
            for par in range(2):
                sp.wait_ge(s_b, 2 * WT - 2 + par + 3)
                f_load(WT - 1, par)
                qkv_load(False, 0, par)
            with sp.Fori(1, WT) as t:
                for par in range(2):
                    sp.wait_ge(s_b, H + 2 * t + par + 1)
                    qkv_load(False, t, par)
            sp.wait_ge(s_gw0, 1)
            for g, name in enumerate(("w_rgate", "w_igate")):
                bw = i[name].shape[2]
                for n in range(i[name].shape[1]):
                    r = n * bw % P
                    sp.dma_start(gate_w[r:r + bw, g, n * bw // P, r:r + bw], i[name][0, n]).then_inc(s_gw, 16)
            sp.dma_start(o["s_lru_conv"][0, :, 0:2], i["state_lru_conv"][0, :, 1:3]).then_inc(s_cc, 16)
            sp.dma_start(o["s_ffn_conv"][0, :, 0:1], i["state_ffn_conv"][0, :, 1:2]).then_inc(s_cc, 16)
            def g_load(m, slot, src, nk=KT):
                sp.wait_ge(g_ws, m + 1)
                sp.dma_start(w_raw[:, slot, 0:nk], src).then_inc(g_wl[slot], 16)

            sp.wait_ge(s_b, 2 * H + 2)
            for j in range(2):
                g_load(j, j, w_out[:, :, j * P:j * P + P])
            with sp.Fori(0, NB) as b:
                v_pages(sp, b, 0)
            sp.wait_ge(r_p, 5)
            sp.wait_ge(r_d, R_ROWS)
            sp.dma_start(o["p_lru_conv"][0, 0], lru_rows[0:3]).then_inc(s_lr, 16)
            sp.dma_start(o["p_lru_h"][0], lru_rows[3:4]).then_inc(s_lr, 16)
            sp.dma_start(o["s_lru_h"][0], lru_rows[4:4 + NB]).then_inc(s_lr, 16)
            sp.dma_start(o["s_lru_conv"][0, :, 2], lru_rows[4 + NB:4 + 2 * NB]).then_inc(s_lr, 16)

            with sp.Fori(1, KT // 2) as t:
                for j in range(2):
                    g_load(2 * t + j, j, w_out[:, :, ds((2 * t + j) * P, P)])
            for j in range(2):
                g_load(KT + j, j, w_up[:, :, j * DFF:j * DFF + P])
            for tt in range(TT):
                if tt == 0:
                    sp.wait_ge(d_v, 2 * NPG * (NB + 1))
                    sp.wait_ge(s_lr, 64)
                    sp.wait_ge(d_d, D_LAST)
                    sp.wait_ge(d_t, 6)
                    sp.wait_ge(r_p, 5)
                if tt >= 2:
                    sp.wait_ge(n_r, 6 * (tt - 2) + 6)
                sp.dma_start(x_tile[:, tt % 2], x_rows_d[:, tt]).then_inc(n_x[tt % 2], 16)
            sp.dma_start(xs_hat[:, 0], xs_rows_d).then_inc(y_b, 16)
            for k, gs in enumerate(GROUPS):
                with sp.Fori(1 if k == 0 else 0, gs) as f:
                    for j in range(2):
                        g_load(G_UP0[k] + 2 * f + j, j, w_up[:, :, ds((NF[k] + f) * P + j * DFF, P)])
                with sp.Fori(0, KT // 2) as t:
                    for j in range(2):
                        g_load(G_DN0[k] + 2 * t + j, j, w_down[:, NF[k]:NF[k] + gs, ds((2 * t + j) * P, P)], gs)
            sp.wait_ge(g_pm, G_DN0[-1] + KT + 2)
            sp.dma_start(ln2g[:], i["ln2_g"].to_broadcast([P, D])).then_inc(y_b, 16)
            sp.dma_start(ln2b[:], i["ln2_b"].to_broadcast([P, D])).then_inc(y_b, 16)
            for tt in range(TT + 1):
                sp.wait_ge(y_o, tt + 1)
                if tt < TT:
                    sp.dma_start(y_rows_d[:, tt], y_tile[:, tt % 3]).then_inc(y_s[tt % 3], 16)
                else:
                    sp.dma_start(o["y_sample"][:, 0], y_tile[0:NB, tt % 3]).then_inc(y_s[tt % 3], 16)
            sp.wait_ge(y_f, 4)
            sp.dma_start(o["p_ffn_conv"][0, 0].rearrange("r (f p) -> r f p", p=P), ffn_rows[0:2]).then_inc(y_fs, 16)
            sp.dma_start(o["s_ffn_conv"][0, :, 1].rearrange("r (f p) -> r f p", p=P), ffn_rows[2:2 + NB]).then_inc(y_fs, 16)
            for n in range(3):
                sp.wait_ge(y_s[n], 16 * 3)
            sp.wait_ge(y_fs, 32)
            sp.wait_ge(s_lr, 64)
            sp.wait_ge(s_cc, 32)
            sp.wait_ge(s_sq, 16 * 5)

        @block.gpsimd
        def _(pool):
            nc.gpsimd.memset(ident[:], 0.0).then_inc(s_idz, 1)
            pool.wait_ge(s_idz, 1)
            nc.gpsimd.affine_select(out=ident[:], in_=ident[:], compare_op=ALU.not_equal, fill=1.0, base=0,
                                    pattern=[[-1, P]], channel_multiplier=1).then_inc(s_ident, 1)

            nc.gpsimd.memset(mask_f[:], 0.0)
            nc.gpsimd.memset(tri[:], 1.0)
            nc.gpsimd.memset(ones[:], 1.0).then_inc(s_const, 1)
            pool.wait_ge(s_const, 1)
            nc.gpsimd.affine_select(out=mask_f[:, 0], in_=mask_f[:, 0], compare_op=ALU.is_ge, fill=-1e30, base=0,
                                    pattern=[[-1, P]], channel_multiplier=1)
            nc.gpsimd.affine_select(out=mask_f[:, 1], in_=mask_f[:, 1], compare_op=ALU.is_ge, fill=-1e30, base=-1,
                                    pattern=[[1, P]], channel_multiplier=-1)
            nc.gpsimd.affine_select(out=tri[:, 0], in_=tri[:, 0], compare_op=ALU.is_ge, fill=0.0, base=0,
                                    pattern=[[-1, P]], channel_multiplier=1)
            nc.gpsimd.affine_select(out=tri[:, 1], in_=tri[:, 1], compare_op=ALU.is_ge, fill=0.0, base=-1,
                                    pattern=[[1, P]], channel_multiplier=-1).then_inc(s_const, 1)

            def unit(u, kind, round_):
                for p in range(NPG):
                    if p == 0:
                        pool.wait_ge(s_ql[kind], 16 * round_)
                    pool.wait_ge(s_kl[p], 16 * (u + 1))
                    last = nc.gpsimd.tensor_tensor(k_page[:, p], k_page[:, p], q_row[:, kind], ALU.mult)
                    last.then_inc(s_km, 1)

            pool.sem_inc(s_km, 2 * NPG)
            with pool.Fori(0, WT) as t:
                for j in range(4):
                    unit(4 * t + j, j % 2, 2 * t + j // 2 + 1)
            with pool.Fori(0, LT) as t:
                for j in range(2):
                    unit(4 * WT + 2 * t + j, j, 2 * WT + t + 1)
            pool.wait_ge(s_fc, 9)
            pool.wait_ge(s_kfree, NPG + 2 * NB * NPG)
            nc.gpsimd.memset(fq_rows[:].bitcast(F32), 0.0)
            nc.gpsimd.memset(fk_rows[:].bitcast(F32), 0.0).then_inc(s_fz, 1)
            pool.wait_ge(s_fz, 1)
            nc.gpsimd.memset(fq_rows[0:4].bitcast(F32), 1.0)
            nc.gpsimd.memset(fk_rows[0:4].bitcast(F32), 1.0).then_inc(s_fz, 1)
            with pool.Fori(0, WT) as t:
                for x in range(B_N):
                    par, c, kb, q0 = B_STEPS[x]
                    pool.wait_ge(b_h, B_N * t + x + 1)
                    nc.gpsimd.tensor_tensor(w_lo2[:, x % 2, q0:512], z_w[:, x % 4, q0:512], w_hi2[:, x % 2, q0:512].bitcast(F32),
                                            ALU.subtract).then_inc(b_lo, 1)
            with pool.Fori(0, NB) as b:
                v_pages(pool, b, 1)
            for n in range(2 * KT):
                f, cols = n % KT, slice(n // KT * 512, n // KT * 512 + 512)
                pool.wait_ge(n_hi, n + 1)
                nc.gpsimd.tensor_tensor(acts_lo[:, f, cols], h2_full[:, n % 2], acts_hi[:, f, cols].bitcast(F32), ALU.subtract).then_inc(n_lo, 1)
            pool.wait_ge(y_b, 48)
            for tt in range(TT + 1):
                rows = P if tt < TT else NB
                pool.wait_ge(y_g, tt + 1)
                nc.gpsimd.tensor_tensor(y_tile[0:rows, tt % 3], y_tile[0:rows, tt % 3], ln2b[0:rows], ALU.add).then_inc(y_o, 1)

        @block.vector
        def _(dve):
            dve.sem_inc(s_wlo, 2)
            dve.sem_inc(s_kfree, NPG)
            dve.wait_ge(s_c, 32)
            nc.vector.tensor_scalar(c_half, c_rows, 0.5, None, ALU.mult).then_inc(s_csil, 1)
            dve.wait_ge(s_ctanh, 1)
            nc.vector.scalar_tensor_tensor(out=c_rows, in0=c_rows, scalar=1.0, in1=c_half,
                                           op0=ALU.add, op1=ALU.mult).then_inc(s_csil, 1)
            dve.wait_ge(s_vt, 1)
            nc.vector.memset(cT[:, :, NC:2 * NC], 0.0)
            nc.vector.tensor_copy(cT[:, :, 0:NC], psT[:, 0, 0:KT * NC].rearrange("p (k c) -> p k c", c=NC)).then_inc(s_vte, 1)
            dve.wait_ge(s_vt, 2)
            nc.vector.tensor_copy(vecT[:, 0:NVA + NVB + NVC], psT[:, 1, 0:NVA + NVB + NVC]).then_inc(s_vte, 1)
            nc.vector.tensor_copy(vecT[:, A_SFC:A_SFC + NVD], psT[:, 0, 0:NVD]).then_inc(s_vte, 1)
            dve.wait_ge(s_vte, 3)

            def mod_evict(n, chunk, bank):
                dve.wait_ge(s_atr, n + 1)
                rows = bank.rearrange("p (k c) -> p k c", c=2 * NC)
                mod = modT[:, ds(4 * chunk, 4)]
                nc.vector.tensor_tensor(mod, rows[:, :, 0:NC], vecT[:, ds(4 * chunk, 4)].rearrange("p (k c) -> p k c", c=1).to_broadcast([P, 4, NC]),
                                        ALU.add).then_inc(s_av, 1)
                dve.wait_ge(s_av, n + 1)
                nc.vector.tensor_tensor(mod, mod, rows[:, :, NC:2 * NC], ALU.add).then_inc(s_aev, 1)

            for n in range(ADA1):
                mod_evict(n, n, psB[:, n % 2, 0:8 * NC])
            dve.wait_ge(s_aev, ADA1)
            nc.vector.tensor_scalar(modT[:, KT:2 * KT], modT[:, KT:2 * KT], 1.0, None, ALU.add).then_inc(s_one, 1)

            def split(n, half, round_, cols=P):
                dve.wait_ge(s_wl[half], 16 * round_)
                dve.wait_ge(s_pm, n + 1)
                nc.vector.tensor_copy(w_hi[:, half, :, 0:cols], w_raw[:, half, :, 0:cols]).then_inc(s_whi, 1)
                dve.wait_ge(s_whi, n + 1)
                nc.vector.tensor_tensor(w_lo[:, half, :, 0:cols], w_raw[:, half, :, 0:cols], w_hi[:, half, :, 0:cols].bitcast(F32),
                                        ALU.subtract).then_inc(s_wlo, 1)

            split(0, 0, 1)
            for h in range(2):
                for f in range(KT):
                    n = h * KT + f
                    dve.wait_ge(s_hf, n + 1)
                    nc.vector.tensor_copy(acts_hi[:, f, h * 512:h * 512 + 512], h_full[:, n % 2]).then_inc(s_hhi, 1)
                    dve.wait_ge(s_hhi, n + 1)
                    nc.vector.tensor_tensor(acts_lo[:, f, h * 512:h * 512 + 512], h_full[:, n % 2],
                                            acts_hi[:, f, h * 512:h * 512 + 512].bitcast(F32), ALU.subtract).then_inc(s_hlo, 1)
            dve.wait_ge(s_vt, 3)
            dve.wait_ge(s_one, 1)
            nc.vector.tensor_tensor(hs_full[:], psB[:, 2, 0:KT * NB].rearrange("p (k b) -> p k b", b=NB), modT[:, KT:2 * KT, 1:NC], ALU.mult).then_inc(s_hs, 1)
            dve.wait_ge(s_hs, 1)
            nc.vector.tensor_tensor(hs_full[:], hs_full[:], modT[:, 0:KT, 1:NC], ALU.add).then_inc(s_hs, 1)
            dve.wait_ge(s_hs, 2)
            nc.vector.tensor_copy(acts_hi[:, :, SEQ:TOK], hs_full[:]).then_inc(s_hs, 1)
            dve.wait_ge(s_hs, 3)
            nc.vector.tensor_tensor(acts_lo[:, :, SEQ:TOK], hs_full[:], acts_hi[:, :, SEQ:TOK].bitcast(F32), ALU.subtract).then_inc(s_hs, 1)

            for n in range(ADA1, ADA1 + ADA_IN - 1):
                mod_evict(n, n, psT[:, 1, 0:8 * NC])

            def reduce(u, kind, b):
                for p in range(NPG):
                    dve.wait_ge(s_km, 8 * u + p + 1 + 2 * NPG)
                    nc.vector.tensor_reduce(scores[:, kind, p, ds(b, 1), :].rearrange("p a h -> p (a h)"),
                                            k_page[:, p].rearrange("p (h d) -> p h d", d=HD),
                                            AX.X, ALU.add).then_inc(s_kfree, 1)

            nc.vector.tensor_copy(c_parts[:, :, 0:NC], cT[:, :, 0:NC]).then_inc(s_hs, 1)
            dve.wait_ge(s_hs, 5)
            nc.vector.tensor_tensor(c_parts[:, :, NC:2 * NC], cT[:, :, 0:NC], c_parts[:, :, 0:NC].bitcast(F32), ALU.subtract).then_inc(s_hs, 1)

            def ada_split(n, slot, round_):
                for q in range(KT // 2):
                    if q == 0:
                        dve.wait_ge(s_al[slot], 16 * round_)
                        dve.wait_ge(s_amm, ADA1 + ADA_IN + n)
                    if q == 3:
                        dve.wait_ge(s_ap, n + 1)
                    nc.vector.tensor_copy(a_hi[:, q % 3], w_ada1[:, slot, 2 * q:2 * q + 2]).then_inc(s_hhi, 1)
                    dve.wait_ge(s_hhi, 2 * KT + 4 * n + q + 1)
                    nc.vector.tensor_tensor(a_lo[:, q % 3], w_ada1[:, slot, 2 * q:2 * q + 2], a_hi[:, q % 3].bitcast(F32), ALU.subtract).then_inc(s_hlo, 1)

            with dve.Fori(0, WT) as t:
                for j in range(2):
                    split(2 * t + j + 1, 1 - j, t + j + 1)
                    ada_split(2 * t + j, j, (ADA1 + ADA_IN) // 2 + t + 1)
                    c = ADA1 + ADA_IN + 2 * t + j - 1
                    mod_evict(c, c, psT[:, 1, 0:8 * NC])
            mod_evict(ADA1 + ADA2 - 1, ADA1 + ADA2 - 1, psT[:, 1, 0:8 * NC])
            with dve.Fori(0, WT) as t:
                for j in range(4):
                    split(2 * WT + 4 * t + j + 1, (j + 1) % 2, WT + 2 * t + (j + 1) // 2 + 1)
                    reduce(4 * t + j, j % 2, 2 * t + j // 2)
            V = nc.vector

            def step(ins):
                ins.then_inc(s_fc, 1)

            def gates_logit():
                dve.wait_ge(s_const, 2)
                V.tensor_copy(ident_r[:], ident[:])
                V.tensor_copy(mask_r[:], mask_f[:]).then_inc(s_cr, 1)
                dve.wait_ge(s_c, 48)
                dve.wait_ge(s_pe, FG_N + 3)
                step(V.tensor_scalar(fg_y[:], fgT, bfg[:, 0:1], -1.0, ALU.add, ALU.mult))
                dve.wait_ge(s_fc, 1)
                step(V.tensor_scalar(fg_e[:], fg_y[:], BIG, None, ALU.min))

            def gates_log():
                dve.wait_ge(s_fa, 2)
                step(V.tensor_tensor(fg_e[:], fg_e[:], fg_y[:], ALU.max))
                dve.wait_ge(s_fc, 3)
                step(V.tensor_scalar(lgT[:], fg_e[:], -1.0, None, ALU.mult))

            def gates_sum():
                dve.wait_ge(s_fc, 4)
                step(V.tensor_tensor_scan(fcum[:], ones[0:H].to_broadcast([H, SEQ]), lgT[:, 0:SEQ], 0.0, ALU.mult, ALU.add))
                dve.wait_ge(s_fc, 5)
                step(V.tensor_copy(fparts[:, 0], fcum[:]))
                dve.wait_ge(s_fc, 6)
                step(V.tensor_tensor(fparts[:, 1], fcum[:], fparts[:, 0].bitcast(F32), ALU.subtract))
                step(V.tensor_scalar(fparts[:, 2], fparts[:, 0].bitcast(F32), -1.0, None, ALU.mult))
                dve.wait_ge(s_fc, 7)
                step(V.tensor_scalar(fparts[:, 3], fparts[:, 1].bitcast(F32), -1.0, None, ALU.mult))

            split(FG_N + 1, 1, (FG_N + 1) // 2 + 1)
            for t in range(LT):
                for j in range(2):
                    n = FG_N + 2 + 2 * t + j
                    if n <= FG_N + 2 * LT:
                        split(n, j, n // 2 + 1)
                    if 2 * t + j < 3:
                        (gates_logit, gates_log, gates_sum)[2 * t + j]()
                    reduce(4 * WT + 2 * t + j, j, 2 * WT + t)
            dve.wait_ge(s_aev, ADA1 + ADA2)
            nc.vector.tensor_scalar(modT[:, 4 * KT:5 * KT], modT[:, 4 * KT:5 * KT], 1.0, None, ALU.add).then_inc(s_one, 1)
            dve.wait_ge(s_fp, 1)
            step(V.tensor_copy(lg_out[:, 0:TT], psT[:, 0, 0:TT * H].rearrange("p (t h) -> p t h", h=H)))
            V.tensor_copy(lg_out[0:NB, TT], psT[0:NB, 0, TT * H:TT * H + H]).then_inc(s_fp, 1)
            dve.wait_ge(s_pe, FG_N + 2 * LT + 3)
            for h in range(2):
                dve.wait_ge(s_st[h], 16 * 2 * WT)
                dve.wait_ge(s_so[h], 16 * 2 * WT)

            dve.sem_inc(s_b, 2)

            def build_qk(m, par):
                dve.wait_ge(s_hl[par], 16 * 5 * (m + 1))
                V.tensor_scalar(q_hi[:, par], q_raw[:, par], SCALE, None, ALU.mult)
                V.tensor_copy(k_st[:, par], k_raw[:, par]).then_inc(s_bh[par], 1)
                dve.wait_ge(s_bh[par], 2 * m + 1)
                V.scalar_tensor_tensor(out=q_lo[:, par], in0=q_raw[:, par], scalar=SCALE, in1=q_hi[:, par].bitcast(F32),
                                       op0=ALU.mult, op1=ALU.subtract)
                V.tensor_tensor(k_st[HD:P, par], k_raw[HD:P, par], k_st[HD:P, par].bitcast(F32), ALU.subtract)

            def build_v(m, par):
                V.tensor_copy(v_st[:, par, :, 0:HD], v_raw[:, par]).then_inc(s_bh[par], 1)
                dve.wait_ge(s_bh[par], 2 * m + 2)
                V.tensor_tensor(v_st[:, par, :, HD:2 * HD], v_raw[:, par], v_st[:, par, :, 0:HD].bitcast(F32), ALU.subtract).then_inc(s_b, 1)

            def build(m, par):
                build_qk(m, par)
                build_v(m, par)

            def fox_bank(n, par, tile, q0, bank):
                r = slice(par * HD, par * HD + HD)
                dve.wait_ge(o_l, n)
                dve.wait_ge(o_c, n + 1)
                V.tensor_tensor(o_sum[r], bank[0:HD], o_low[r], ALU.add).then_inc(o_x, 1)
                dve.wait_ge(o_x, n + 1)
                parts = o_sum[r].rearrange("p (q e n) -> p q e n", q=2, e=2)
                V.tensor_tensor(parts[:, :, 0], parts[:, :, 0], parts[:, :, 1], ALU.add).then_inc(o_y, 1)
                dve.wait_ge(o_y, n + 1)
                hi = acts_hi[r, ds(tile, 1), q0:q0 + 2 * P].rearrange("p a (q n) -> p (a q) n", q=2)
                lo = acts_lo[r, ds(tile, 1), q0:q0 + 2 * P].rearrange("p a (q n) -> p (a q) n", q=2)
                V.tensor_copy(hi, parts[:, :, 0]).then_inc(o_h, 1)
                dve.wait_ge(o_h, n + 1)
                V.tensor_tensor(lo, parts[:, :, 0], hi.bitcast(F32), ALU.subtract).then_inc(o_l, 1)

            def out_bank(n, par, tile, q0, bank):
                r = slice(par * HD, par * HD + HD)
                dve.wait_ge(o_c, n + 1)
                V.tensor_tensor(o_sum[r], bank[0:HD], o_low[r], ALU.add).then_inc(o_x, 1)
                dve.wait_ge(o_x, n + 1)
                V.tensor_copy(acts_hi[r, ds(tile, 1), q0:q0 + 512].rearrange("p a n -> p (a n)"), o_sum[r]).then_inc(o_h, 1)
                dve.wait_ge(o_h, n + 1)
                V.tensor_tensor(acts_lo[r, ds(tile, 1), q0:q0 + 512].rearrange("p a n -> p (a n)"), o_sum[r],
                                acts_hi[r, ds(tile, 1), q0:q0 + 512].rearrange("p a n -> p (a n)").bitcast(F32), ALU.subtract).then_inc(o_l, 1)

            build(0, 0)
            dve.wait_ge(s_fs, 64)
            dve.wait_ge(s_lo_, 32)
            with dve.Fori(0, WT) as t:
                for s in range(F_STEPS + 5):
                    if s < F_STEPS:
                        dve.wait_ge(f_s, F_STEPS * t + s + 1)
                        nk = (s % TT + 1) * P
                        ps = proj_ps[s % 2][:, 0:2].rearrange("p a n -> p (a n)")[:, 0:nk]
                        V.tensor_reduce(row_max[:, s:s + 1], ps, AX.X, ALU.max, negate=True).then_inc(f_m, 1)
                    if 1 <= s < F_STEPS + 1:
                        x = s - 1
                        dve.wait_ge(f_e, F_STEPS * t + x + 1)
                        V.reciprocal(row_inv[:, x:x + 1], row_sum[:, x:x + 1]).then_inc(f_r, 1)
                        dve.wait_ge(f_r, F_STEPS * t + x + 1)
                        nk = (x % TT + 1) * P
                        V.tensor_scalar(probs[:, x % 3, 0:nk], probs[:, x % 3, 0:nk], row_inv[:, x:x + 1], None, ALU.mult).then_inc(f_n, 1)
                    if 2 <= s < F_STEPS + 2:
                        x = s - 2
                        for u, (y, b) in enumerate(F_USES):
                            if y == x:
                                nb = min(4, x % TT + 1 - 4 * b)
                                dve.wait_ge(f_h, F_N * t + u + 1)
                                V.tensor_tensor(pt[:, x % 2, 4 * b:4 * b + nb, 1], psT[:, b, 0:nb * P].rearrange("p (k n) -> p k n", n=P),
                                                pt[:, x % 2, 4 * b:4 * b + nb, 0].bitcast(F32), ALU.subtract).then_inc(f_l, 1)
                    if s >= 5 and s % 2 == 1:
                        g = (s - 5) // 2
                        fox_bank(F_BANKS * t + g, g // (TT // 2), t, g % (TT // 2) * 2 * P, proj_ps[g % 2][:, 2])
                    if s == 3:
                        dve.wait_ge(f_o, F_STEPS * t)
                        build(t, 1)
                    if s == TT + 3:
                        dve.wait_ge(f_o, F_STEPS * t + TT)
                        build(t + 1, 0)

            def stick_breaking(t, last_one):
                for k in range(B_N + 5):
                    if k >= B_N and k < B_N + 2 and not last_one:
                        dve.wait_ge(b_z, B_N * t + B_N)
                        build_qk(WT + t + 1, k - B_N)
                    if k < B_N:
                        par, c, kb, q0 = B_STEPS[k]
                        dve.wait_ge(b_c, B_N * t + k + 1)
                        V.tensor_scalar(z_e[:, k % 3, q0:512], z_s[:, k % 4, q0:512], BIG, None, ALU.min).then_inc(b_m, 1)
                    if 2 <= k < B_N + 2:
                        x = k - 2
                        par, c, kb, q0 = B_STEPS[x]
                        dve.wait_ge(b_k, B_N * t + x + 1)
                        dve.wait_ge(b_lo, B_N * t + max(0, x - 3))
                        V.tensor_tensor(z_w[:, x % 4, q0:512], z_s[:, x % 4, q0:512], proj_ps[par][:, 2, q0:512], ALU.subtract).then_inc(b_t, 1)
                    if 4 <= k < B_N + 4:
                        x = k - 4
                        par, c, kb, q0 = B_STEPS[x]
                        dve.wait_ge(b_w, B_N * t + x + 1)
                        dve.wait_ge(b_o, B_N * t + max(0, x - 1))
                        V.tensor_copy(w_hi2[:, x % 2, q0:512], z_w[:, x % 4, q0:512]).then_inc(b_h, 1)
                    if 1 <= k < B_N + 1:
                        x = k - 1
                        par, c, kb, q0 = B_STEPS[x]
                        dve.wait_ge(b_l, B_N * t + x + 1)
                        V.tensor_tensor(z_sp[:, x % 4, q0:512], z_e[:, x % 3, q0:512], z_s[:, x % 4, q0:512], ALU.max).then_inc(b_s, 1)
                    for g in range(4):
                        if k == min(B_LAST[g] + 5, B_N + 4):
                            out_bank(F_BANKS * WT + 4 * t + g, g % 2, WT + t, g // 2 * 512, proj_ps[g % 2][:, 1])
                if not last_one:
                    dve.wait_ge(b_o, B_N * t + B_N)
                    for par in range(2):
                        build_v(WT + t + 1, par)

            build(WT, 1)
            with dve.Fori(0, WT - 1) as t:
                stick_breaking(t, False)
            stick_breaking(WT - 1, True)

            dve.sem_inc(g_ws, 2)
            V.memset(gate_w[:], 0.0).then_inc(s_gw0, 1)
            dd = 0

            def dstep(ins):
                nonlocal dd
                dd += 1
                ins.then_inc(d_d, 1)
                dve.wait_ge(d_d, dd)

            dstep(V.tensor_tensor(d_qk[:], smpT[:, 0:2 * WT:2], smpT[:, 2 * WT:6 * WT:4], ALU.mult))
            V.memset(d_hm[:], 0.0).then_inc(d_d, 1)
            dd += 1
            dve.wait_ge(d_d, dd)
            for t in range(WT):
                V.memset(d_hm[0:HD, t, 2 * t:2 * t + 1], 1.0)
                last = V.memset(d_hm[HD:P, t, 2 * t + 1:2 * t + 2], 1.0)
            dstep(last)
            for t in range(WT):
                V.tensor_tensor(d_zq[:, t], d_qk[:, t].rearrange("p (b a) -> p b a", a=1).to_broadcast([P, NB, H]),
                                d_hm[:, t].rearrange("p (a h) -> p a h", a=1).to_broadcast([P, NB, H]), ALU.mult)
            V.tensor_reduce(d_grp[:], ident[0:R48, 0:R48].rearrange("p (b h) -> p b h", h=H), AX.X, ALU.add)
            dstep(V.tensor_tensor(d_spread[:], lgT[:, SEQ:TOK].rearrange("p (b a) -> p b a", a=1).to_broadcast([H, NB, H]),
                                  ident[0:H, 0:H].rearrange("p (a h) -> p a h", a=1).to_broadcast([H, NB, H]), ALU.mult))
            assert dd == D_SELF
            dve.wait_ge(d_t, 2)
            dstep(V.tensor_copy(d_g[:, SEQ:SEQ + 1], psA[0:R48, 2, 1:2]))
            dstep(V.tensor_tensor_scan(d_g[:, 0:SEQ][:, ::-1], ones[0:R48].to_broadcast([R48, SEQ]),
                                       psT[0:R48].rearrange("p a n -> p (a n)")[:, ::-1], d_g[:, SEQ:SEQ + 1], ALU.mult, ALU.add))
            V.tensor_scalar(d_f[:, SEQ:SEQ + 1], psA[0:R48, 2, 0:1], SCALE, None, ALU.mult)
            dstep(V.scalar_tensor_tensor(out=d_f[:, 0:SEQ], in0=psA[0:R48, 0:2].rearrange("p a n -> p (a n)"), scalar=SCALE,
                                         in1=d_g[:, 1:SEQ + 1], op0=ALU.mult, op1=ALU.add))
            dstep(V.tensor_reduce(d_small[:, 0:1], d_f[:], AX.X, ALU.max, negate=True))
            assert dd == D_MAX
            dstep(V.tensor_scalar(d_z[:], psB[0:R48, 0:2].rearrange("p a n -> p (a n)"), SCALE, None, ALU.mult))
            dstep(V.tensor_scalar(d_e[:], d_z[:], BIG, None, ALU.min))
            assert dd == D_MIN
            dve.wait_ge(d_a, 1)
            dstep(V.reciprocal(d_small[:, 2:3], d_small[:, 1:2]))
            dstep(V.tensor_scalar(d_f[:], d_f[:], d_small[:, 2:3], None, ALU.mult))
            dstep(V.tensor_scalar(d_diag[:], ident[0:R48, 0:R48], d_f[:, SEQ:SEQ + 1], None, ALU.mult))
            assert dd == D_FOX
            dve.wait_ge(d_a, 3)
            dstep(V.tensor_tensor(d_e[:], d_e[:], d_z[:], ALU.max))
            dstep(V.tensor_tensor_scan(d_g[:, 0:SEQ][:, ::-1], ones[0:R48].to_broadcast([R48, SEQ]), d_e[:, ::-1], 0.0, ALU.mult, ALU.add))
            dstep(V.tensor_tensor(d_z[:], d_z[:], d_g[:, 0:SEQ], ALU.subtract))
            assert dd == D_SB
            dve.wait_ge(d_t, 4)
            V.tensor_copy(d_self[:], psA[0:NB, 2, 0:R48])
            V.tensor_copy(d_p[:, 0], psT[:, 0, 0:NPG * R48].rearrange("p (k n) -> p k n", n=R48))
            dstep(V.tensor_copy(d_p[:, 1], psT[:, 1, 0:NPG * R48].rearrange("p (k n) -> p k n", n=R48)))
            assert dd == D_P
            dve.wait_ge(d_t, 5)
            V.memset(d_acc[:, 1], 0.0)
            dstep(V.tensor_copy(d_acc[:, 0], psT[0:R48, 1, 0:W]))
            assert dd == D_ACC

            rd = 0

            def rstep(ins):
                nonlocal rd
                rd += 1
                ins.then_inc(r_d, 1)
                dve.wait_ge(r_d, rd)

            for t in range(LT):
                rstep(V.tensor_scalar(r_xc[:, t], xrT[:, t], vecT[:, A_WLC + 3 * LT + t:A_WLC + 3 * LT + t + 1],
                                      vecT[:, A_BLC + t:A_BLC + t + 1], ALU.mult, ALU.add))
                for k in range(3):
                    w = vecT[:, A_WLC + k * LT + t:A_WLC + k * LT + t + 1]
                    rstep(V.scalar_tensor_tensor(out=r_xc[:, t, 3 - k:SEQ], in0=xrT[:, t, 0:SEQ - 3 + k], scalar=w,
                                                 in1=r_xc[:, t, 3 - k:SEQ], op0=ALU.mult, op1=ALU.add))
                    past = vecT[:, A_SLC:A_SLH].rearrange("p (b k f) -> p b k f", k=3, f=LT)[:, :, k, t]
                    now = r_xc[:, t, SEQ:TOK]
                    rstep(V.scalar_tensor_tensor(out=now, in0=past, scalar=w, in1=now, op0=ALU.mult, op1=ALU.add))
            rstep(V.tensor_scalar(r_c[:, 0:2], vecT[:, A_BR:A_BR + 2 * LT].rearrange("p (g t) -> p g t", t=LT), 0.5, None, ALU.mult))
            assert rd == R_CONV
            rstep(V.tensor_scalar(r_c[:, 2], vecT[:, A_LAM:A_LAM + LT], -1.0, None, ALU.mult))
            rstep(V.tensor_scalar(r_c[:, 3], r_c[:, 2], BIG, None, ALU.min))
            dve.wait_ge(r_s, 2)
            rstep(V.tensor_tensor(r_c[:, 3], r_c[:, 3], r_c[:, 2], ALU.max))
            rstep(V.tensor_scalar(r_c[:, 4], r_c[:, 3], -4.0, None, ALU.mult))
            def v_units(t):
                for i4 in range(NB // 2):
                    for kind in range(2):
                        u = NB * t + 2 * i4 + kind
                        dve.wait_ge(d_v, NPG * (u + 3))
                        dve.wait_ge(d_ac, u + 7)
                        b = NB // 2 * t + i4
                        V.scalar_tensor_tensor(out=d_acc[:, kind], in0=V_BANKS[2 * i4 + kind][0:R48, 0:W], scalar=d_grp[:, b:b + 1],
                                               in1=d_acc[:, kind], op0=ALU.mult, op1=ALU.add).then_inc(d_ac, 1)

            dve.sem_inc(d_ac, 8)
            v_units(0)
            dve.wait_ge(r_s, 6)
            for t in range(LT):
                rstep(V.tensor_scalar(r_t[:, t], r_t[:, t], r_c[:, 4, t:t + 1], r_c[:, 4, t:t + 1], ALU.mult, ALU.add))
            assert rd == R_LOGA
            dve.wait_ge(r_s, 8)
            rstep(V.tensor_tensor(r_t[:], r_a[:], r_a[:], ALU.mult))
            rstep(V.tensor_scalar(r_t[:], r_t[:], 1.0, None, ALU.add))
            rstep(V.scalar_tensor_tensor(out=r_h[:], in0=r_h[:], scalar=-1.0, in1=r_t[:], op0=ALU.mult, op1=ALU.mult))
            assert rd == R_ONE
            rstep(V.scalar_tensor_tensor(out=r_i[:], in0=r_i[:], scalar=1.0, in1=r_xc[:], op0=ALU.add, op1=ALU.mult))
            dve.wait_ge(r_s, 9)
            rstep(V.scalar_tensor_tensor(out=r_i[:], in0=r_i[:], scalar=0.5, in1=r_h[:], op0=ALU.mult, op1=ALU.mult))
            for t in range(LT):
                rstep(V.tensor_tensor_scan(r_t[:, t, 0:SEQ], r_a[:, t, 0:SEQ], r_i[:, t, 0:SEQ], 0.0, ALU.mult, ALU.add))
            h0 = vecT[:, A_SLH:A_SLH + NB * LT].rearrange("p (b f) -> p f b", f=LT)
            rstep(V.tensor_tensor(r_t[:, :, SEQ:TOK], r_a[:, :, SEQ:TOK], h0, ALU.mult))
            rstep(V.tensor_tensor(r_t[:, :, SEQ:TOK], r_t[:, :, SEQ:TOK], r_i[:, :, SEQ:TOK], ALU.add))
            V.tensor_copy(lru_cols[:, :, 0:3], xrT[:, :, SEQ - 3:SEQ])
            V.tensor_copy(lru_cols[:, :, 3:4 + NB], r_t[:, :, SEQ - 1:TOK])
            rstep(V.tensor_copy(lru_cols[:, :, 4 + NB:4 + 2 * NB], xrT[:, :, SEQ:TOK]))
            assert rd == R_COLS
            dve.wait_ge(r_s, 10)
            rstep(V.tensor_tensor(r_xc[:], r_t[:], xgT[:], ALU.mult))
            rstep(V.tensor_copy(acts_hi[:, 2 * WT:KT], r_xc[:]))
            rstep(V.tensor_tensor(acts_lo[:, 2 * WT:KT], r_xc[:], acts_hi[:, 2 * WT:KT].bitcast(F32), ALU.subtract))

            def g_split(m, slot, round_, nk=KT):
                dve.wait_ge(g_wl[slot], 16 * round_)
                dve.wait_ge(g_pm, m + 1)
                V.tensor_copy(w_hi[:, slot, 0:nk], w_raw[:, slot, 0:nk]).then_inc(g_wh, 1)
                dve.wait_ge(g_wh, m + 1)
                V.tensor_tensor(w_lo[:, slot, 0:nk], w_raw[:, slot, 0:nk], w_hi[:, slot, 0:nk].bitcast(F32), ALU.subtract).then_inc(g_ws, 1)

            g_split(0, 0, 1)
            v_units(1)
            dve.wait_ge(r_p, 5)
            rstep(V.tensor_copy(lru_rows[:], psA[0:4 + 2 * NB, 0, 0:DL]))
            assert rd == R_ROWS
            dve.wait_ge(d_t, 6)
            for kind in range(2):
                last = V.tensor_tensor(d_heads[:, kind], psB[:, 0, kind * WT * R48:(kind + 1) * WT * R48].rearrange("p (w b h) -> p w b h", w=WT, b=NB),
                                       d_hm[:].rearrange("p w (a h) -> p w a h", a=1).to_broadcast([P, WT, NB, H]), ALU.mult)
            dstep(last)
            dstep(V.tensor_reduce(d_out[:].rearrange("p w b -> p (w b)"), d_heads.rearrange("p e w b h -> p (e w b) h"), AX.X, ALU.add))
            dstep(V.tensor_copy(acts_hi[:, 0:2 * WT, SEQ:TOK], d_out[:]))
            dstep(V.tensor_tensor(acts_lo[:, 0:2 * WT, SEQ:TOK], d_out[:], acts_hi[:, 0:2 * WT, SEQ:TOK].bitcast(F32), ALU.subtract))
            assert dd == D_LAST

            def col(ap):
                return ap.rearrange("p a n -> p (a n)")

            with dve.Fori(0, KT // 2) as t:
                for j in range(2):
                    m = 2 * t + j
                    g_split(m + 1, 1 - j, t + 1 + j)
                    dve.wait_ge(m_ev, m + 1)
                    V.tensor_tensor(resT[:, ds(m, 1), SEQ:TOK], proj_ps[j][:, 2:3, CH - NB:CH], modT[:, ds(2 * KT + m, 1), 1:NC], ALU.mult).then_inc(g_ev[j], 1)
            k1 = slice(4 * KT, 5 * KT)
            V.tensor_tensor(ln_f[:, 0], vecT[:, A_L1G:A_L1G + KT], modT[:, k1, 0], ALU.mult)
            V.tensor_tensor(ln_f[:, 1], vecT[:, A_L1B:A_L1B + KT], modT[:, k1, 0], ALU.mult)
            V.tensor_scalar(ln_f[:, 2], vecT[:, A_L1G:A_L1G + KT], ALPHA, None, ALU.mult)
            V.tensor_scalar(ln_f[:, 3], vecT[:, A_L1B:A_L1B + KT], ALPHA, None, ALU.mult).then_inc(n_k, 1)
            dve.wait_ge(n_k, 1)
            V.tensor_tensor(ln_f[:, 1], ln_f[:, 1], modT[:, 3 * KT:4 * KT, 0], ALU.add).then_inc(n_k, 1)

            def norm_rows(n, rows, src, sem_, sq, inc0):
                st = ln_st[0:rows, n % 2]
                for c in range(2):
                    last = V.bn_stats(st[:, 6 * c:6 * c + 6], src[:, 512 * c:512 * c + 512])
                last.then_inc(sem_, 1)
                dve.wait_ge(sem_, inc0 + 1)
                V.bn_aggr(st[:, 12:14], st[:, 0:12]).then_inc(sem_, 1)
                dve.wait_ge(sem_, inc0 + 2)
                V.tensor_scalar(st[:, 14:15], st[:, 13:14], EPS, None, ALU.add).then_inc(sem_, 1)
                dve.wait_ge(sq, n + 1)
                V.reciprocal(st[:, 15:16], st[:, 14:15]).then_inc(sem_, 1)
                dve.wait_ge(sem_, inc0 + 4)

            def h2_hi(tt):
                for n in H2_AT[tt]:
                    f, h = n % KT, n // KT
                    dve.wait_ge(n_h, n + 1)
                    V.tensor_copy(acts_hi[:, f, h * 512:h * 512 + 512], h2_full[:, n % 2]).then_inc(n_hi, 1)

            for tt in range(TT + 1):
                if tt < TT:
                    dve.wait_ge(n_x[tt % 2], 16 * (tt // 2 + 1))
                    x, rows = x_tile[:, tt % 2], P
                else:
                    dve.wait_ge(y_b, 16)
                    x, rows = xs_hat[:, 0], NB
                dve.wait_ge(n_t, tt + 1)
                src = y_bank(tt)[0:rows].rearrange("p a n -> p (a n)")
                V.scalar_tensor_tensor(out=x, in0=x, scalar=ALPHA, in1=src, op0=ALU.mult, op1=ALU.add).then_inc(n_r, 1)
                dve.wait_ge(n_r, 6 * tt + 1)
                norm_rows(tt, rows, x, n_r, n_q, 6 * tt + 1)
                dst = x_hat[:, tt] if tt < TT else xs_hat[:, 1]
                st = ln_st[0:rows, tt % 2]
                V.tensor_scalar(dst, x, st[:, 12:13], st[:, 15:16], ALU.subtract, ALU.mult).then_inc(n_r, 1)
                h2_hi(tt)
            dve.wait_ge(n_b, 2 * KT + 1)

            def over_b(ap):
                return ap.rearrange("p (k a) -> p k a", a=1).to_broadcast([P, KT, NB])

            xs = psA[:, 2, 0:KT * NB].rearrange("p (k b) -> p k b", b=NB)
            V.tensor_tensor(hs2[:, 0], xs, over_b(vecT[:, A_L1G:A_L1G + KT]), ALU.mult).then_inc(n_s, 1)
            dve.wait_ge(n_s, 1)
            V.tensor_tensor(hs2[:, 0], hs2[:, 0], over_b(vecT[:, A_L1B:A_L1B + KT]), ALU.add).then_inc(n_s, 1)
            dve.wait_ge(n_s, 2)
            V.tensor_scalar(resT[:, :, SEQ:TOK], hs2[:, 0], ALPHA, None, ALU.mult)
            V.tensor_tensor(hs2[:, 1], hs2[:, 0], modT[:, k1, 1:NC], ALU.mult).then_inc(n_s, 1)
            dve.wait_ge(n_s, 3)
            V.tensor_tensor(hs2[:, 1], hs2[:, 1], modT[:, 3 * KT:4 * KT, 1:NC], ALU.add).then_inc(n_s, 1)
            dve.wait_ge(n_s, 4)
            V.tensor_copy(acts_hi[:, :, SEQ:TOK], hs2[:, 1]).then_inc(n_s, 1)
            dve.wait_ge(n_s, 5)
            V.tensor_tensor(acts_lo[:, :, SEQ:TOK], hs2[:, 1], acts_hi[:, :, SEQ:TOK].bitcast(F32), ALU.subtract).then_inc(n_s, 1)
            dve.wait_ge(n_s, 6)

            sfc = vecT[:, A_SFC:A_SFC + NVD].rearrange("p (b k f) -> p b k f", k=2, f=FT)
            def wc(n, F):
                return vecT[:, ds(A_WFC + n * FT + F, 1)]

            def conv(k, F):
                dve.wait_ge(g_ev[0], KT // 2 * (k + 1) + F + 2)
                V.tensor_scalar(u_c[:], u_a[:], wc(2, F), vecT[:, ds(A_BFC + F, 1)], ALU.mult, ALU.add).then_inc(u_d, 1)
                dve.wait_ge(u_d, 3 * F + 1)
                for n in (1, 0):
                    d = 2 - n
                    V.scalar_tensor_tensor(out=u_c[:, d:SEQ], in0=u_a[:, 0:SEQ - d], scalar=wc(n, F), in1=u_c[:, d:SEQ], op0=ALU.mult, op1=ALU.add)
                    V.scalar_tensor_tensor(out=u_c[:, SEQ:TOK], in0=sfc[:, :, n, ds(F, 1)].rearrange("p b a -> p (b a)"), scalar=wc(n, F),
                                           in1=u_c[:, SEQ:TOK], op0=ALU.mult, op1=ALU.add).then_inc(u_d, 1)
                    if n == 1:
                        dve.wait_ge(u_d, 3 * F + 2)

            def gated(k, f, F):
                dve.wait_ge(u_g_, F + 1)
                dve.wait_ge(g_pm, G_UP0[k] + 2 * f + 4)
                V.tensor_tensor(u_g[:].rearrange("p (c n) -> p c n", c=NCH), u_g[:].rearrange("p (c n) -> p c n", c=NCH),
                                psB[:, :, 0:CH], ALU.mult).then_inc(g_ev[1], 1)
                dve.wait_ge(g_ev[1], KT // 2 * (k + 1) + F + 2)
                V.tensor_copy(g_hi[:, ds(f, 1)], u_g[:].rearrange("p (a n) -> p a n", a=1)).then_inc(u_h, 1)
                dve.wait_ge(u_h, F + 1)
                V.tensor_tensor(g_lo[:, ds(f, 1)], u_g[:].rearrange("p (a n) -> p a n", a=1), g_hi[:, ds(f, 1)].bitcast(F32), ALU.subtract).then_inc(u_l, 1)

            def up(k, f, first=False):
                F = NF[k] + f
                round_ = KT // 2 * (k + 1) + F + 1
                g_split(G_UP0[k] + 2 * f + 1, 1, round_)
                if not first:
                    gated(k, f - 1, F - 1)
                g_split(G_UP0[k] + 2 * f + 2, 0, round_ + 1)
                conv(k, F)

            def down(k, t, last):
                for j in range(2):
                    m = 2 * t + j
                    M = G_DN0[k] + m
                    round_ = KT // 2 * (k + 1) + NF[k + 1] + t + 1
                    if not (last and j == 1 and k == len(GROUPS) - 1):
                        g_split(M + 1, 1 - j, round_ + j)
                    gate = modT[:, ds(5 * KT + m, 1), 0:1].rearrange("p a n -> p (a n)")
                    dve.wait_ge(g_pm, M + 3)
                    acc = resT[:, ds(m, 1)].rearrange("p a n -> p (a n)")
                    V.scalar_tensor_tensor(out=acc[:, 0:2 * CH].rearrange("p (c n) -> p c n", c=2), in0=proj_ps[j][:, 0:2, 0:CH], scalar=gate,
                                           in1=acc[:, 0:2 * CH].rearrange("p (c n) -> p c n", c=2), op0=ALU.mult, op1=ALU.add)
                    V.scalar_tensor_tensor(out=acc[:, 2 * CH:SEQ], in0=proj_ps[j][:, 2, 0:SEQ - 2 * CH], scalar=gate,
                                           in1=acc[:, 2 * CH:SEQ], op0=ALU.mult, op1=ALU.add)
                    V.tensor_tensor(g_tmp[:], proj_ps[j][:, 2, CH - NB:CH], modT[:, ds(5 * KT + m, 1), 1:NC].rearrange("p a n -> p (a n)"),
                                    ALU.mult).then_inc(g_ev[j], 1)
                    dve.wait_ge(g_ev[j], round_ + 1)
                    V.tensor_tensor(acc[:, SEQ:TOK], acc[:, SEQ:TOK], g_tmp[:], ALU.add).then_inc(u_s, 1)
                    dve.wait_ge(u_s, KT * k + m + 1)

            for k, gs in enumerate(GROUPS):
                up(k, 0, first=True)
                with dve.Fori(1, gs) as f:
                    up(k, f)
                gated(k, gs - 1, NF[k + 1] - 1)
                with dve.Fori(0, KT // 2 - 1) as t:
                    down(k, t, False)
                down(k, KT // 2 - 1, True)

            for tt in range(TT + 2):
                if tt <= TT:
                    rows = P if tt < TT else NB
                    dve.wait_ge(y_t, tt + 1)
                    norm_rows(tt, rows, y_bank(tt)[0:rows].rearrange("p a n -> p (a n)"), y_d, y_q, 5 * tt)
                    st = ln_st[0:rows, tt % 2]
                    V.scalar_tensor_tensor(out=st[:, 14:15], in0=st[:, 12:13], scalar=-1.0, in1=st[:, 15:16],
                                           op0=ALU.mult, op1=ALU.mult).then_inc(y_d, 1)
                if tt >= 1:
                    x = tt - 1
                    rows = P if x < TT else NB
                    dve.wait_ge(y_n, x + 1)
                    if x == 0:
                        dve.wait_ge(y_b, 48)
                    V.tensor_tensor(y_tile[0:rows, x % 3], y_tile[0:rows, x % 3], ln2g[0:rows], ALU.mult).then_inc(y_g, 1)
            for c in range(2):
                dve.wait_ge(y_f, c + c + 1)
                nf = FT // 2
                bank = (psA, psB)[c]
                V.tensor_copy(ffn_rows[:, c * nf:(c + 1) * nf], bank[0:2 + NB].rearrange("p a n -> p (a n)")[:, 0:nf * P].rearrange("p (f n) -> p f n", n=P)).then_inc(y_f, 1)

        @block.scalar
        def _(act):
            act.wait_ge(s_csil, 1)
            nc.scalar.activation(c_rows, c_half, ACT.Tanh).then_inc(s_ctanh, 1)

            def mod_rows(n, slot, bank, reused=True):
                act.wait_ge(s_amm, n + 1)
                if reused:
                    act.wait_ge(s_atr, n - 1)
                nc.scalar.activation(ada_rows[:, slot], bank[0:2 * NC], ACT.Copy).then_inc(s_arow, 1)

            for n in range(ADA1):
                mod_rows(n, n % 2, psA[:, n % 2], reused=n >= 2)
            act.wait_ge(s_one, 1)
            for h in range(2):
                for f in range(KT):
                    n = h * KT + f
                    act.wait_ge(s_xt, n + 1)
                    if n >= 2:
                        act.wait_ge(s_hlo, n - 1)
                    nc.scalar.activation(h_full[:, n % 2], proj_ps[n % 2][:, n // 2 % 2], ACT.Identity,
                                         bias=modT[:, f, 0:1], scale=modT[:, KT + f, 0:1]).then_inc(s_hf, 1)
            for n in range(ADA1, ADA1 + ADA_IN):
                mod_rows(n, n % 2, psT[:, 0])

            def evict(n, half, dst, rows=P, samples=False):
                act.wait_ge(s_pm, n + 3)
                if samples:
                    nc.scalar.activation(smpT[:, ds(n, 1), :].rearrange("p a b -> p (a b)"), proj_ps[half][:, NCH - 1, CH - NB:CH], ACT.Copy)
                nc.scalar.activation(dst.rearrange("p (c n) -> p c n", c=NCH), proj_ps[half][0:rows, :, 0:CH], ACT.Copy).then_inc(s_pe, 1)

            with act.Fori(0, WT) as t:
                for j in range(2):
                    n = 2 * t + j
                    act.wait_ge(s_st[j], 16 * t)
                    evict(n, j, tile_out[:, j], samples=True)
                    act.wait_ge(s_pe, n + 3)
                    act.dma_start(qk_scr[0, ds(j * W + P * t, P)], tile_out[:, j, 0:SEQ]).then_inc(s_st[j], 16)
                    mod_rows(ADA1 + ADA_IN + n, j, psT[:, 0])
            act.wait_ge(s_tt, 1)
            nc.scalar.activation(smp_out[:, 0:2 * WT].rearrange("p (a j) n -> p a (j n)", a=2), psT[0:NB, :, 0:W], ACT.Copy).then_inc(s_te, 1)
            act.wait_ge(s_te, 1)
            act.dma_start(sq_scr.rearrange("b (k w) -> b k w", k=2), smp_out[:, 0:2 * WT].rearrange("p (k j) n -> p k (j n)", k=2)).then_inc(s_sq, 16)
            act.wait_ge(s_sq, 16)
            toks = [o[k][0].rearrange("a (t p) h d -> p (a t) (h d)", p=P) for k in ("p_fox_k", "p_sb_k", "p_fox_v", "p_sb_v")]
            smps = [o[k][0].rearrange("b t h d -> (b t) (h d)") for k in ("s_fox_k", "s_sb_k", "s_fox_v", "s_sb_v")]

            def tok_evict(t, j):
                m = 4 * t + j
                act.wait_ge(s_tt, m + 2)
                act.wait_ge(s_so[j % 2], 16 * (2 * t + j // 2))
                nc.scalar.activation(tok_out[:, j % 2].rearrange("p (a t) n -> p a (t n)", a=2), psT[:], ACT.Copy).then_inc(s_te, 1)
                act.wait_ge(s_te, m + 2)
                act.dma_start(toks[j][:, :, ds(P * t, P)], tok_out[:, j % 2]).then_inc(s_so[j % 2], 16)

            with act.Fori(0, WT) as t:
                for j in range(4):
                    n = 2 * WT + 4 * t + j
                    act.wait_ge(s_st[j % 2], 16 * (WT + t + (1 if j >= 2 else 0)))
                    evict(n, j % 2, tile_out[:, j % 2], samples=True)
                    if j < 2:
                        act.wait_ge(s_pe, n + 3)
                        act.dma_start(qk_scr[1, ds(j * W + P * t, P)], tile_out[:, j % 2, 0:SEQ]).then_inc(s_st[j % 2], 16)
                    if j >= 1:
                        tok_evict(t, j - 1)
                tok_evict(t, 3)
            act.wait_ge(s_tt, 4 * WT + 2)
            nc.scalar.activation(smp_out[:].rearrange("p (t j) n -> p t (j n)", j=4), psB[0:NB], ACT.Copy).then_inc(s_te, 1)
            act.wait_ge(s_te, 4 * WT + 2)
            for j in range(4):
                act.dma_start(smps[j].rearrange("b (t n) -> b t n", n=P), smp_out[:].rearrange("p (t j) n -> p j t n", j=4)[:, j]).then_inc(s_sq, 16)
            act.wait_ge(s_sq, 16 * 5)
            evict(FG_N, 0, fgT, H)
            evict(FG_N + 1, 1, xrT[:, 0])
            act.preload_act_table_set(LN_EXP)
            act.wait_ge(s_fc, 2)
            nc.scalar.activation(fg_e[:], fg_e[:], ACT.Exp).then_inc(s_fa, 1)
            act.wait_ge(s_fa, 1)
            nc.scalar.activation(fg_e[:], fg_e[:], ACT.Ln, bias=1.0).then_inc(s_fa, 1)
            for n in range(1, 2 * LT):
                evict(FG_N + 1 + n, (n + 1) % 2, (xrT, xgT)[n % 2][:, n // 2])

            def low_half(n, par, bank):
                act.wait_ge(o_x, n)
                nc.scalar.activation(o_low[par * HD:par * HD + HD], bank[HD:P], ACT.Copy).then_inc(o_c, 1)

            with act.Fori(0, WT) as t:
                for s in range(F_STEPS + 5):
                    if 2 <= s < F_STEPS + 2:
                        x = s - 2
                        act.wait_ge(f_o, F_STEPS * t + max(0, x - 1))
                        for u, (y, b) in enumerate(F_USES):
                            if y == x:
                                nb = min(4, x % TT + 1 - 4 * b)
                                act.wait_ge(f_t, F_N * t + u + 1)
                                nc.scalar.activation(pt[:, x % 2, 4 * b:4 * b + nb, 0], psT[:, b, 0:nb * P].rearrange("p (k n) -> p k n", n=P),
                                                     ACT.Copy).then_inc(f_h, 1)
                    if s < F_STEPS:
                        act.wait_ge(f_m, F_STEPS * t + s + 1)
                        act.wait_ge(f_t, F_N * t + (f_cum(s - 3) if s >= 3 else 0))
                        nk = (s % TT + 1) * P
                        ps = proj_ps[s % 2][:, 0:2].rearrange("p a n -> p (a n)")[:, 0:nk]
                        nc.scalar.activation(probs[:, s % 3, 0:nk], ps, ACT.Exp, bias=row_max[:, s:s + 1],
                                             accum_out=row_sum[:, s:s + 1]).then_inc(f_e, 1)
                    if s >= 5 and s % 2 == 1:
                        g = (s - 5) // 2
                        act.wait_ge(f_o, F_STEPS * t + 2 * g + 2)
                        low_half(F_BANKS * t + g, g // (TT // 2), proj_ps[g % 2][:, 2])
            with act.Fori(0, WT) as t:
                for k in range(B_N + 5):
                    if k < B_N:
                        par, c, kb, q0 = B_STEPS[k]
                        act.wait_ge(b_z, B_N * t + k + 1)
                        act.wait_ge(b_t, B_N * t + max(0, k - 3))
                        nc.scalar.activation(z_s[:, k % 4, q0:512], z_bank(k)[:, q0:512], ACT.Copy).then_inc(b_c, 1)
                    if 1 <= k < B_N + 1:
                        x = k - 1
                        par, c, kb, q0 = B_STEPS[x]
                        act.wait_ge(b_m, B_N * t + x + 1)
                        nc.scalar.activation(z_e[:, x % 3, q0:512], z_e[:, x % 3, q0:512], ACT.Exp).then_inc(b_e, 1)
                        act.wait_ge(b_e, B_N * t + x + 1)
                        nc.scalar.activation(z_e[:, x % 3, q0:512], z_e[:, x % 3, q0:512], ACT.Ln, bias=1.0).then_inc(b_l, 1)
                    if 3 <= k < B_N + 3:
                        x = k - 3
                        par, c, kb, q0 = B_STEPS[x]
                        act.wait_ge(b_t, B_N * t + x + 1)
                        nc.scalar.activation(z_w[:, x % 4, q0:512], z_w[:, x % 4, q0:512], ACT.Exp).then_inc(b_w, 1)
                    for g in range(4):
                        if k == min(B_LAST[g] + 5, B_N + 4):
                            act.wait_ge(b_o, B_N * t + B_LAST[g] + 1)
                            low_half(F_BANKS * WT + 4 * t + g, g % 2, proj_ps[g % 2][:, 1])

            A = nc.scalar
            act.wait_ge(d_d, D_MAX)
            act.preload_act_table_set(LN_EXP)
            A.activation(d_f[:], d_f[:], ACT.Exp, bias=d_small[:, 0:1], accum_out=d_small[:, 1:2]).then_inc(d_a, 1)
            act.wait_ge(d_d, D_MIN)
            A.activation(d_e[:], d_e[:], ACT.Exp).then_inc(d_a, 1)
            act.wait_ge(d_a, 2)
            A.activation(d_e[:], d_e[:], ACT.Ln, bias=1.0).then_inc(d_a, 1)
            act.wait_ge(d_d, D_SB)
            A.activation(d_z[:], d_z[:], ACT.Exp).then_inc(d_a, 1)
            act.wait_ge(r_d, R_CONV + 2)
            A.activation(r_c[:, 3], r_c[:, 3], ACT.Exp).then_inc(r_s, 1)
            act.wait_ge(r_s, 1)
            A.activation(r_c[:, 3], r_c[:, 3], ACT.Ln, bias=1.0).then_inc(r_s, 1)
            act.wait_ge(r_d, R_CONV)
            for g in range(2):
                for t in range(LT):
                    act.wait_ge(r_p, 2 * g + t + 1)
                    A.activation((r_t, r_i)[g][:, t].rearrange("p (c n) -> p c n", c=NCH), proj_ps[t][:, :, 0:CH], ACT.Tanh,
                                 bias=r_c[:, g, t:t + 1], scale=0.5).then_inc(r_s, 1)
            act.wait_ge(r_d, R_LOGA)
            A.activation(r_a[:], r_t[:], ACT.Exp).then_inc(r_s, 1)
            A.activation(r_h[:], r_t[:], ACT.Tanh).then_inc(r_s, 1)
            act.wait_ge(r_d, R_ONE)
            A.activation(r_h[:], r_h[:], ACT.Sqrt).then_inc(r_s, 1)
            A.activation(xgT[:], xgT[:], ACT.Gelu_apprx_tanh).then_inc(r_s, 1)
            act.wait_ge(d_d, D_LAST)
            act.wait_ge(d_v, 2 * NPG * (NB + 1))
            with act.Fori(0, KT // 2) as t:
                for j in range(2):
                    m = 2 * t + j
                    act.wait_ge(g_pm, m + 3)
                    A.activation(resT[:, ds(m, 1)].rearrange("p a (c n) -> p (a c) n", c=NCH), proj_ps[j][:, :, 0:CH], ACT.Identity,
                                 scale=modT[:, ds(2 * KT + m, 1), 0:1].rearrange("p a n -> p (a n)")).then_inc(m_ev, 1)

            def roots(n, rows, d, q, count):
                act.wait_ge(d, count)
                A.activation(ln_st[0:rows, n % 2, 14:15], ln_st[0:rows, n % 2, 14:15], ACT.Sqrt).then_inc(q, 1)

            act.wait_ge(n_k, 2)
            for tt in range(TT + 1):
                roots(tt, P if tt < TT else NB, n_r, n_q, 6 * tt + 4)
                for n in H2_AT[tt]:
                    f, h = n % KT, n // KT
                    act.wait_ge(n_b, n + 1)
                    bank = psA[:, n % 2]
                    A.activation(resT[:, f, h * 512:h * 512 + 512], bank, ACT.Identity, bias=ln_f[:, 3, f:f + 1], scale=ln_f[:, 2, f:f + 1])
                    if n >= 2:
                        act.wait_ge(n_lo, n - 1)
                    A.activation(h2_full[:, n % 2], bank, ACT.Identity, bias=ln_f[:, 1, f:f + 1], scale=ln_f[:, 0, f:f + 1]).then_inc(n_h, 1)
            act.wait_ge(n_s, 6)
            for k, gs in enumerate(GROUPS):
                with act.Fori(0, gs) as f:
                    F = NF[k] + f
                    act.wait_ge(g_pm, G_UP0[k] + 2 * f + 3)
                    act.wait_ge(u_d, 3 * F)
                    A.activation(ffn_cols[:, ds(F, 1)].rearrange("p a n -> p (a n)"), psA[:, 2, CH - NB - 2:CH], ACT.Copy)
                    A.activation(u_a[:].rearrange("p (c n) -> p c n", c=NCH), psA[:, :, 0:CH], ACT.Copy).then_inc(g_ev[0], 1)
                    act.wait_ge(u_d, 3 * F + 3)
                    act.wait_ge(u_l, F)
                    A.activation(u_g[:], u_c[:], ACT.Gelu_apprx_tanh).then_inc(u_g_, 1)
            for tt in range(TT + 1):
                rows = P if tt < TT else NB
                roots(tt, rows, y_d, y_q, 5 * tt + 3)
                if tt >= 3:
                    act.wait_ge(y_s[tt % 3], 16 * (tt // 3))
                act.wait_ge(y_d, 5 * tt + 5)
                A.activation(y_tile[0:rows, tt % 3], y_bank(tt)[0:rows].rearrange("p a n -> p (a n)"), ACT.Identity,
                             bias=ln_st[0:rows, tt % 2, 14:15], scale=ln_st[0:rows, tt % 2, 15:16]).then_inc(y_n, 1)

        @block.tensor
        def _(pe):
            pe.sem_inc(s_pm, 2)
            pe.wait_ge(s_ident, 1)
            pe.wait_ge(s_csil, 2)
            for k in range(KT):
                last = nc.tensor.transpose(psT[:, 0, k * NC:(k + 1) * NC], c_rows[:, k * P:(k + 1) * P], ident[0:NC, 0:NC])
            last.then_inc(s_vt, 1)
            pe.wait_ge(s_small, 16 * NSMALL)
            pe.wait_ge(s_vte, 1)
            at = 0
            for n, r in enumerate((NVA, NVB, NVC)):
                nc.tensor.transpose(psT[:, 1, at:at + r], vec_rows[0:r, n], ident[0:r, 0:r])
                at += r
            for n in range(3):
                r = min(P, NVD - n * P)
                last = nc.tensor.transpose(psT[:, 0, n * P:n * P + r], vec_rows[0:r, 3 + n], ident[0:r, 0:r])
            last.then_inc(s_vt, 1)

            def ada(w, dst):
                for k in range(KT):
                    last = nc.tensor.matmul(dst[0:2 * NC], cT[:, k], w[:, k], start=k == 0, stop=k == KT - 1)
                last.then_inc(s_amm, 1)

            def ada_parts(n, dst):
                for k in range(KT):
                    if k % 2 == 0:
                        pe.wait_ge(s_hlo, 2 * KT + 4 * n + k // 2 + 1)
                    at = k // 2 % 3
                    nc.tensor.matmul(dst[0:2 * NC], c_parts[:, k], a_hi[:, at, k % 2], start=k == 0, stop=False)
                    last = nc.tensor.matmul(dst[0:NC], c_parts[:, k, 0:NC], a_lo[:, at, k % 2], start=False, stop=k == KT - 1)
                    if k == 1:
                        last.then_inc(s_ap, 1)
                last.then_inc(s_amm, 1)

            def ada_turn(slot, dst):
                for m in range(4):
                    last = nc.tensor.transpose(dst[:, 2 * m * NC:2 * (m + 1) * NC], ada_rows[:, slot, m * P:(m + 1) * P], ident[0:2 * NC, 0:2 * NC])
                last.then_inc(s_atr, 1)

            for n in range(ADA1 + 1):
                if n < ADA1:
                    pe.wait_ge(s_al[n % 2], 16 * (n // 2 + 1))
                    if n >= 2:
                        pe.wait_ge(s_arow, n - 1)
                    ada(w_ada1[:, n % 2], psA[:, n % 2])
                if n >= 1:
                    if n >= 3:
                        pe.wait_ge(s_aev, n - 2)
                    pe.wait_ge(s_arow, n)
                    ada_turn((n - 1) % 2, psB[:, (n - 1) % 2])
            for k in range(KT):
                last = nc.tensor.transpose(psB[:, 2, k * NB:(k + 1) * NB], xs_rows[:, k * P:(k + 1) * P], ident[0:NB, 0:NB])
            last.then_inc(s_vt, 1)
            pe.wait_ge(s_aev, ADA1)
            for h in range(2):
                pe.wait_ge(s_x[h], 16)
                for f in range(KT):
                    n = h * KT + f
                    if n >= 4:
                        pe.wait_ge(s_hf, n - 3)
                    for q in range(TT // 2):
                        last = nc.tensor.transpose(proj_ps[n % 2][:, n // 2 % 2, q * P:(q + 1) * P],
                                                   x_rows[:, h * TT // 2 + q, f * P:(f + 1) * P], ident[:])
                    last.then_inc(s_xt, 1)
            for n in range(ADA1, ADA1 + ADA_IN):
                if n > ADA1:
                    pe.wait_ge(s_arow, n)
                    ada_turn((n - 1) % 2, psT[:, 1])
                pe.wait_ge(s_al[n % 2], 16 * (n // 2 + 1))
                ada(w_ada1[:, n % 2], psT[:, 0])
            pe.wait_ge(s_hf, 2 * KT)
            pe.wait_ge(s_hlo, 2 * KT)
            pe.wait_ge(s_hs, 4)

            def project(n, half, cols=P):
                pe.wait_ge(s_wlo, n + 3)
                pe.wait_ge(s_pe, n + 1)
                for k in range(KT):
                    for w, a in ((w_hi, acts_hi), (w_hi, acts_lo), (w_lo, acts_hi)):
                        for c in range(NCH):
                            last = nc.tensor.matmul(proj_ps[half][0:cols, c, 0:CH], w[:, half, k, 0:cols], a[:, k, c * CH:(c + 1) * CH],
                                                    start=k == 0 and w is w_hi and a is acts_hi, stop=k == KT - 1 and w is w_lo)
                last.then_inc(s_pm, 1)

            pe.sem_inc(s_pe, 2)
            with pe.Fori(0, WT) as t:
                for j in range(2):
                    project(2 * t + j, j)
                    c = ADA1 + ADA_IN + 2 * t + j
                    pe.wait_ge(s_aev, c - 1)
                    pe.wait_ge(s_arow, c)
                    ada_parts(2 * t + j, psT[:, 0])
                    ada_turn(1 - j, psT[:, 1])
            pe.wait_ge(s_aev, ADA1 + ADA2 - 1)
            pe.wait_ge(s_arow, ADA1 + ADA2)
            ada_turn(1, psT[:, 1])
            pe.wait_ge(s_aev, ADA1 + ADA2)
            pe.wait_ge(s_pe, 2 * WT + 2)
            for j in range(2):
                for t in range(WT):
                    last = nc.tensor.transpose(psT[0:NB, j, t * P:(t + 1) * P], smpT[:, 2 * t + j], ident[:])
            last.then_inc(s_tt, 1)

            def to_tokens(t, j):
                pe.wait_ge(s_pe, 2 * WT + 4 * t + j + 3)
                pe.wait_ge(s_te, 4 * t + j + 1)
                for q in range(TT):
                    last = nc.tensor.transpose(psT[:, q // 4, q % 4 * P:q % 4 * P + P], tile_out[:, j % 2, q * P:(q + 1) * P], ident[:])
                last.then_inc(s_tt, 1)

            with pe.Fori(0, WT) as t:
                for j in range(4):
                    project(2 * WT + 4 * t + j, j % 2)
                    if j >= 1:
                        to_tokens(t, j - 1)
                to_tokens(t, 3)
            pe.wait_ge(s_pe, 6 * WT + 2)
            for t in range(WT):
                for j in range(4):
                    last = nc.tensor.transpose(psB[0:NB, t, j * P:(j + 1) * P], smpT[:, 2 * WT + 4 * t + j], ident[:])
            last.then_inc(s_tt, 1)
            pe.wait_ge(s_te, 4 * WT + 2)
            project(FG_N, 0, H)
            with pe.Fori(0, LT) as t:
                for j in range(2):
                    project(FG_N + 1 + 2 * t + j, 1 - j)
            pe.wait_ge(s_fc, 4)
            for q in range(TT):
                nc.tensor.transpose(psT[:, 0, q * H:(q + 1) * H], lgT[:, q * P:(q + 1) * P], ident[0:H, 0:H])
            nc.tensor.transpose(psT[0:NB, 0, TT * H:TT * H + H], lgT[:, SEQ:TOK], ident[0:H, 0:H]).then_inc(s_fp, 1)
            pe.wait_ge(s_cr, 1)
            pe.wait_ge(s_fp, 2)

            with pe.Fori(0, WT) as t:
                for s in range(F_STEPS + 3):
                    if s < F_STEPS:
                        par, qb = s // TT, s % TT
                        if qb == 0:
                            pe.wait_ge(s_b, 2 * t + par + 3)
                            pe.wait_ge(s_fl[par], 32 * (t + 1))
                        pe.wait_ge(f_e, F_STEPS * t + max(0, s - 1))
                        rows = slice(qb * P, qb * P + P)
                        for c in range(qb // 4 + 1):
                            ks = slice(c * 512, min(c * 512 + 512, qb * P + P))
                            bank = proj_ps[s % 2][:, c, 0:ks.stop - ks.start]
                            diag = c == qb // 4
                            nc.tensor.matmul(bank, q_hi[:, par, rows], k_st[:, par, ks], start=True, stop=False)
                            nc.tensor.matmul(bank, q_lo[:, par, rows], k_st[:, par, ks], start=False, stop=False)
                            last = nc.tensor.matmul(bank, fq_rows[:, par, rows], fk_rows[:, par, ks], start=False, stop=not diag)
                            if diag:
                                last = nc.tensor.matmul(bank[:, qb % 4 * P:qb % 4 * P + P], ident_r[:], mask_r[:, 0], start=False, stop=True)
                        last.then_inc(f_s, 1)
                    if 2 <= s < F_STEPS + 2:
                        x = s - 2
                        pe.wait_ge(f_n, F_STEPS * t + x + 1)
                        for u, (y, b) in enumerate(F_USES):
                            if y == x:
                                before = [v for v in range(u) if F_USES[v][1] == b]
                                pe.wait_ge(f_l, F_N * t + (before[-1] + 1 if before else 0))
                                for kb in range(4 * b, min(4 * b + 4, x % TT + 1)):
                                    last = nc.tensor.transpose(psT[:, b, kb % 4 * P:kb % 4 * P + P], probs[:, x % 3, kb * P:kb * P + P], ident[:])
                                last.then_inc(f_t, 1)
                    if s >= 3:
                        x = s - 3
                        par, qb = x // TT, x % TT
                        pe.wait_ge(f_l, F_N * t + f_cum(x))
                        if qb % 2 == 0:
                            pe.wait_ge(o_x, F_BANKS * t + max(0, x // 2 - 1))
                        for kb in range(qb + 1):
                            last = nc.tensor.matmul(proj_ps[x // 2 % 2][:, 2, qb % 2 * 2 * P:(qb % 2 + 1) * 2 * P], v_st[:, par, kb],
                                                    pt[:, x % 2, kb].rearrange("p e n -> p (e n)"), start=kb == 0, stop=kb == qb)
                        last.then_inc(f_o, 1)

            with pe.Fori(0, WT) as t:
                pe.wait_ge(s_b, H + 2 * t + 4)
                for k in range(-1, B_N + 5):
                    if k + 1 < B_N:
                        x = k + 1
                        par, c, kb, q0 = B_STEPS[x]
                        pe.wait_ge(b_c, B_N * t + max(0, x - 2))
                        qs = slice(512 * c + q0, 512 * c + 512)
                        bank = z_bank(x)[:, q0:512]
                        diag = kb >= 4 * c
                        nc.tensor.matmul(bank, k_st[:, par, kb * P:kb * P + P], q_hi[:, par, qs], start=True, stop=False)
                        last = nc.tensor.matmul(bank, k_st[:, par, kb * P:kb * P + P], q_lo[:, par, qs], start=False, stop=not diag)
                        if diag:
                            last = nc.tensor.matmul(bank[:, 0:P], ident_r[:], mask_r[:, 1], start=False, stop=True)
                        last.then_inc(b_z, 1)
                    if 3 <= k < B_N + 3:
                        x = k - 3
                        par, c, kb, q0 = B_STEPS[x]
                        pe.wait_ge(b_t, B_N * t + x + 1)
                        if kb > 0:
                            nc.tensor.matmul(proj_ps[par][:, 2, q0:512], tri[:, 1], z_sp[:, x % 4, q0:512], start=False, stop=True,
                                             skip_group_check=True)
                    if 1 <= k < B_N + 1:
                        x = k - 1
                        par, c, kb, q0 = B_STEPS[x]
                        pe.wait_ge(b_s, B_N * t + x + 1)
                        nc.tensor.matmul(proj_ps[par][:, 2, q0:512], tri[:, 0], z_sp[:, x % 4, q0:512], start=kb == 4 * c + 3, stop=True,
                                         skip_group_check=True).then_inc(b_k, 1)
                    if k >= 5:
                        x = k - 5
                        par, c, kb, q0 = B_STEPS[x]
                        pe.wait_ge(b_lo, B_N * t + x + 1)
                        if kb == 4 * c + 3:
                            pe.wait_ge(o_x, F_BANKS * WT + 4 * t + (0 if c == 0 else par + 1))
                        nc.tensor.matmul(proj_ps[par][:, 1, q0:512], v_st[:, par, kb], w_hi2[:, x % 2, q0:512], start=kb == 4 * c + 3, stop=False,
                                         skip_group_check=True)
                        nc.tensor.matmul(proj_ps[par][:, 1, q0:512], v_st[:, par, kb], w_lo2[:, x % 2, q0:512], start=False, stop=kb == 0,
                                         skip_group_check=True).then_inc(b_o, 1)

            pe.wait_ge(o_x, (F_BANKS + 4) * WT)
            pe.sem_inc(d_v, 2 * NPG)
            pe.wait_ge(s_kfree, NPG + 2 * NB * NPG)
            pe.wait_ge(s_lf, 16 * NB * NPG)
            for p in range(NPG):
                dst = slice(p % 4 * P, p % 4 * P + P)
                nc.tensor.transpose(psA[0:R48, p // 4, dst], scores[:, 0, p].rearrange("p b h -> p (b h)"), ident[:])
                nc.tensor.transpose(psB[0:R48, p // 4, dst], scores[:, 1, p].rearrange("p b h -> p (b h)"), ident[:])
                last = nc.tensor.transpose(psT[0:R48, p // 4, dst], lf_pages[:, p].rearrange("p b h -> p (b h)"), ident[:])
            last.then_inc(d_t, 1)
            pe.wait_ge(d_d, D_SELF)
            for t in range(WT):
                nc.tensor.matmul(psA[0:R48, 2, 0:1], d_zq[:, t].rearrange("p b h -> p (b h)"), ones[:], start=t == 0, stop=t == WT - 1)
            nc.tensor.matmul(psA[0:R48, 2, 1:2], d_spread[:].rearrange("p b h -> p (b h)"), ones[0:H], start=True, stop=True).then_inc(d_t, 1)
            pe.wait_ge(d_d, D_FOX)
            for p in range(NPG):
                nc.tensor.transpose(psT[:, 0, p * R48:(p + 1) * R48], d_f[:, p * P:(p + 1) * P], ident[0:R48, 0:R48])
            nc.tensor.matmul(psA[0:NB, 2, 0:R48], d_grp[:], d_diag[:], start=True, stop=True).then_inc(d_t, 1)
            pe.wait_ge(d_a, 4)
            for p in range(NPG):
                last = nc.tensor.transpose(psT[:, 1, p * R48:(p + 1) * R48], d_z[:, p * P:(p + 1) * P], ident[0:R48, 0:R48])
            last.then_inc(d_t, 1)
            pe.wait_ge(d_d, D_P)
            nc.tensor.matmul(psT[0:R48, 1, 0:W], d_self[:], smp_out[:, 2:4 * WT:4], start=True, stop=True).then_inc(d_t, 1)
            def v_products(t):
                for i4 in range(NB // 2):
                    for kind in range(2):
                        if (t, 2 * i4 + kind) == (0, 7):
                            pe.wait_ge(d_d, D_ACC)
                        for p in range(NPG):
                            pe.wait_ge(s_vl[NPG * kind + p], 16 * (NB // 2 * t + i4 + 1))
                            nc.tensor.matmul(V_BANKS[2 * i4 + kind][0:R48, 0:W], d_p[:, kind, p], v_page[:, kind, p],
                                             start=p == 0, stop=p == NPG - 1).then_inc(d_v, 1)

            v_products(0)
            pe.wait_ge(r_d, R_CONV)
            pe.wait_ge(s_gw, 16 * 8)
            pe.wait_ge(d_ac, 8 + NB)
            for g in range(2):
                for t in range(LT):
                    if g == 1:
                        pe.wait_ge(r_s, 3 + t)
                    for c in range(NCH):
                        last = nc.tensor.matmul(proj_ps[t][:, c, 0:CH], gate_w[:, g, t], r_xc[:, t, c * CH:(c + 1) * CH], start=True, stop=True)
                    last.then_inc(r_p, 1)
            pe.wait_ge(r_s, 6)
            pe.sem_inc(g_pm, 2)
            v_products(1)
            pe.wait_ge(d_ac, 8 + 2 * NB)
            for kind in range(2):
                for v in range(WT):
                    at = (kind * WT + v) * R48
                    last = nc.tensor.transpose(psB[:, 0, at:at + R48], d_acc[:, kind, v * P:(v + 1) * P], ident[0:R48, 0:R48])
            last.then_inc(d_t, 1)
            pe.wait_ge(r_d, R_COLS)
            for t in range(LT):
                last = nc.tensor.transpose(psA[0:4 + 2 * NB, 0, t * P:(t + 1) * P], lru_cols[:, t], ident[:])
            last.then_inc(r_p, 1)
            pe.wait_ge(r_d, R_ROWS)
            pe.wait_ge(d_d, D_LAST)
            pe.wait_ge(o_l, (F_BANKS + 4) * WT)

            def g_project(m, half, round_, hi, lo, nk=KT, gated_=None):
                pe.wait_ge(g_ws, m + 3)
                pe.wait_ge(g_ev[half], round_)
                for k in range(nk):
                    if k == nk - 1 and gated_ is not None:
                        pe.wait_ge(u_l, gated_)
                    for w, a in ((w_hi, hi), (w_hi, lo), (w_lo, hi)):
                        for c in range(NCH):
                            last = nc.tensor.matmul(proj_ps[half][:, c, 0:CH], w[:, half, k], a[:, k, c * CH:(c + 1) * CH],
                                                    start=k == 0 and w is w_hi and a is hi, stop=k == nk - 1 and w is w_lo)
                last.then_inc(g_pm, 1)

            pe.sem_inc(g_ev[0], 1)
            pe.sem_inc(g_ev[1], 1)
            with pe.Fori(0, KT // 2) as t:
                for j in range(2):
                    g_project(2 * t + j, j, t + 1, acts_hi, acts_lo)
            for j in range(2):
                pe.wait_ge(g_ev[j], KT // 2 + 1)

            def to_rows(tt, dst, src):
                cols = slice(tt * P, tt * P + P) if tt < TT else slice(SEQ, TOK)
                for f in range(KT):
                    last = nc.tensor.transpose(dst[0:cols.stop - cols.start, f // 4, f % 4 * P:f % 4 * P + P], src[:, f, cols], ident[:])
                return last

            for tt in range(TT + 1):
                if tt >= 2:
                    pe.wait_ge(n_r, 6 * (tt - 2) + 1)
                to_rows(tt, y_bank(tt), resT).then_inc(n_t, 1)
                for n in H2_AT[tt]:
                    f, h = n % KT, n // KT
                    pe.wait_ge(n_r, 6 * (4 * h + 4))
                    if n >= 2:
                        pe.wait_ge(n_h, n - 1)
                    for q in range(4):
                        last = nc.tensor.transpose(psA[:, n % 2, q * P:(q + 1) * P], x_hat[:, 4 * h + q, f * P:(f + 1) * P], ident[:])
                    last.then_inc(n_b, 1)
            pe.wait_ge(n_r, 6 * (TT + 1))
            for f in range(KT):
                last = nc.tensor.transpose(psA[:, 2, f * NB:(f + 1) * NB], xs_hat[:, 1, f * P:(f + 1) * P], ident[0:NB, 0:NB])
            last.then_inc(n_b, 1)
            pe.wait_ge(n_h, 2 * KT)
            pe.wait_ge(n_lo, 2 * KT)
            pe.wait_ge(n_s, 6)
            for k, gs in enumerate(GROUPS):
                with pe.Fori(0, gs) as f:
                    for j in range(2):
                        g_project(G_UP0[k] + 2 * f + j, j, KT // 2 * (k + 1) + NF[k] + f + 1, acts_hi, acts_lo)
                pe.wait_ge(u_l, NF[k + 1] - 1)
                for j in range(2):
                    g_project(G_DN0[k] + j, j, KT // 2 * (k + 1) + NF[k + 1] + 1, g_hi, g_lo, gs, NF[k + 1] if j == 0 else None)
                with pe.Fori(1, KT // 2) as t:
                    for j in range(2):
                        g_project(G_DN0[k] + 2 * t + j, j, KT // 2 * (k + 1) + NF[k + 1] + t + 1, g_hi, g_lo, gs)
            pe.wait_ge(u_s, KT * len(GROUPS))
            for tt in range(TT + 1):
                if tt >= 2:
                    pe.wait_ge(y_n, tt - 1)
                to_rows(tt, y_bank(tt), resT).then_inc(y_t, 1)
            for c in range(2):
                nf = FT // 2
                bank = (psA, psB)[c]
                if c == 1:
                    pe.wait_ge(y_n, TT + 1)
                    pe.wait_ge(y_f, 2)
                for f in range(nf):
                    last = nc.tensor.transpose(bank[0:2 + NB, f // 4, f % 4 * P:f % 4 * P + P], ffn_cols[:, c * nf + f], ident[:])
                last.then_inc(y_f, 1)


_INS = ["x_prompt", "x_sample", "cache_fox_k", "cache_fox_v", "cache_fox_logf", "cache_sb_k", "cache_sb_v",
        "state_lru_h", "state_lru_conv", "state_ffn_conv", "page_table", "c_prompt", "c_sample",
        "w_ada", "b_ada", "w_in", "b_fgate", "w_lru_conv", "b_lru_conv", "w_rgate", "b_rgate", "w_igate", "b_igate",
        "lru_lambda", "w_out", "ln1_g", "ln1_b", "w_up", "w_ffn_conv", "b_ffn_conv", "w_down", "ln2_g", "ln2_b"]


def _out_shapes(a):
    d, b, s = a["w_in"].shape[0], a["x_prompt"].shape[0], a["x_prompt"].shape[1]
    nb = a["x_sample"].shape[0]
    h, hd = a["cache_fox_k"].shape[3:]
    dl, ff = a["state_lru_h"].shape[2], a["w_down"].shape[1]
    out = [("y_prompt", a["x_prompt"].shape), ("y_sample", a["x_sample"].shape)]
    for pre, n, t in (("p", b, s), ("s", nb, 1)):
        out += [(pre + "_fox_k", (d, n, t, h, hd)), (pre + "_fox_v", (d, n, t, h, hd)), (pre + "_fox_logf", (d, n, t, h)),
                (pre + "_sb_k", (d, n, t, h, hd)), (pre + "_sb_v", (d, n, t, h, hd)), (pre + "_lru_h", (d, n, dl)),
                (pre + "_lru_conv", (d, n, a["state_lru_conv"].shape[2], dl)), (pre + "_ffn_conv", (d, n, a["state_ffn_conv"].shape[2], ff))]
    return out


def kernel(**inputs):
    import numpy as np
    import concourse.bacc as bacc
    from concourse.bass_utils import run_bass_kernel_spmd

    nc = bacc.Bacc("TRN2", target_bir_lowering=False, num_devices=1)
    arrays = {f"in_{n}": np.ascontiguousarray(inputs[n]) for n in _INS}
    ins = {n: nc.dram_tensor(f"in_{n}", arrays[f"in_{n}"].shape, mybir.dt.from_np(arrays[f"in_{n}"].dtype), kind="ExternalInput").ap()
           for n in _INS}
    shapes = _out_shapes({n: arrays[f"in_{n}"] for n in _INS})
    outs = {n: nc.dram_tensor(f"out_{n}", list(s), F32, kind="ExternalOutput").ap() for n, s in shapes}
    hybrid_step(nc, ins, outs)
    r = run_bass_kernel_spmd(nc, [arrays], core_ids=[0])
    return tuple(r.results[0][f"out_{n}"] for n, _ in shapes)
```
